# Optimizing a Trainium2 kernel written in Bass

```python
import jax, jax.numpy as jnp
from jax import lax
import numpy as np

D_MODEL = 1024
BATCH = 1
SEQ = 2048
DEPTH = 1

N_HEADS = 8
QK_NOPE_DIM = 64
QK_ROPE_DIM = 32
QK_DIM = QK_NOPE_DIM + QK_ROPE_DIM
V_HEAD_DIM = 64
Q_LORA_RANK = 384
KV_LORA_RANK = 256
ROPE_THETA = 10000.0
Q_BLOCK = 128
CONV_CHANNELS = 512
CONV_WIDTH = 31
FFN_HIDDEN = -(-8 * D_MODEL // (3 * 256)) * 256
N_MOD = 6
EPS = 1e-6
NEG_INF = -1e30

IN_WIDTHS = (Q_LORA_RANK, KV_LORA_RANK, QK_ROPE_DIM, 2 * CONV_CHANNELS, D_MODEL, D_MODEL)
SPLIT_IDX = (Q_LORA_RANK,
             Q_LORA_RANK + KV_LORA_RANK,
             Q_LORA_RANK + KV_LORA_RANK + QK_ROPE_DIM,
             Q_LORA_RANK + KV_LORA_RANK + QK_ROPE_DIM + 2 * CONV_CHANNELS,
             Q_LORA_RANK + KV_LORA_RANK + QK_ROPE_DIM + 2 * CONV_CHANNELS + D_MODEL)
IN_WIDTH = sum(IN_WIDTHS)

kernel_name = "hybrid_mla_conformer_adaln_block"

def rms_norm(x, gain):
    xf = x.astype(jnp.float32)
    y = xf * lax.rsqrt(jnp.mean(xf * xf, axis=-1, keepdims=True) + EPS)
    return (y * gain.astype(jnp.float32)).astype(x.dtype)

def layer_norm(x, gain, bias):
    xf = x.astype(jnp.float32)
    mu = jnp.mean(xf, axis=-1, keepdims=True)
    xc = xf - mu
    y = xc * lax.rsqrt(jnp.mean(xc * xc, axis=-1, keepdims=True) + EPS)
    return (y * gain.astype(jnp.float32) + bias.astype(jnp.float32)).astype(x.dtype)

def rope_tables(positions, dtype):
    inv_freq = ROPE_THETA ** (-jnp.arange(0, QK_ROPE_DIM, 2, dtype=jnp.float32) / QK_ROPE_DIM)
    ang = positions.astype(jnp.float32)[..., None] * inv_freq
    return jnp.cos(ang).astype(dtype), jnp.sin(ang).astype(dtype)

def apply_rope(t, cos, sin):
    t1, t2 = jnp.split(t, 2, axis=-1)
    return jnp.concatenate([t1 * cos - t2 * sin, t2 * cos + t1 * sin], axis=-1)

def mla_attention(q_nope, q_rope, k_nope, k_rope, v):
    seq = q_nope.shape[1]
    scale = QK_DIM ** -0.5
    outs = []
    for i in range(seq // Q_BLOCK):
        s0, s1 = i * Q_BLOCK, (i + 1) * Q_BLOCK
        logits = (jnp.einsum('bqhd,bkhd->bhqk', q_nope[:, s0:s1], k_nope[:, :s1])
                  + jnp.einsum('bqhr,bkr->bhqk', q_rope[:, s0:s1], k_rope[:, :s1]))
        logits = logits.astype(jnp.float32) * scale
        causal = (s0 + jnp.arange(Q_BLOCK))[:, None] >= jnp.arange(s1)[None, :]
        probs = jax.nn.softmax(jnp.where(causal, logits, NEG_INF), axis=-1).astype(v.dtype)
        outs.append(jnp.einsum('bhqk,bkhd->bqhd', probs, v[:, :s1]))
    return jnp.concatenate(outs, axis=1)

def causal_depthwise_conv(u, w, b):
    rhs = w.astype(u.dtype)[:, None, :]
    y = lax.conv_general_dilated(u, rhs, window_strides=(1,), padding=[(CONV_WIDTH - 1, 0)],
                                 dimension_numbers=('NWC', 'WIO', 'NWC'),
                                 feature_group_count=u.shape[-1])
    return y + b

def hybrid_layer(x, c_act, cos, sin, w_ada, b_ada, g_mix, w_in, g_q, w_uq, g_kv, w_ukv, w_o_attn,
                 w_dw, b_dw, g_cn, b_cn, w_pw2, w_out, g_ffn, w_gu, w_down):
    bsz, seq, _ = x.shape
    mod = (c_act @ w_ada + b_ada)[:, None, :]
    sh1, sc1, gt1, sh2, sc2, gt2 = jnp.split(mod, N_MOD, axis=-1)

    h = rms_norm(x, g_mix) * (1 + sc1) + sh1
    proj = h @ w_in
    q_lat, kv_lat, k_rope, glu_in, gate_a, gate_b = jnp.split(proj, SPLIT_IDX, axis=-1)

    q = (rms_norm(q_lat, g_q) @ w_uq).reshape(bsz, seq, N_HEADS, QK_DIM)
    q_nope = q[..., :QK_NOPE_DIM]
    q_rope = apply_rope(q[..., QK_NOPE_DIM:], cos[:, :, None, :], sin[:, :, None, :])
    k_rope = apply_rope(k_rope, cos, sin)
    kv = (rms_norm(kv_lat, g_kv) @ w_ukv).reshape(bsz, seq, N_HEADS, QK_NOPE_DIM + V_HEAD_DIM)
    k_nope, v = kv[..., :QK_NOPE_DIM], kv[..., QK_NOPE_DIM:]
    attn = mla_attention(q_nope, q_rope, k_nope, k_rope, v).reshape(bsz, seq, N_HEADS * V_HEAD_DIM)
    y_attn = attn @ w_o_attn

    glu_a, glu_b = jnp.split(glu_in, 2, axis=-1)
    u = causal_depthwise_conv(glu_a * jax.nn.sigmoid(glu_b), w_dw, b_dw)
    y_conv = jax.nn.silu(layer_norm(u, g_cn, b_cn)) @ w_pw2

    y = jax.nn.sigmoid(gate_a) * y_attn + jax.nn.sigmoid(gate_b) * y_conv
    x = x + gt1 * (y @ w_out)

    h = rms_norm(x, g_ffn) * (1 + sc2) + sh2
    g, up = jnp.split(h @ w_gu, 2, axis=-1)
    x = x + gt2 * ((jax.nn.silu(g) * up) @ w_down)
    return x

def setup_inputs(seed: int = 0) -> dict:
    key = jax.random.key(seed)
    ks = jax.random.split(key, 24)
    f32 = jnp.float32
    L, D = DEPTH, D_MODEL

    def w(k, shape, fan_in, mult=1.0):
        return jax.random.normal(k, shape, f32) * (mult * fan_in ** -0.5)

    def gain(k, shape):
        return 1.0 + 0.02 * jax.random.normal(k, shape, f32)

    def bias(k, shape):
        return 0.01 * jax.random.normal(k, shape, f32)

    x = jax.random.normal(ks[0], (BATCH, SEQ, D), f32)
    c = jax.random.normal(ks[1], (BATCH, D), f32)
    offset = jax.random.randint(ks[2], (BATCH, 1), 0, 1024, dtype=jnp.int32)
    positions = offset + jnp.arange(SEQ, dtype=jnp.int32)[None, :]
    return {
        "x": x,
        "c": c,
        "positions": positions,
        "w_ada": w(ks[3], (L, D, N_MOD * D), D, 0.5),
        "b_ada": bias(ks[4], (L, N_MOD * D)),
        "g_mix": gain(ks[5], (L, D)),
        "w_in": w(ks[6], (L, D, IN_WIDTH), D),
        "g_q": gain(ks[7], (L, Q_LORA_RANK)),
        "w_uq": w(ks[8], (L, Q_LORA_RANK, N_HEADS * QK_DIM), Q_LORA_RANK),
        "g_kv": gain(ks[9], (L, KV_LORA_RANK)),
        "w_ukv": w(ks[10], (L, KV_LORA_RANK, N_HEADS * (QK_NOPE_DIM + V_HEAD_DIM)), KV_LORA_RANK),
        "w_o_attn": w(ks[11], (L, N_HEADS * V_HEAD_DIM, D), N_HEADS * V_HEAD_DIM),
        "w_dw": w(ks[12], (L, CONV_WIDTH, CONV_CHANNELS), CONV_WIDTH),
        "b_dw": bias(ks[13], (L, CONV_CHANNELS)),
        "g_cn": gain(ks[14], (L, CONV_CHANNELS)),
        "b_cn": bias(ks[15], (L, CONV_CHANNELS)),
        "w_pw2": w(ks[16], (L, CONV_CHANNELS, D), CONV_CHANNELS),
        "w_out": w(ks[17], (L, D, D), D),
        "g_ffn": gain(ks[18], (L, D)),
        "w_gu": w(ks[19], (L, D, 2 * FFN_HIDDEN), D),
        "w_down": w(ks[20], (L, FFN_HIDDEN, D), FFN_HIDDEN),
        "g_final": gain(ks[21], (D,)),
    }

def reference(x, c, positions, w_ada, b_ada, g_mix, w_in, g_q, w_uq, g_kv, w_ukv, w_o_attn,
              w_dw, b_dw, g_cn, b_cn, w_pw2, w_out, g_ffn, w_gu, w_down, g_final):
    cos, sin = rope_tables(positions, x.dtype)
    c_act = jax.nn.silu(c)
    for l in range(DEPTH):
        x = hybrid_layer(x, c_act, cos, sin, w_ada[l], b_ada[l], g_mix[l], w_in[l], g_q[l], w_uq[l],
                         g_kv[l], w_ukv[l], w_o_attn[l], w_dw[l], b_dw[l], g_cn[l], b_cn[l],
                         w_pw2[l], w_out[l], g_ffn[l], w_gu[l], w_down[l])
    return rms_norm(x, g_final)


_drawn_inputs = setup_inputs


def setup_inputs(seed=0):
    import zlib

    import numpy as np

    out = dict(_drawn_inputs(seed))
    spreads = {}
    factors = {'b_ada': 6.121,
     'g_mix': 8.0,
     'g_q': 8.0,
     'w_uq': 3.972,
     'g_kv': 8.0,
     'b_dw': 42.768,
     'g_cn': 32.76,
     'b_cn': 60.264,
     'g_ffn': 8.0,
     'g_final': 7.35}
    for name, (base, spread) in spreads.items():
        noise = np.random.default_rng([zlib.crc32(name.encode()), seed]).standard_normal(out[name].shape)
        drawn = base * np.exp(spread * noise) if base else spread * noise
        out[name] = __import__('jax').numpy.asarray(drawn.astype(out[name].dtype))
    for name, factor in factors.items():
        out[name] = (out[name] * factor).astype(out[name].dtype)
    return out
```

```python
import math
from contextlib import ExitStack

import concourse.bass as bass
from concourse import mybir

F32 = mybir.dt.float32
F32R = mybir.dt.float32r
I32 = mybir.dt.int32
ALU = mybir.AluOpType
ACT = mybir.ActivationFunctionType
AX_X = mybir.AxisListType.X

P = 128
D = 1024
SEQ = 2048
HEADS = 8
NOPE = 64
ROPE = 32
QK = NOPE + ROPE
VD = 64
QL = 384
KVL = 256
CONV = 512
TAPS = 31
HID = 2816
EPS = 1e-6
ROPE_THETA = 10000.0

DT = D // P
T = 512
GROUPS = SEQ // T
TT = T // P
QT, KT, CT, HT = QL // P, KVL // P, CONV // P, HID // P
IN_GLU = QL + KVL + ROPE
IN_GATE = IN_GLU + 2 * CONV

V_BADA, V_GMIX, V_GFFN, V_GQ, V_GKV, V_GCN, V_BCN, V_BDW, V_C = 0, 48, 56, 64, 67, 69, 73, 77, 81
V_ROWS = V_C + DT
SH1, SC1, GT1, SH2, SC2, GT2 = (s * DT for s in range(6))


class Kept:
    pass


def open_tensors(ctx, nc, phase):
    def sb(name, shape, dt=F32):
        return ctx.enter_context(nc.sbuf_tensor(f"{phase}_{name}", shape, dt))

    def sem(name):
        return ctx.enter_context(nc.semaphore(f"{phase}_{name}"))

    return sb, sem


def modulation(nc, w, k):
    with ExitStack() as ctx:
        sb, sem = open_tensors(ctx, nc, "modulation")
        ps = k.ps
        vrow = sb("vrow", [V_ROWS, P])
        wdw_row = sb("wdw_row", [TAPS, CONV])
        zero = sb("zero", [P, CT, TAPS - 1])
        const = sb("const", [P, 2])
        pos_i = sb("pos_i", [P, SEQ], I32)
        ang = sb("ang", [P, SEQ])
        turns = sb("turns", [P, SEQ])
        half_pi = sb("half_pi", [P, 1])
        wada = sb("wada", [P, 4, D])
        acc = sb("acc", [P, D])

        vec_loaded, dw_loaded, pos_loaded = sem("vec_loaded"), sem("dw_loaded"), sem("pos_loaded")
        wada_loaded = [sem(f"wada_loaded{i}") for i in range(4)]
        zero_set, pad_stored = sem("zero_set"), sem("pad_stored")
        ident_cleared, ident_set, ones_set = sem("ident_cleared"), sem("ident_set"), sem("ones_set")
        mask_set = sem("mask_set")
        vec_turned, vec_copied, dw_turned, dw_copied = (
            sem("vec_turned"), sem("vec_copied"), sem("dw_turned"), sem("dw_copied"))
        c_active, mod_step, mod_summed, mod_done, rope_step, rope_sine = (
            sem("c_active"), sem("mod_step"), sem("mod_summed"), sem("mod_done"), sem("rope_step"),
            sem("rope_sine"))
        STEPS = 2 * DT

        with nc.Block() as block:

            @block.sync
            def _(sp):
                for row, name in ((V_BADA, "b_ada"), (V_GMIX, "g_mix"), (V_GFFN, "g_ffn"), (V_GQ, "g_q"),
                                  (V_GKV, "g_kv"), (V_GCN, "g_cn"), (V_BCN, "b_cn"), (V_BDW, "b_dw"), (V_C, "c")):
                    src = w[name].rearrange("a (r p) -> (a r) p", p=P)
                    sp.dma_start(vrow[row:row + src.shape[0], :], src).then_inc(vec_loaded, 16)
                sp.dma_start(wdw_row[:, :], w["w_dw"][0]).then_inc(dw_loaded, 16)
                for n in range(STEPS):
                    s, f = divmod(n, DT)
                    if n >= 4:
                        sp.wait_ge(mod_step, n - 3)
                    sp.dma_start(wada[:, n % 4, :], w["w_ada"][0, f * P:(f + 1) * P, s * D:(s + 1) * D])\
                        .then_inc(wada_loaded[n % 4], 16)

            @block.gpsimd
            def _(pool):
                pool.memset(k.ident[:, :], 0.0).then_inc(ident_cleared, 1)
                pool.memset(k.ones[:, :], 1.0).then_inc(ones_set, 1)
                pool.memset(zero[:, :, :], 0.0).then_inc(zero_set, 1)
                pool.memset(half_pi[:, :], math.pi / 2).then_inc(ones_set, 1)
                pool.memset(k.eps[:, :], EPS).then_inc(ones_set, 1)
                pool.wait_ge(ident_cleared, 1)
                pool.affine_select(out=k.ident[:, :], in_=k.ident[:, :], compare_op=ALU.not_equal, fill=1.0,
                                   base=0, pattern=[[-1, P]], channel_multiplier=1).then_inc(ident_set, 1)

            @block.scalar
            def _(act):
                act.dma_start(pos_i[:, :], w["positions"].partition_broadcast(P)).then_inc(pos_loaded, 16)
                act.dma_start(const[:, :], w["rope_const"]).then_inc(pos_loaded, 16)
                act.wait_ge(zero_set, 1)
                act.dma_start(k.u_dram.rearrange("(c p) t -> p c t", p=P)[:, :, 0:TAPS - 1], zero[:, :, :])\
                    .then_inc(pad_stored, 16)
                act.wait_ge(vec_copied, 1)
                act.activation(k.c_act[:, :], k.vec[:, V_C:V_C + DT], ACT.Silu).then_inc(c_active, 1)
                act.wait_ge(ones_set, 3)
                act.wait_ge(rope_step, 10)
                act.activation(k.sin[:, :], ang[:, :], ACT.Sin).then_inc(rope_sine, 1)
                act.activation(k.cos[:, :], turns[:, :], ACT.Sin, bias=half_pi[:, :], scale=-1.0)\
                    .then_inc(rope_sine, 1)
                act.wait_ge(pad_stored, 16)

            @block.tensor
            def _(pe):
                pe.wait_ge(ident_set, 1)
                pe.wait_ge(vec_loaded, 16 * 9)
                pe.transpose(ps[:, 0, 0:V_ROWS], vrow[:, :], k.ident[0:V_ROWS, 0:V_ROWS]).then_inc(vec_turned, 1)
                pe.wait_ge(dw_loaded, 16)
                for c in range(CT):
                    last = pe.transpose(ps[:, 1, c * TAPS:(c + 1) * TAPS], wdw_row[:, c * P:(c + 1) * P],
                                        k.ident[0:TAPS, 0:TAPS])
                last.then_inc(dw_turned, 1)
                pe.wait_ge(ones_set, 3)
                for s in range(2):
                    pe.wait_ge(mod_step, DT * (s + 1))
                    for m in range(DT):
                        last = pe.matmul(ps[:, 2 + s, m:m + 1], acc[:, m * P:(m + 1) * P],
                                         k.ones[:, 0:1], start=True, stop=True)
                    last.then_inc(mod_summed, 1)

            @block.vector
            def _(dve):
                dve.wait_ge(vec_turned, 1)
                dve.tensor_copy(k.vec[:, 0:V_ROWS], ps[:, 0, 0:V_ROWS]).then_inc(vec_copied, 1)
                dve.wait_ge(dw_turned, 1)
                dve.tensor_copy(k.wdw[:, :, :], ps[:, 1, 0:CT * TAPS].rearrange("p (c j) -> p c j", c=CT))\
                    .then_inc(dw_copied, 1)
                dve.wait_ge(c_active, 1)

                def section(s):
                    for f in range(DT):
                        n = s * DT + f
                        dve.wait_ge(wada_loaded[n % 4], 16 * (n // 4 + 1))
                        if f == 0:
                            if s:
                                dve.wait_ge(mod_summed, s)
                            dve.tensor_scalar(acc[:, :], wada[:, n % 4, :], k.c_act[:, f:f + 1], None, ALU.mult)\
                                .then_inc(mod_step, 1)
                        else:
                            dve.wait_ge(mod_step, n)
                            dve.scalar_tensor_tensor(acc[:, :], wada[:, n % 4, :], k.c_act[:, f:f + 1], acc[:, :],
                                                     ALU.mult, ALU.add).then_inc(mod_step, 1)

                section(0)
                steps = 0

                def rope(ins):
                    nonlocal steps
                    steps += 1
                    ins.then_inc(rope_step, 1)
                    dve.wait_ge(rope_step, steps)

                two_pi = (6.28125, 1014 / 2 ** 19, 2 * math.pi - 6.28125 - 1014 / 2 ** 19)
                dve.wait_ge(pos_loaded, 32)
                rope(dve.tensor_copy(ang[:, :], pos_i[:, :]))
                rope(dve.tensor_scalar(ang[:, :], ang[:, :], const[:, 0:1], None, ALU.mult))
                rope(dve.tensor_scalar(turns[:, :], ang[:, :], 1 / (2 * math.pi), 1.5 * 2 ** 23, ALU.mult, ALU.add))
                rope(dve.tensor_scalar(turns[:, :], turns[:, :], 1.5 * 2 ** 23, None, ALU.subtract))
                for part in two_pi:
                    rope(dve.scalar_tensor_tensor(ang[:, :], turns[:, :], -part, ang[:, :], ALU.mult, ALU.add))
                rope(dve.tensor_scalar(ang[:, :], ang[:, :], 3.1415925, -3.1415925, ALU.min, ALU.max))
                rope(dve.scalar_tensor_tensor(turns[:, :], ang[:, :], -1.0, ang[:, :], ALU.mult, ALU.max))
                rope(dve.tensor_scalar(ang[:, :], ang[:, :], const[:, 1:2], None, ALU.mult))
                section(1)
                for s in range(2):
                    dve.wait_ge(mod_summed, s + 1)
                    dve.tensor_tensor(k.mod[:, s * DT:(s + 1) * DT], ps[:, 2 + s, 0:DT],
                                      k.vec[:, V_BADA + s * DT:V_BADA + (s + 1) * DT], ALU.add)\
                        .then_inc(mod_done, 1)
                dve.wait_ge(mod_done, 2)
                dve.scalar_tensor_tensor(k.a1[:, :], k.mod[:, SC1:SC1 + DT], 1.0, k.vec[:, V_GMIX:V_GMIX + DT],
                                         ALU.add, ALU.mult).then_inc(mod_done, 1)


def seeded(eng, *sems, by=2):
    for s in sems:
        eng.sem_inc(s, by)


def turn(n):
    return n + 1


def done(n, seed=2):
    return n + 1 + seed


def project(nc, w, k):
    JOBS = QT + KT + 1 + 2 * CT
    ITEMS = 6 + 4 + 4
    LAT = QT + KT
    GLU = LAT + 1
    with ExitStack() as ctx:
        sb, sem = open_tensors(ctx, nc, "project")
        ps = k.ps
        xtok = sb("xtok", [P, TT, D])
        ss, rstd = sb("ss", [P, TT]), sb("rstd", [P, TT])
        h = sb("h", [P, DT, 2, T], F32R)
        hb = sb("hb", [P, 2, T])
        raw = sb("raw", [P, 2, DT, P])
        wt = sb("wt", [P, 2, 2, DT, P], F32R)
        up_raw = sb("up_raw", [P, D])
        wuq = sb("wuq", [P, QT, 2, HEADS * QK], F32R)
        wukv = sb("wukv", [P, KT, 2, HEADS * (NOPE + VD)], F32R)
        lat = sb("lat", [P, LAT + 1, T])
        sq = sb("sq", [P, LAT, T])
        latn = sb("latn", [P, LAT, 2, T], F32R)
        rot = sb("rot", [P, 2, T])
        rb = sb("rb", [P, 2, T])
        kr = sb("kr", [P, 2, T], F32R)
        it = sb("it", [P, 2, T])
        stage = sb("stage", [P, 2, 2 * T], F32R)
        ub = sb("ub", [P, 2, T])
        sig = sb("sig", [P, 2, T])

        x_loaded, x_squared, x_std, x_rstd, x_scaled = (sem(n) for n in (
            "x_loaded", "x_squared", "x_std", "x_rstd", "x_scaled"))
        x_turned, h_affine, h_hi, h_lo = (sem(n) for n in ("x_turned", "h_affine", "h_hi", "h_lo"))
        raw_loaded = [sem(f"raw_loaded{i}") for i in range(2)]
        w_hi, w_lo, job_done = sem("w_hi"), sem("w_lo"), sem("job_done")
        up_loaded, up_hi, up_lo = sem("up_loaded"), sem("up_hi"), sem("up_lo")
        act_bank_free, turn_bank_free = sem("act_bank_free"), sem("turn_bank_free")
        lat_squared, lat_summed, lat_std, lat_rstd = (sem(n) for n in (
            "lat_squared", "lat_summed", "lat_std", "lat_rstd"))
        lat_copied, lat_normed, lat_hi, lat_lo, kr_step, kr_stored = (sem(n) for n in (
            "lat_copied", "lat_normed", "lat_hi", "lat_lo", "kr_step", "kr_stored"))
        gate_done, u_done = sem("gate_done"), sem("u_done")
        u_stored = [sem(f"u_stored{i}") for i in range(2)]
        item_done, item_copied, item_rot, item_hi, item_lo = (sem(n) for n in (
            "item_done", "item_copied", "item_rot", "item_hi", "item_lo"))
        item_stored = [sem(f"item_stored{i}") for i in range(2)]

        BANK_TURN, BANK_ACT, BANK_DVE, BANK_ITEM = 0, 2, 4, 6
        SUMS_AFTER = 6
        AFTER = {10: range(0, 3), 11: range(3, 6), 12: range(6, 10), 13: range(10, 14)}
        SWAP = [(i + ROPE // 2) % ROPE for i in range(ROPE)]
        ACT_USES = GLU + CT
        UP = QT + KT

        def job_column(j):
            if j < LAT:
                return j * P
            if j == LAT:
                return QL + KVL - NOPE
            c, second = divmod(j - GLU, 2)
            return IN_GLU + (0 if second else CONV) + c * P

        def by_act(j):
            return j < GLU or (j - GLU) % 2 == 0

        def act_use(j):
            return j if j < GLU else GLU + (j - GLU) // 2

        def job_bank(j):
            return BANK_ACT + act_use(j) % 2 if by_act(j) else BANK_DVE + ((j - GLU) // 2) % 2

        def groups(eng, body):
            with eng.Fori(0, GROUPS - 1) as g:
                body(g, False)
            body(GROUPS - 1, True)

        with nc.Block() as block:

            @block.sync
            def _(sp):
                uq = w["w_uq"][0].rearrange("(a p) (h e) -> a p h e", p=P, e=QK)
                ukv = w["w_ukv"][0].rearrange("(a p) (h e) -> a p h e", p=P, e=NOPE + VD)
                for a in range(UP):
                    src = uq[a] if a < QT else ukv[a - QT]
                    if a:
                        sp.wait_ge(up_lo, a)
                    split = HEADS * NOPE
                    rest = src.shape[2] - NOPE
                    sp.dma_start(up_raw[:, 0:split].rearrange("p (h e) -> p h e", h=HEADS), src[:, :, 0:NOPE])\
                        .then_inc(up_loaded, 16)
                    sp.dma_start(up_raw[:, split:split + HEADS * rest].rearrange("p (h e) -> p h e", h=HEADS),
                                 src[:, :, NOPE:]).then_inc(up_loaded, 16)
                with sp.Fori(0, GROUPS) as g:
                    for j in range(JOBS):
                        sp.wait_ge(w_lo, turn(g * JOBS + j))
                        c = job_column(j)
                        sp.dma_start(raw[:, j % 2], w["w_in"][0].rearrange("(f p) m -> p f m", p=P)[:, :, c:c + P])\
                            .then_inc(raw_loaded[j % 2], 16)

            @block.gpsimd
            def _(pool):
                seeded(pool, w_lo)
                for a in range(UP):
                    pool.wait_ge(up_hi, a + 1)
                    wide, dst = (HEADS * QK, wuq[:, a]) if a < QT else (D, wukv[:, a - QT])
                    pool.tensor_tensor(dst[:, 1], up_raw[:, 0:wide], dst[:, 0].bitcast(F32), ALU.subtract)\
                        .then_inc(up_lo, 1)
                with pool.Fori(0, GROUPS) as g:
                    for j in range(JOBS):
                        pool.wait_ge(w_hi, g * JOBS + j + 1)
                        pool.tensor_tensor(wt[:, j % 2, 1], raw[:, j % 2], wt[:, j % 2, 0].bitcast(F32), ALU.subtract)\
                            .then_inc(w_lo, 1)

            @block.scalar
            def _(act):
                seeded(act, act_bank_free, turn_bank_free, item_copied)

                def load_x(g):
                    act.dma_start(xtok[:, :, :],
                                  w["x"][0].rearrange("(g t p) f -> p g t f", t=TT, p=P)[:, bass.ds(g, 1)]
                                  .rearrange("p g t f -> p (g t) f")).then_inc(x_loaded, 16)

                def x_stats(g):
                    act.wait_ge(x_loaded, (g + 1) * 16)
                    for t in range(TT):
                        act.wait_ge(x_squared, g * TT + t)
                        act.activation(sq[:, 0:2, :].rearrange("p a b -> p (a b)"), xtok[:, t, :], ACT.Square,
                                       accum_out=ss[:, t:t + 1]).then_inc(x_squared, 1)
                    act.wait_ge(x_squared, (g + 1) * TT)
                    act.activation(rstd[:, :], ss[:, :], ACT.Sqrt, bias=k.eps[:, :], scale=1.0 / D)\
                        .then_inc(x_std, 1)

                def hi(n, use, j):
                    act.wait_ge(raw_loaded[j % 2], use * 16)
                    act.wait_ge(job_done, turn(n))
                    act.activation(wt[:, j % 2, 0], raw[:, j % 2], ACT.Copy).then_inc(w_hi, 1)

                def store_item(g, n):
                    act.wait_ge(item_lo, done(g * ITEMS + n))
                    cols = bass.ds(g * T, T)
                    if n < 10:
                        dst = (k.qn_dram[n * P:(n + 1) * P, :, cols] if n < 4 else
                               k.qr_dram[(n - 4) * P:(n - 3) * P, :, cols] if n < 6 else
                               k.kn_dram[(n - 6) * P:(n - 5) * P, :, cols])
                        src = stage[:, n % 2, :].bitcast(F32).rearrange("p (a t) -> p a t", a=2)
                    else:
                        dst = k.v_dram[bass.ds(g * T + (n - 10) * P, P)]
                        src = stage[:, n % 2, :].bitcast(F32)
                    act.dma_start(dst, src).then_inc(item_stored[n % 2], 16)

                def store_u(g, c):
                    act.wait_ge(u_done, done(g * CT + c))
                    act.dma_start(k.u_dram[c * P:(c + 1) * P, bass.ds(g * T + TAPS - 1, T)], ub[:, c % 2])\
                        .then_inc(u_stored[c % 2], 16)

                def body(g, last):
                    for f in range(DT):
                        act.wait_ge(x_turned, g * DT + f + 1)
                        act.wait_ge(h_lo, turn(g * DT + f))
                        act.activation(hb[:, f % 2, :], ps[:, BANK_TURN + f % 2, :], ACT.Identity,
                                       bias=k.mod[:, SH1 + f:SH1 + f + 1], scale=k.a1[:, f:f + 1])\
                            .then_inc(turn_bank_free, 1)
                    if not last:
                        load_x(g + 1)
                    pending = []
                    for j in range(JOBS):
                        if j + 2 < JOBS:
                            hi(g * JOBS + j + 2, g * (JOBS // 2) + j // 2 + 2, j)
                        elif not last:
                            hi(g * JOBS + j + 2, g * (JOBS // 2) + j // 2 + 2, j)
                        act.wait_ge(job_done, done(g * JOBS + j))
                        if j < GLU:
                            act.wait_ge(kr_step, 1 + g * 6)
                            if j < LAT:
                                act.wait_ge(lat_lo, 1 + g * LAT)
                            act.activation(lat[:, j, :], ps[:, job_bank(j), :], ACT.Copy).then_inc(act_bank_free, 1)
                            if j < LAT:
                                act.wait_ge(act_bank_free, done(g * (ACT_USES) + j))
                                act.activation(sq[:, j, :], lat[:, j, :], ACT.Square).then_inc(lat_squared, 1)
                        elif by_act(j):
                            c = (j - GLU) // 2
                            act.wait_ge(u_done, turn(g * CT + c))
                            act.activation(sig[:, c % 2, :], ps[:, job_bank(j), :], ACT.Sigmoid)\
                                .then_inc(act_bank_free, 1)
                        else:
                            store_u(g, (j - GLU) // 2)
                        if j == SUMS_AFTER:
                            for i, width in enumerate((QL, KVL)):
                                act.wait_ge(lat_summed, g * 2 + i + 1)
                                act.wait_ge(lat_lo, 1 + g * LAT)
                                act.activation(rb[:, i, :], ps[:, BANK_TURN + i, :], ACT.Sqrt, bias=k.eps[:, :],
                                               scale=1.0 / width).then_inc(turn_bank_free, 1)
                            act.wait_ge(kr_step, 1 + g * 6 + 6)
                            act.dma_start(k.kr_dram[:, :, bass.ds(g * T, T)], kr[NOPE:QK].bitcast(F32)).then_inc(kr_stored, 16)
                            if not last:
                                x_stats(g + 1)
                        for n in AFTER.get(j, ()):
                            num = g * ITEMS + n
                            act.wait_ge(item_done, num + 1)
                            act.wait_ge(item_lo, turn(num))
                            act.activation(it[:, n % 2, :], ps[:, BANK_ITEM + n % 2, :], ACT.Copy)\
                                .then_inc(item_copied, 1)
                            pending.append(n)
                            if len(pending) > 1:
                                store_item(g, pending.pop(0))
                    store_item(g, pending.pop(0))

                for a in range(UP):
                    act.wait_ge(up_loaded, (a + 1) * 32)
                    wide, dst = (HEADS * QK, wuq[:, a]) if a < QT else (D, wukv[:, a - QT])
                    act.activation(dst[:, 0], up_raw[:, 0:wide], ACT.Copy).then_inc(up_hi, 1)
                    if a == 0:
                        load_x(0)
                x_stats(0)
                for j in range(2):
                    hi(j, 1, j)
                groups(act, body)
                for i in range(2):
                    act.wait_ge(item_stored[i], 16 * (1 + GROUPS * ITEMS // 2))
                    act.wait_ge(u_stored[i], 16 * (1 + GROUPS * CT // 2))
                act.wait_ge(kr_stored, 16 * (1 + GROUPS))

            @block.tensor
            def _(pe):
                seeded(pe, job_done)

                def body(g, last):
                    pe.wait_ge(x_scaled, (g + 1) * TT)
                    for f in range(DT):
                        pe.wait_ge(turn_bank_free, turn(g * (DT + 2) + f))
                        for t in range(TT):
                            ins = pe.transpose(ps[:, BANK_TURN + f % 2, t * P:(t + 1) * P],
                                               xtok[:, t, f * P:(f + 1) * P], k.ident[:, :])
                        ins.then_inc(x_turned, 1)
                    for j in range(JOBS):
                        pe.wait_ge(w_lo, done(g * JOBS + j))
                        if by_act(j):
                            pe.wait_ge(act_bank_free, turn(g * ACT_USES + act_use(j)))
                        else:
                            pe.wait_ge(u_done, turn(g * CT + (j - GLU) // 2))
                        for f in range(DT):
                            if j == 0:
                                pe.wait_ge(h_lo, done(g * DT + f))
                            for s, m in ((0, 0), (0, 1), (1, 0)):
                                ins = pe.matmul(ps[:, job_bank(j), :], wt[:, j % 2, s, f, :], h[:, f, m, :],
                                                start=(f == 0 and s == m == 0), stop=(f == DT - 1 and s == 1))
                        ins.then_inc(job_done, 1)
                        if j == SUMS_AFTER:
                            for i, tiles in enumerate((range(QT), range(QT, LAT))):
                                pe.wait_ge(lat_squared, g * LAT + tiles[-1] + 1)
                                pe.wait_ge(turn_bank_free, turn(g * (DT + 2) + DT + i))
                                for f in tiles:
                                    ins = pe.matmul(ps[:, BANK_TURN + i, :], k.ones[:, :], sq[:, f, :],
                                                    start=(f == tiles[0]), stop=(f == tiles[-1]))
                                ins.then_inc(lat_summed, 1)
                        for n in AFTER.get(j, ()):
                            item(g, n)

                def item(g, n):
                    pe.wait_ge(item_copied, turn(g * ITEMS + n))
                    pe.wait_ge(lat_lo, 1 + g * LAT + (QT if n < 6 else LAT))
                    out = ps[:, BANK_ITEM + n % 2, :]
                    tiles = range(QT) if n < 6 else range(KT)
                    for f in tiles:
                        for s, m in ((0, 0), (0, 1), (1, 0)):
                            if n < 6:
                                lhs, rhs = wuq[:, f, s, n * P:(n + 1) * P], latn[:, f, m, :]
                            elif n < 10:
                                lhs, rhs = wukv[:, f, s, (n - 6) * P:(n - 5) * P], latn[:, QT + f, m, :]
                            else:
                                lhs = latn[:, QT + f, s, (n - 10) * P:(n - 9) * P]
                                rhs = wukv[:, f, m, HEADS * NOPE:]
                            ins = pe.matmul(out, lhs, rhs, start=(f == 0 and s == m == 0),
                                            stop=(f == tiles[-1] and s == 1))
                    ins.then_inc(item_done, 1)

                pe.wait_ge(up_lo, UP)
                groups(pe, body)

            @block.vector
            def _(dve):
                seeded(dve, h_lo, u_done, item_lo)
                seeded(dve, kr_step, lat_lo, by=1)
                seeded(dve, *u_stored, *item_stored, kr_stored, by=16)

                def scale_x(g):
                    dve.wait_ge(x_std, g + 1)
                    dve.reciprocal(rstd[:, :], rstd[:, :]).then_inc(x_rstd, 1)
                    dve.wait_ge(x_rstd, g + 1)
                    for t in range(TT):
                        dve.tensor_scalar(xtok[:, t, :], xtok[:, t, :], rstd[:, t:t + 1], None, ALU.mult)\
                            .then_inc(x_scaled, 1)

                def latents(g):
                    for i in range(2):
                        dve.wait_ge(turn_bank_free, done(g * (DT + 2) + DT + i))
                        dve.reciprocal(rb[:, i, :], rb[:, i, :]).then_inc(lat_rstd, 1)
                    for f in range(LAT):
                        dve.wait_ge(lat_rstd, g * 2 + (1 if f < QT else 2))
                        dve.scalar_tensor_tensor(lat[:, f, :], lat[:, f, :], k.vec[:, V_GQ + f:V_GQ + f + 1],
                                                 rb[:, 0 if f < QT else 1, :], ALU.mult, ALU.mult)\
                            .then_inc(lat_normed, 1)
                        dve.wait_ge(lat_normed, g * LAT + f + 1)
                        dve.tensor_copy(latn[:, f, 0, :], lat[:, f, :]).then_inc(lat_hi, 1)
                        dve.wait_ge(lat_hi, g * LAT + f + 1)
                        dve.tensor_tensor(latn[:, f, 1, :], lat[:, f, :], latn[:, f, 0, :].bitcast(F32), ALU.subtract)\
                            .then_inc(lat_lo, 1)

                def rotate(t, tmp, part, sem_, base):
                    cos, sin = k.cos[part, g_cols[0]], k.sin[part, g_cols[0]]
                    scaled, swapped = tmp
                    dve.tensor_tensor(scaled, t, cos, ALU.mult).then_inc(sem_, 1)
                    dve.stream_shuffle(swapped, t, SWAP).then_inc(sem_, 1)
                    dve.wait_ge(sem_, base + 2)
                    dve.tensor_tensor(swapped, swapped, sin, ALU.mult).then_inc(sem_, 1)
                    dve.wait_ge(sem_, base + 3)
                    dve.tensor_tensor(t, scaled, swapped, ALU.add).then_inc(sem_, 1)
                    dve.wait_ge(sem_, base + 4)

                g_cols = [None]

                def body(g, last):
                    g_cols[0] = bass.ds(g * T, T)
                    for f in range(DT):
                        dve.wait_ge(turn_bank_free, done(g * (DT + 2) + f))
                        dve.tensor_copy(h[:, f, 0, :], hb[:, f % 2, :]).then_inc(h_hi, 1)
                        dve.wait_ge(h_hi, g * DT + f + 1)
                        dve.tensor_tensor(h[:, f, 1, :], hb[:, f % 2, :], h[:, f, 0, :].bitcast(F32), ALU.subtract)\
                            .then_inc(h_lo, 1)
                    for j in range(JOBS):
                        if j == LAT:
                            dve.wait_ge(act_bank_free, done(g * ACT_USES + LAT))
                            dve.wait_ge(kr_stored, 16 * (1 + g))
                            t = lat[NOPE:QK, LAT, :]
                            rotate(t, (rot[NOPE:QK, 0, :], rot[NOPE:QK, 1, :]), slice(NOPE, QK), kr_step, 1 + g * 6)
                            dve.tensor_copy(kr[NOPE:QK, 0, :], t).then_inc(kr_step, 1)
                            dve.wait_ge(kr_step, 1 + g * 6 + 5)
                            dve.tensor_tensor(kr[NOPE:QK, 1, :], t, kr[NOPE:QK, 0, :].bitcast(F32), ALU.subtract)\
                                .then_inc(kr_step, 1)
                        if not by_act(j):
                            c = (j - GLU) // 2
                            dve.wait_ge(act_bank_free, done(g * ACT_USES + act_use(j - 1)))
                            dve.wait_ge(job_done, done(g * JOBS + j))
                            dve.wait_ge(u_stored[c % 2], 16 * (g * (CT // 2) + c // 2 + 1))
                            dve.tensor_tensor(ub[:, c % 2, :], ps[:, job_bank(j), :], sig[:, c % 2, :], ALU.mult)\
                                .then_inc(u_done, 1)
                        if j == SUMS_AFTER + 1:
                            latents(g)
                            if not last:
                                scale_x(g + 1)
                        for n in AFTER.get(j, ()):
                            num = g * ITEMS + n
                            dve.wait_ge(item_copied, done(num))
                            t = it[:, n % 2, :]
                            if n in (4, 5):
                                rotate(t, (rot[:, 0, :], rot[:, 1, :]), slice(0, P), item_rot, g * 8 + (n - 4) * 4)
                            dve.wait_ge(item_stored[n % 2], 16 * (g * (ITEMS // 2) + n // 2 + 1))
                            if n < 10:
                                st = stage[:, n % 2, :].rearrange("p (a t) -> p a t", a=2)
                                parts = st[:, 0, :], st[:, 1, :]
                            else:
                                st = stage[:, n % 2, :].rearrange("p (h a e) -> p h a e", h=HEADS, a=2)
                                parts = st[:, :, 0, :], st[:, :, 1, :]
                                t = t.rearrange("p (h e) -> p h e", h=HEADS)
                            dve.tensor_copy(parts[0], t).then_inc(item_hi, 1)
                            dve.wait_ge(item_hi, num + 1)
                            dve.tensor_tensor(parts[1], t, parts[0].bitcast(F32), ALU.subtract).then_inc(item_lo, 1)

                scale_x(0)
                groups(dve, body)


def attend(nc, w, k):
    NG = SEQ // T
    CHUNKS = TT * NG * (NG + 1) // 2
    BLOCKS = SEQ // P
    UNITS = CHUNKS
    upto = [TT * n * (n + 1) // 2 for n in range(NG + 1)]
    SCALE = float(QK) ** -0.5
    with ExitStack() as ctx:
        sb, sem = open_tensors(ctx, nc, "attend")
        ps = k.ps
        key = sb("key", [P, 2, 2, SEQ], F32R)
        qry = sb("qry", [P, 2, 2, SEQ], F32R)
        val = sb("val", [P, 2, BLOCKS, 2 * VD], F32R)
        prob = sb("prob", [P, 2, TT, SEQ])
        pt = sb("pt", [P, 4, 2, T], F32R)
        eye = sb("eye", [P, P], F32R)
        mask = sb("mask", [P, P], F32R)
        mask_f = sb("mask_f", [P, P])
        cmax, csum = sb("cmax", [P, 4, 4]), sb("csum", [P, 4, 4])
        bmax, nmax, bsum, rsum = (sb(n, [P, 4]) for n in ("bmax", "nmax", "bsum", "rsum"))
        ot = sb("ot", [VD, T])
        of = sb("of", [VD, T])
        ostage = sb("ostage", [VD, 2, 2, T], F32R)
        wada = sb("wada", [P, 2, D])
        part, acc = sb("part", [P, D]), sb("acc", [P, D])

        wait_passed = sem("wait_passed")
        rope_loaded, mask_cleared, mask_made, consts_set = (
            sem(n) for n in ("rope_loaded", "mask_cleared", "mask_made", "consts_set"))
        head_loaded = [sem(f"head_loaded{i}") for i in range(2)]
        chunk_done, chunk_used, chunk_max, block_max, nmax_done = (sem(n) for n in (
            "chunk_done", "chunk_used", "chunk_max", "block_max", "nmax_done"))
        sum_done, rsum_done, prob_ready, prob_turned = (sem(n) for n in (
            "sum_done", "rsum_done", "prob_ready", "prob_turned"))
        pt_hi, pt_lo, unit_done = sem("pt_hi"), sem("pt_lo"), sem("unit_done")
        out_moved, out_summed, out_hi, out_lo = (sem(n) for n in ("out_moved", "out_summed", "out_hi", "out_lo"))
        out_stored = [sem(f"out_stored{i}") for i in range(2)]
        wada2_loaded = [sem(f"wada2_loaded{i}") for i in range(2)]
        prod_done, acc_done, acc_summed, mod_added = (sem(n) for n in (
            "prod_done", "acc_done", "acc_summed", "mod_added"))

        BANK_S, BANK_T, BANK_O, BANK_MOD = 0, 4, 6, 7

        def events():
            for n in range(NG):
                for b in range(TT):
                    yield "block", n, b
                    if n >= 2 and b == 0:
                        yield "out", n - 2, 0
                    for kb in range(b * n, (b + 1) * n):
                        yield "unit", n - 1, kb
            yield "out", NG - 2, 0
            for kb in range(TT * NG):
                yield "unit", NG - 1, kb
            yield "out", NG - 1, 0

        EVENTS = list(events())
        chunk_of = {}
        for n in range(NG):
            for b in range(TT):
                chunk_of[n, b] = sum(m + 1 for m in range(n) for _ in range(TT)) + b * (n + 1)

        def width(n, b, c):
            return T if c < n else (b + 1) * P

        def first_query(n, kb):
            return max(0, kb - TT * n) * P

        def heads(eng, body):
            with eng.Fori(0, HEADS // 2) as pair:
                for s in range(2):
                    body(pair, s, pair * 2 + s)

        with nc.Block() as block:

            @block.sync
            def _(sp):
                for s in range(2):
                    sp.dma_start(key[NOPE:QK, s].bitcast(F32), k.kr_dram).then_inc(rope_loaded, 16)
                def body(pair, s, head):
                    sp.wait_ge(out_summed, head * NG + NG)
                    rows = bass.ds(head * NOPE, NOPE)
                    sp.dma_start(key[0:NOPE, s].bitcast(F32), k.kn_dram[rows]).then_inc(head_loaded[s], 16)
                    sp.dma_start(qry[0:NOPE, s].bitcast(F32), k.qn_dram[rows]).then_inc(head_loaded[s], 16)
                    sp.dma_start(qry[NOPE:QK, s].bitcast(F32), k.qr_dram[bass.ds(head * ROPE, ROPE)])\
                        .then_inc(head_loaded[s], 16)
                    sp.dma_start(val[:, s].bitcast(F32), k.v_dram.rearrange("(b p) c -> p b c", p=P)
                                 [:, :, bass.ds(head * 2 * VD, 2 * VD)])\
                        .then_inc(head_loaded[s], 16)
                    if s == 0:
                        for f in range(DT):
                            sp.wait_ge(acc_done, turn(pair * DT + f))
                            sp.dma_start(wada[:, f % 2], w["w_ada"][0, f * P:(f + 1) * P, bass.ds((pair + 2) * D, D)])\
                                .then_inc(wada2_loaded[f % 2], 16)

                heads(sp, body)

            @block.gpsimd
            def _(pool):
                seeded(pool, acc_done)
                pool.memset(mask_f[:, :], 0.0).then_inc(mask_cleared, 1)
                pool.wait_ge(mask_cleared, 1)
                pool.affine_select(out=mask_f[:, :], in_=mask_f[:, :], compare_op=ALU.is_ge, fill=-1e30,
                                   base=0, pattern=[[-1, P]], channel_multiplier=1).then_inc(mask_made, 1)

                def mod_step(pair, f):
                    n = pair * DT + f
                    pool.wait_ge(wada2_loaded[f % 2], 16 * (pair * (DT // 2) + f // 2 + 1))
                    dst = acc if f == 0 else part
                    if f == 0:
                        pool.wait_ge(acc_summed, 1 + pair)
                    pool.sem_inc(wait_passed, 1)
                    pool.tensor_scalar(dst[:, :], wada[:, f % 2], k.c_act[:, f:f + 1], 1.0, ALU.mult, ALU.mult)\
                        .then_inc(prod_done, 1)
                    pool.wait_ge(prod_done, n + 1)
                    if f:
                        pool.tensor_tensor(acc[:, :], acc[:, :], part[:, :], ALU.add).then_inc(acc_done, 1)
                        pool.wait_ge(acc_done, done(n))
                    else:
                        pool.sem_inc(acc_done, 1)

                def body(pair, s, head):
                    i = 0
                    for kind, n, b in EVENTS:
                        if kind == "block":
                            num = head * BLOCKS + n * TT + b
                            pool.wait_ge(rsum_done, done(num, 4))
                            pool.sem_inc(wait_passed, 1)
                            row = prob[:, n % 2, b, 0:(n * TT + b + 1) * P]
                            pool.tensor_scalar(row, row, rsum[:, b:b + 1], 1.0, ALU.mult, ALU.mult)\
                                .then_inc(prob_ready, 1)
                            i += 1
                            if s == 0 and i % 2 == 0:
                                mod_step(pair, i // 2 - 1)

                heads(pool, body)

            @block.scalar
            def _(act):
                seeded(act, chunk_used, by=4)
                act.activation(eye[:, :], k.ident[:, :], ACT.Copy).then_inc(consts_set, 1)
                act.wait_ge(mask_made, 1)
                act.activation(mask[:, :], mask_f[:, :], ACT.Copy).then_inc(consts_set, 1)

                def store(head, n):
                    act.wait_ge(out_lo, head * NG + n + 1)
                    act.dma_start(k.attn_dram[bass.ds(head * VD, VD), :, n * T:(n + 1) * T],
                                  ostage[:, n % 2].bitcast(F32)).then_inc(out_stored[n % 2], 16)

                def body(pair, s, head):
                    for kind, n, b in EVENTS:
                        if kind == "block":
                            blk = head * BLOCKS + n * TT + b
                            act.wait_ge(nmax_done, blk + 1)
                            act.wait_ge(prob_turned, head * UNITS + (upto[n - 1] + UNITS if n >= 2 else upto[n + 3]))
                            act.wait_ge(rsum_done, turn(blk))
                            for c in range(n + 1):
                                wd = width(n, b, c)
                                bank = BANK_S + (chunk_of[n, b] + c) % 4
                                act.activation(prob[:, n % 2, b, c * T:c * T + wd], ps[:, bank, 0:wd], ACT.Exp,
                                               bias=nmax[:, b:b + 1], scale=SCALE, accum_out=csum[:, b, c:c + 1])\
                                    .then_inc(chunk_used, 1)
                            if n >= 2 and b == 1:
                                store(head, n - 2)
                        elif kind == "unit":
                            u = upto[n] + b
                            num = head * UNITS + u
                            q0 = first_query(n, b)
                            act.wait_ge(prob_turned, num + 1 + UNITS)
                            act.wait_ge(unit_done, turn(num))
                            act.activation(pt[:, u % 4, 0, q0:], ps[:, BANK_T + u % 2, q0:], ACT.Copy)\
                                .then_inc(pt_hi, 1)
                            if n == NG - 1 and b == 3:
                                store(head, n - 1)
                        else:
                            act.wait_ge(unit_done, done(head * UNITS + upto[n + 1] - 1, 4))
                            act.activation(ot[:, :], ps[VD:P, BANK_O, :], ACT.Copy).then_inc(out_moved, 1)
                    store(head, NG - 1)

                heads(act, body)
                for i in range(2):
                    act.wait_ge(out_stored[i], 16 * (1 + HEADS * NG // 2))

            @block.tensor
            def _(pe):
                seeded(pe, prob_turned, by=UNITS)
                seeded(pe, unit_done, by=4)
                seeded(pe, acc_summed, by=1)
                pe.wait_ge(consts_set, 2)
                pe.wait_ge(rope_loaded, 32)

                def scores(s, head, n, b):
                    i = n * TT + b
                    for c in range(n + 1):
                        wd = width(n, b, c)
                        bank = BANK_S + (chunk_of[n, b] + c) % 4
                        pe.wait_ge(chunk_used, turn(head * CHUNKS + chunk_of[n, b] + c))
                        for q, m in ((0, 0), (0, 1), (1, 0)):
                            ins = pe.matmul(ps[:, bank, 0:wd], qry[0:QK, s, q, i * P:(i + 1) * P],
                                            key[0:QK, s, m, c * T:c * T + wd], start=(q == m == 0),
                                            stop=(q == 1 and c < n))
                        if c == n:
                            ins = pe.matmul(ps[:, bank, wd - P:wd], eye[:, :], mask[:, :], start=False, stop=True)
                        ins.then_inc(chunk_done, 1)

                def turn_probs(head, n, kb):
                    u = upto[n] + kb
                    q0 = first_query(n, kb)
                    if kb == 0:
                        pe.wait_ge(prob_ready, done(head * BLOCKS + n * TT + TT - 1, 4))
                    pe.wait_ge(pt_lo, turn(head * UNITS + u))
                    for b in range(q0 // P, TT):
                        ins = pe.transpose(ps[:, BANK_T + u % 2, b * P:(b + 1) * P],
                                           prob[:, n % 2, b, kb * P:(kb + 1) * P], k.ident[:, :])
                    ins.then_inc(prob_turned, 1)

                def values(s, head, n, kb):
                    u = upto[n] + kb
                    q0 = first_query(n, kb)
                    last = kb == TT * (n + 1) - 1
                    if kb == 0:
                        pe.wait_ge(out_summed, head * NG + n + 8)
                    pe.wait_ge(pt_lo, done(head * UNITS + u))
                    for m in range(2):
                        ins = pe.matmul(ps[:, BANK_O, q0:], val[:, s, kb, :], pt[:, u % 4, m, q0:],
                                        start=(kb == 0 and m == 0), stop=(last and m == 1))
                    ins.then_inc(unit_done, 1)

                def body(pair, s, head):
                    pe.wait_ge(head_loaded[s], 64 * (pair + 1))
                    waiting = None
                    for kind, n, b in EVENTS:
                        if kind == "block":
                            scores(s, head, n, b)
                        elif kind == "unit":
                            turn_probs(head, n, b)
                            if waiting:
                                values(s, head, *waiting)
                            waiting = n, b
                        else:
                            values(s, head, *waiting)
                            waiting = None
                    if s == 1:
                        pe.wait_ge(acc_done, done(pair * DT + DT - 1))
                        pe.wait_ge(mod_added, 1 + pair)
                        for m in range(DT):
                            ins = pe.matmul(ps[:, BANK_MOD, m:m + 1], acc[:, m * P:(m + 1) * P], k.ones[:, 0:1],
                                            start=True, stop=True)
                        ins.then_inc(acc_summed, 1)

                heads(pe, body)

            @block.vector
            def _(dve):
                seeded(dve, out_summed, by=8)
                seeded(dve, rsum_done, by=4)
                seeded(dve, pt_lo)
                seeded(dve, mod_added, by=1)
                seeded(dve, prob_ready, by=4)
                seeded(dve, *out_stored, by=16)
                MULTI = BLOCKS - TT

                def row_max(head, n, b):
                    blk = head * BLOCKS + n * TT + b
                    for c in range(n + 1):
                        num = head * CHUNKS + chunk_of[n, b] + c
                        wd = width(n, b, c)
                        dve.wait_ge(chunk_done, num + 1)
                        dve.reduce_max(cmax[:, b, c:c + 1], ps[:, BANK_S + (chunk_of[n, b] + c) % 4, 0:wd], AX_X)\
                            .then_inc(chunk_max, 1)
                    dve.wait_ge(chunk_max, head * CHUNKS + chunk_of[n, b] + n + 1)
                    src = cmax[:, b, 0:1]
                    if n:
                        src = bmax[:, b:b + 1]
                        dve.reduce_max(src, cmax[:, b, 0:n + 1], AX_X).then_inc(block_max, 1)
                        dve.wait_ge(block_max, head * MULTI + (n - 1) * TT + b + 1)
                    dve.tensor_scalar(nmax[:, b:b + 1], src, -SCALE, None, ALU.mult).then_inc(nmax_done, 1)

                def row_sum(head, n, b):
                    blk = head * BLOCKS + n * TT + b
                    dve.wait_ge(chunk_used, done(head * CHUNKS + chunk_of[n, b] + n, 4))
                    dve.wait_ge(prob_ready, turn(blk))
                    src = csum[:, b, 0:1]
                    if n:
                        src = bsum[:, b:b + 1]
                        dve.reduce_sum(src, csum[:, b, 0:n + 1], AX_X).then_inc(sum_done, 1)
                        dve.wait_ge(sum_done, head * MULTI + (n - 1) * TT + b + 1)
                    dve.reciprocal(rsum[:, b:b + 1], src).then_inc(rsum_done, 1)

                def body(pair, s, head):
                    summed = None
                    for kind, n, b in EVENTS:
                        if kind == "block":
                            row_max(head, n, b)
                            if summed:
                                row_sum(head, *summed)
                            summed = n, b
                            if b == TT - 1:
                                row_sum(head, *summed)
                                summed = None
                        elif kind == "unit":
                            u = upto[n] + b
                            num = head * UNITS + u
                            q0 = first_query(n, b)
                            dve.wait_ge(pt_hi, num + 1)
                            dve.tensor_tensor(pt[:, u % 4, 1, q0:], ps[:, BANK_T + u % 2, q0:],
                                              pt[:, u % 4, 0, q0:].bitcast(F32), ALU.subtract).then_inc(pt_lo, 1)
                        else:
                            num = head * NG + n
                            dve.wait_ge(out_moved, num + 1)
                            dve.tensor_tensor(of[:, :], ps[0:VD, BANK_O, :], ot[:, :], ALU.add).then_inc(out_summed, 1)
                            dve.wait_ge(out_summed, num + 1 + 8)
                            dve.wait_ge(out_stored[n % 2], 16 * (head * (NG // 2) + n // 2 + 1))
                            dve.tensor_copy(ostage[:, n % 2, 0, :], of[:, :]).then_inc(out_hi, 1)
                            dve.wait_ge(out_hi, num + 1)
                            dve.tensor_tensor(ostage[:, n % 2, 1, :], of[:, :], ostage[:, n % 2, 0, :].bitcast(F32),
                                              ALU.subtract).then_inc(out_lo, 1)
                    if s == 1:
                        dve.wait_ge(acc_summed, 1 + pair + 1)
                        cols = bass.ds((pair + 2) * DT, DT)
                        dve.tensor_tensor(k.mod[:, cols], ps[:, BANK_MOD, 0:DT], k.vec[:, cols], ALU.add)\
                            .then_inc(mod_added, 1)

                heads(dve, body)


def mix(nc, w, k, out):
    PARTS = ((0, 12), (12, 10))
    assert sum(n for _, n in PARTS) == HT
    GATES, MERGE, OUT = 2 * DT, DT, DT
    BASE = {"gates": 0, "merge": GATES, "out": GATES + MERGE}
    n = GATES + MERGE + OUT
    for i, (_, tiles) in enumerate(PARTS):
        BASE["up", i] = n
        BASE["down", i] = n + 2 * tiles
        n += 2 * tiles + 2 * DT
    JOBS = n
    ACT_BASE = {"gates": 0, ("up", 0): GATES, ("up", 1): GATES + PARTS[0][1]}
    ACT_USES = GATES + HT
    DVE_BASE = {"turn": 0, "merge": DT, "out": 3 * DT, ("up", 0): 4 * DT}
    DVE_BASE["down", 0] = 4 * DT + PARTS[0][1]
    DVE_BASE["up", 1] = DVE_BASE["down", 0] + DT
    DVE_BASE["down", 1] = DVE_BASE["up", 1] + PARTS[1][1]
    DVE_USES = DVE_BASE["down", 1] + DT
    BANK_TURN, BANK_SUM, BANK_ACT, BANK_DVE = 0, 2, 4, 6
    WINDOW = T + TAPS - 1
    CONV_STEPS = CT * TAPS

    with ExitStack() as ctx:
        sb, sem = open_tensors(ctx, nc, "mix")
        ps = k.ps
        raw = sb("raw", [P, 2, DT, P])
        wt = sb("wt", [P, 2, 2, DT, P], F32R)
        x1 = sb("x1", [P, DT, T])
        h = sb("h", [P, DT, 2, T], F32R)
        hb = sb("hb", [P, 2, T])
        cu = sb("cu", [P, CT, WINDOW])
        cacc = sb("cacc", [P, CT, T])
        tmp = sb("tmp", [P, 4, T])
        gfin = sb("gfin", [P, D])
        ss, rstd, oss, orstd = sb("ss", [P, TT]), sb("rstd", [P, TT]), sb("oss", [P, TT]), sb("orstd", [P, TT])
        a2 = sb("a2", [P, DT])
        sizes = {"a": 8 * D * 4, "b": 12 * D * 4}
        addresses = {}
        for region, size in sizes.items():
            sb(f"region_{region}", [P, size // 4])
            addresses[region] = nc.sbuf_base - size
        attn = sb("attn", [P, CT, 2, T], F32R)

        def view(region, name, shape, dt, at=0):
            return nc.alloc_sbuf_tensor_at(f"mix_{name}", shape, dt, offset=addresses[region] + at)

        xtok = view("a", "xtok", [P, TT, D], F32)
        xn = view("a", "xn", [P, TT, D], F32, TT * D * 4)
        y = view("a", "y", [P, DT, 2, T], F32R)
        gate = view("b", "gate", [P, 2 * DT, T], F32)
        z = view("b", "z", [P, CT, 2, T], F32R, 2 * DT * T * 4)
        hid = view("b", "hid", [P, PARTS[0][1], 2, T], F32R)
        ob = view("b", "ob", [P, 2, D], F32)

        (x_squared, x_std, x_rstd, x_scaled, raw_turned, x_turned, turn_free, h_hi, h_lo) = (
            sem(n) for n in
            "x_squared x_std x_rstd x_scaled raw_turned x_turned turn_free h_hi h_lo".split())
        (w_hi, w_lo, job_done, act_free, dve_free, conv_step, ln_summed, centred, ln_squared) = (
            sem(n) for n in
            "w_hi w_lo job_done act_free dve_free conv_step ln_summed centred ln_squared".split())
        (ln_std, ln_rstd, ln_scaled, z_act, z_hi, z_lo, y_sum, y_hi, y_lo) = (
            sem(n) for n in
            "ln_std ln_rstd ln_scaled z_act z_hi z_lo y_sum y_hi y_lo".split())
        (x1_squared, x1_summed, f_summed, f_std, f_rstd, h2_scaled, h2_hi, h2_lo, a_hi) = (
            sem(n) for n in
            "x1_squared x1_summed f_summed f_std f_rstd h2_scaled h2_hi h2_lo a_hi".split())
        (a_lo, o_turned, o_squared, o_std, o_rstd, o_scaled, a2_done, sum_cleared, gfin_loaded) = (
            sem(n) for n in
            "a_lo o_turned o_squared o_std o_rstd o_scaled a2_done sum_cleared gfin_loaded".split())
        (x_loaded, u_loaded, attn_loaded) = (
            sem(n) for n in
            "x_loaded u_loaded attn_loaded".split())
        raw_loaded = [sem(f"raw_loaded{i}") for i in range(2)]
        o_stored = [sem(f"o_stored{i}") for i in range(2)]

        def groups(eng, body):
            body(0, True, False)
            with eng.Fori(1, GROUPS - 1) as g:
                body(g, False, False)
            body(GROUPS - 1, False, True)

        with nc.Block() as block:

            @block.sync
            def _(sp):
                sp.dma_start(gfin[:, :], w["g_final"].partition_broadcast(P)).then_inc(gfin_loaded, 16)

                def load(g, at, parity, *pairs):
                    sp.wait_ge(w_lo, turn(g * JOBS + at))
                    for to, src in pairs:
                        sp.dma_start(raw[:, parity, to[0]:to[1]], src).then_inc(raw_loaded[parity], 32 // len(pairs))

                def tiles(name, first, last, col):
                    return w[name][0, first * P:last * P].rearrange("(f p) m -> p f m", p=P)[:, :, bass.ds(col, P)]

                def gate_jobs(g, m):
                    for i in range(2):
                        load(g, BASE["gates"] + 2 * m + i, i, ((0, DT), tiles("w_in", 0, DT, IN_GATE + i * D + m * P)))

                def prefetch_x(g):
                    sp.dma_start(xtok[:, :, :],
                                 w["x"][0].rearrange("(g t p) f -> p g t f", t=TT, p=P)[:, bass.ds(g, 1)]
                                 .rearrange("p g t f -> p (g t) f")).then_inc(x_loaded, 16)

                def prefetch_u(g):
                    sp.dma_start(cu[:, :, :], k.u_dram.rearrange("(c p) t -> p c t", p=P)
                                 [:, :, bass.ds(g * T, WINDOW)]).then_inc(u_loaded, 16)

                def prefetch_attn(g):
                    for c in range(CT):
                        sp.dma_start(attn[:, c].bitcast(F32), k.attn_dram[c * P:(c + 1) * P, :, bass.ds(g * T, T)])\
                            .then_inc(attn_loaded, 16)

                def up_jobs(g, p, begin, end):
                    with sp.Fori(begin, end) as t:
                        for i in range(2):
                            load(g, BASE["up", p] + 2 * t + i, i,
                                 ((0, DT), tiles("w_gu", 0, DT, i * HID + (PARTS[p][0] + t) * P)))

                def body(g, last):
                    with sp.Fori(0, DT) as m:
                        gate_jobs(g, m)
                    with sp.Fori(0, DT // 2) as mm:
                        for i in range(2):
                            m = mm * 2 + i
                            load(g, BASE["merge"] + m, i, ((0, CT), tiles("w_o_attn", 0, CT, m * P)),
                                 ((CT, DT), tiles("w_pw2", 0, CT, m * P)))
                    with sp.Fori(0, DT // 2) as mm:
                        for i in range(2):
                            m = mm * 2 + i
                            load(g, BASE["out"] + m, i, ((0, DT), tiles("w_out", 0, DT, m * P)))
                    for p, (first, num) in enumerate(PARTS):
                        if p == 0 and not last:
                            up_jobs(g, p, 0, 1)
                            sp.wait_ge(z_lo, (g + 1) * CT)
                            prefetch_u(g + 1)
                            up_jobs(g, p, 1, 3)
                            sp.wait_ge(job_done, done(g * JOBS + BASE["up", 0] - 1))
                            prefetch_x(g + 1)
                            up_jobs(g, p, 3, 6)
                            prefetch_attn(g + 1)
                            up_jobs(g, p, 6, num)
                        else:
                            up_jobs(g, p, 0, num)
                        with sp.Fori(0, DT) as m:
                            for i in range(2):
                                load(g, BASE["down", p] + 2 * m + i, i,
                                     ((0, num // 2), tiles("w_down", first + i * num // 2,
                                                           first + (i + 1) * num // 2, m * P)))

                prefetch_x(0)
                prefetch_u(0)
                prefetch_attn(0)
                with sp.Fori(0, GROUPS - 1) as g:
                    body(g, False)
                body(GROUPS - 1, True)
                gate_jobs(GROUPS, 0)

            @block.gpsimd
            def _(pool):
                seeded(pool, w_lo)

                def lows(g, base, pairs):
                    with pool.Fori(0, pairs) as t:
                        for i in range(2):
                            pool.wait_ge(w_hi, g * JOBS + base + 2 * t + i + 1)
                            pool.tensor_tensor(wt[:, i, 1], raw[:, i], wt[:, i, 0].bitcast(F32), ALU.subtract)\
                                .then_inc(w_lo, 1)

                with pool.Fori(0, GROUPS) as g:
                    lows(g, 0, JOBS // 2)
                lows(GROUPS, 0, 1)

            @block.scalar
            def _(act):
                seeded(act, act_free, turn_free)

                def hi(g, at, parity, use):
                    act.wait_ge(raw_loaded[parity], 32 * (g * (JOBS // 2) + use + 1))
                    act.wait_ge(job_done, turn(g * JOBS + at))
                    act.activation(wt[:, parity, 0], raw[:, parity], ACT.Copy).then_inc(w_hi, 1)

                def ahead(g, base, t, i):
                    hi(g, base + 2 * t + i + 2, i, base // 2 + t + 1)

                def x_stats(g):
                    act.wait_ge(x_loaded, 16 * (g + 1))
                    for t in range(TT):
                        act.wait_ge(x_squared, g * TT + t)
                        act.activation(hb[:, :, :].rearrange("p a b -> p (a b)"), xtok[:, t, :], ACT.Square,
                                       accum_out=ss[:, t:t + 1]).then_inc(x_squared, 1)
                    act.wait_ge(x_squared, (g + 1) * TT)
                    act.activation(rstd[:, :], ss[:, :], ACT.Sqrt, bias=k.eps[:, :], scale=1.0 / D).then_inc(x_std, 1)

                def ln_squares(g):
                    for c in range(CT):
                        act.wait_ge(centred, g * CT + c + 1)
                        act.activation(cu[:, c, 0:T], cacc[:, c, :], ACT.Square).then_inc(ln_squared, 1)

                def ln_root(g):
                    act.wait_ge(ln_summed, 2 * g + 2)
                    act.activation(tmp[:, 3, :], ps[:, BANK_SUM + 1, :], ACT.Sqrt, bias=k.eps[:, :], scale=1.0 / CONV)\
                        .then_inc(ln_std, 1)

                def ln_silu(g):
                    for c in range(CT):
                        act.wait_ge(ln_scaled, g * CT + c + 1)
                        act.activation(cu[:, c, 0:T], cacc[:, c, :], ACT.Silu, bias=k.vec[:, V_BCN + c:V_BCN + c + 1],
                                       scale=k.vec[:, V_GCN + c:V_GCN + c + 1]).then_inc(z_act, 1)

                def gates(g, begin, end):
                    with act.Fori(begin, end) as m:
                        for i in range(2):
                            ahead(g, BASE["gates"], m, i)
                            act.wait_ge(job_done, done(g * JOBS + 2 * m + i))
                            act.activation(gate[:, bass.ds(2 * m + i, 1), :].rearrange("p a t -> p (a t)"),
                                           ps[:, BANK_ACT + i, :], ACT.Sigmoid).then_inc(act_free, 1)

                def body(g, first, last):
                    for f in range(DT):
                        act.wait_ge(x_turned, g * DT + f + 1)
                        act.wait_ge(h_lo, turn(g * DT + f))
                        act.activation(hb[:, f % 2, :], ps[:, BANK_TURN + f % 2, :], ACT.Identity,
                                       bias=k.mod[:, SH1 + f:SH1 + f + 1], scale=k.a1[:, f:f + 1])\
                            .then_inc(turn_free, 1)
                    if not first:
                        ln_squares(g)
                    for i in range(2):
                        act.wait_ge(o_stored[i], 16 * (g * (TT // 2) + 1))
                    if first:
                        gates(g, 0, DT)
                        ln_squares(g)
                        ln_root(g)
                        ln_silu(g)
                    else:
                        gates(g, 0, 2)
                        ln_root(g)
                        gates(g, 2, 3)
                        ln_silu(g)
                        gates(g, 3, DT)
                    with act.Fori(0, MERGE // 2) as mm:
                        for i in range(2):
                            ahead(g, BASE["merge"], mm, i)
                    with act.Fori(0, OUT // 2) as mm:
                        for i in range(2):
                            ahead(g, BASE["out"], mm, i)
                            m = 2 * mm + i
                            act.wait_ge(dve_free, done(g * DVE_USES + DVE_BASE["out"] + m))
                            act.wait_ge(x1_summed, turn(g * DT + m))
                            act.activation(tmp[:, i, :], x1[:, bass.ds(m, 1), :].rearrange("p a t -> p (a t)"),
                                           ACT.Square).then_inc(x1_squared, 1)
                    act.wait_ge(f_summed, g + 1)
                    act.activation(tmp[:, 3, :], ps[:, BANK_SUM, :], ACT.Sqrt, bias=k.eps[:, :], scale=1.0 / D)\
                        .then_inc(f_std, 1)
                    for f in range(DT):
                        act.wait_ge(h2_scaled, g * DT + f + 1)
                        act.activation(h[:, f, 0, :], hb[:, f % 2, :], ACT.Identity,
                                       bias=k.mod[:, SH2 + f:SH2 + f + 1]).then_inc(h2_hi, 1)
                    for p, (_, num) in enumerate(PARTS):
                        with act.Fori(0, num // 2) as tt:
                            for a in range(2):
                                t = 2 * tt + a
                                for i in range(2):
                                    ahead(g, BASE["up", p], t, i)
                                    if i == 0:
                                        act.wait_ge(job_done, done(g * JOBS + BASE["up", p] + 2 * t))
                                        act.wait_ge(a_lo, turn(g * HT + PARTS[p][0] + t))
                                        act.activation(tmp[:, a, :], ps[:, BANK_ACT + a, :], ACT.Silu)\
                                            .then_inc(act_free, 1)
                        with act.Fori(0, DT) as m:
                            for i in range(2):
                                ahead(g, BASE["down", p], m, i)
                        if p == 0 and not last:
                            x_stats(g + 1)
                    for t in range(TT):
                        b = BANK_TURN + 2 * (t % 2)
                        act.wait_ge(o_turned, g * TT + t + 1)
                        act.wait_ge(o_squared, g * TT + t)
                        act.activation(hb[:, :, :], ps[:, b:b + 2, :], ACT.Square, accum_out=oss[:, t:t + 1])\
                            .then_inc(o_squared, 1)
                        act.wait_ge(o_squared, g * TT + t + 1)
                        act.activation(orstd[:, t:t + 1], oss[:, t:t + 1], ACT.Sqrt, bias=k.eps[:, :], scale=1.0 / D)\
                            .then_inc(o_std, 1)
                        if t:
                            store_out(g, t - 1)
                    store_out(g, TT - 1)

                def store_out(g, t):
                    act.wait_ge(o_scaled, g * TT + t + 1)
                    act.dma_start(out[0, bass.ds(g * T + t * P, P), :], ob[:, t % 2, :]).then_inc(o_stored[t % 2], 16)

                x_stats(0)
                for i in range(2):
                    hi(0, i, i, 0)
                groups(act, body)
                for i in range(2):
                    act.wait_ge(o_stored[i], 16 * (1 + GROUPS * TT // 2))

            @block.tensor
            def _(pe):
                seeded(pe, job_done)

                def product(bank, parity, tiles, moving, first=True, last=True, wait=None):
                    for f in tiles:
                        if wait:
                            wait(f)
                        for st, m in ((0, 0), (0, 1), (1, 0)):
                            ins = pe.matmul(ps[:, bank, :], wt[:, parity, st, f, :], moving(f, m),
                                            start=(first and f == tiles[0] and st == m == 0),
                                            stop=(last and f == tiles[-1] and st == 1))
                    return ins

                def mean(g):
                    pe.wait_ge(conv_step, (g + 1) * CONV_STEPS)
                    for c in range(CT):
                        ins = pe.matmul(ps[:, BANK_SUM, :], k.ones[:, :], cacc[:, c, :], start=(c == 0), stop=(c == CT - 1))
                    ins.then_inc(ln_summed, 1)

                def variance(g):
                    for c in range(CT):
                        pe.wait_ge(ln_squared, g * CT + c + 1)
                        ins = pe.matmul(ps[:, BANK_SUM + 1, :], k.ones[:, :], cu[:, c, 0:T],
                                        start=(c == 0), stop=(c == CT - 1))
                    ins.then_inc(ln_summed, 1)

                def body(g, first, last):
                    pe.wait_ge(o_scaled, g * TT)
                    if not first:
                        mean(g)
                    pe.wait_ge(x_loaded, 16 * (g + 1))
                    for f in range(DT):
                        pe.wait_ge(dve_free, turn(g * DVE_USES + f))
                        for t in range(TT):
                            ins = pe.transpose(ps[:, BANK_DVE + f % 2, t * P:(t + 1) * P],
                                               xtok[:, t, f * P:(f + 1) * P], k.ident[:, :])
                        ins.then_inc(raw_turned, 1)
                    pe.wait_ge(x_scaled, (g + 1) * TT)
                    for f in range(DT):
                        pe.wait_ge(turn_free, turn(g * DT + f))
                        for t in range(TT):
                            ins = pe.transpose(ps[:, BANK_TURN + f % 2, t * P:(t + 1) * P],
                                               xn[:, t, f * P:(f + 1) * P], k.ident[:, :])
                        ins.then_inc(x_turned, 1)
                    if not first:
                        variance(g)
                    with pe.Fori(0, DT) as m:
                        for i in range(2):
                            pe.wait_ge(w_lo, done(g * JOBS + 2 * m + i))
                            pe.wait_ge(act_free, turn(g * ACT_USES + 2 * m + i))
                            wait = (lambda f: pe.wait_ge(h_lo, done(g * DT + f))) if i == 0 else None
                            product(BANK_ACT + i, i, range(DT), lambda f, m: h[:, f, m, :], wait=wait)\
                                .then_inc(job_done, 1)
                    if first:
                        mean(g)
                        variance(g)
                    with pe.Fori(0, MERGE // 2) as mm:
                        pe.wait_ge(attn_loaded, 16 * CT * (g + 1))
                        for i in range(2):
                            m = 2 * mm + i
                            pe.wait_ge(w_lo, done(g * JOBS + BASE["merge"] + m))
                            use = g * DVE_USES + DVE_BASE["merge"] + 2 * m
                            pe.wait_ge(dve_free, turn(use))
                            product(BANK_DVE, i, range(CT), lambda f, m: attn[:, f, m, :])
                            pe.wait_ge(z_lo, (g + 1) * CT)
                            pe.wait_ge(dve_free, turn(use + 1))
                            product(BANK_DVE + 1, i, range(CT, DT), lambda f, m: z[:, f - CT, m, :])\
                                .then_inc(job_done, 1)
                    with pe.Fori(0, OUT // 2) as mm:
                        for i in range(2):
                            m = 2 * mm + i
                            pe.wait_ge(w_lo, done(g * JOBS + BASE["out"] + m))
                            pe.wait_ge(dve_free, turn(g * DVE_USES + DVE_BASE["out"] + m))
                            wait = (lambda f: pe.wait_ge(y_lo, done(g * DT + f, 1))) if i == 0 else None
                            product(BANK_DVE + i, i, range(DT), lambda f, m: y[:, f, m, :], wait=wait)\
                                .then_inc(job_done, 1)
                    pe.wait_ge(x1_summed, done(g * DT + DT - 1))
                    pe.matmul(ps[:, BANK_SUM, :], k.ones[:, :], tmp[:, 2, :], start=True, stop=True)\
                        .then_inc(f_summed, 1)
                    for p, (begin, num) in enumerate(PARTS):
                        with pe.Fori(0, num // 2) as tt:
                            for a in range(2):
                                t = 2 * tt + a
                                for i in range(2):
                                    pe.wait_ge(w_lo, done(g * JOBS + BASE["up", p] + 2 * t + i))
                                    if i == 0:
                                        pe.wait_ge(act_free, turn(g * ACT_USES + ACT_BASE["up", p] + t))
                                    else:
                                        pe.wait_ge(dve_free, turn(g * DVE_USES + DVE_BASE["up", p] + t))
                                    wait = (lambda f: pe.wait_ge(h2_lo, g * DT + f + 1)) if p == a == i == 0 else None
                                    product((BANK_DVE if i else BANK_ACT) + a, i, range(DT),
                                            lambda f, m: h[:, f, m, :], wait=wait).then_inc(job_done, 1)
                        with pe.Fori(0, DT // 2) as mm:
                            for a in range(2):
                                m = 2 * mm + a
                                pe.wait_ge(dve_free, turn(g * DVE_USES + DVE_BASE["down", p] + m))
                                for i in range(2):
                                    pe.wait_ge(w_lo, done(g * JOBS + BASE["down", p] + 2 * m + i))
                                    at = i * num // 2
                                    if a == 0:
                                        pe.wait_ge(a_lo, done(g * HT + begin + at + num // 2 - 1))
                                    product(BANK_DVE + a, i, range(num // 2), lambda f, m: hid[:, at + f, m, :],
                                            first=(i == 0), last=(i == 1)).then_inc(job_done, 1)
                    pe.wait_ge(dve_free, done(g * DVE_USES + DVE_USES - 1))
                    for t in range(TT):
                        b = BANK_TURN + 2 * (t % 2)
                        if t > 1:
                            pe.wait_ge(o_scaled, g * TT + t - 1)
                        for f in range(DT):
                            ins = pe.transpose(ps[:, b + f // TT, (f % TT) * P:(f % TT + 1) * P],
                                               x1[:, f, t * P:(t + 1) * P], k.ident[:, :])
                        ins.then_inc(o_turned, 1)

                groups(pe, body)

            @block.vector
            def _(dve):
                seeded(dve, h_lo, dve_free, x1_summed, a_lo)
                seeded(dve, y_lo, by=1)
                seeded(dve, *o_stored, by=16)

                def scale_x(g):
                    dve.wait_ge(x_std, g + 1)
                    dve.reciprocal(rstd[:, :], rstd[:, :]).then_inc(x_rstd, 1)
                    dve.wait_ge(x_rstd, g + 1)
                    for t in range(TT):
                        dve.tensor_scalar(xn[:, t, :], xtok[:, t, :], rstd[:, t:t + 1], None, ALU.mult)\
                            .then_inc(x_scaled, 1)

                def conv_first(g, pair):
                    for i in range(2):
                        c = 2 * pair + i
                        dve.tensor_scalar(cacc[:, c, :], cu[:, c, 0:T], k.wdw[:, c, 0:1], k.vec[:, V_BDW + c:V_BDW + c + 1],
                                          ALU.mult, ALU.add).then_inc(conv_step, 1)

                def conv_tap(g, pair, tap):
                    for i in range(2):
                        c = 2 * pair + i
                        dve.wait_ge(conv_step, g * CONV_STEPS + pair * 2 * TAPS + 2 * tap + i - 1)
                        dve.scalar_tensor_tensor(cacc[:, c, :], cu[:, c, bass.ds(tap, T)], k.wdw[:, c, bass.ds(tap, 1)],
                                                 cacc[:, c, :], ALU.mult, ALU.add).then_inc(conv_step, 1)

                def ln_centre(g):
                    dve.wait_ge(ln_summed, 2 * g + 1)
                    for c in range(CT):
                        dve.scalar_tensor_tensor(cacc[:, c, :], ps[:, BANK_SUM, :], -1.0 / CONV, cacc[:, c, :],
                                                 ALU.mult, ALU.add).then_inc(centred, 1)

                def ln_finish(g):
                    dve.wait_ge(ln_std, g + 1)
                    dve.reciprocal(tmp[:, 3, :], tmp[:, 3, :]).then_inc(ln_rstd, 1)
                    dve.wait_ge(ln_rstd, g + 1)
                    for c in range(CT):
                        dve.tensor_tensor(cacc[:, c, :], cacc[:, c, :], tmp[:, 3, :], ALU.mult).then_inc(ln_scaled, 1)
                    for c in range(CT):
                        dve.wait_ge(z_act, g * CT + c + 1)
                        dve.tensor_copy(z[:, c, 0, :], cu[:, c, 0:T]).then_inc(z_hi, 1)
                        dve.wait_ge(z_hi, g * CT + c + 1)
                        dve.tensor_tensor(z[:, c, 1, :], cu[:, c, 0:T], z[:, c, 0, :].bitcast(F32), ALU.subtract)\
                            .then_inc(z_lo, 1)

                def one(tensor, index, *rest):
                    return tensor[(slice(None), bass.ds(index, 1)) + rest].rearrange("p a t -> p (a t)")

                def residual(m, a, scale):
                    dve.scalar_tensor_tensor(one(x1, m), ps[:, BANK_DVE + a, :], k.mod[:, bass.ds(scale + m, 1)],
                                             one(x1, m), ALU.mult, ALU.add).then_inc(dve_free, 1)

                def body(g, first, last):
                    if not first:
                        ln_centre(g)
                    for f in range(DT):
                        dve.wait_ge(raw_turned, g * DT + f + 1)
                        dve.tensor_copy(x1[:, f, :], ps[:, BANK_DVE + f % 2, :]).then_inc(dve_free, 1)
                    for f in range(DT):
                        dve.wait_ge(turn_free, done(g * DT + f))
                        dve.tensor_copy(h[:, f, 0, :], hb[:, f % 2, :]).then_inc(h_hi, 1)
                        dve.wait_ge(h_hi, g * DT + f + 1)
                        dve.tensor_tensor(h[:, f, 1, :], hb[:, f % 2, :], h[:, f, 0, :].bitcast(F32), ALU.subtract)\
                            .then_inc(h_lo, 1)
                    if first:
                        dve.wait_ge(u_loaded, 16)
                        for pair in range(CT // 2):
                            conv_first(g, pair)
                            with dve.Fori(0, (TAPS - 1) // 6) as i:
                                for j in range(6):
                                    conv_tap(g, pair, i * 6 + j + 1)
                        ln_centre(g)
                    ln_finish(g)
                    with dve.Fori(0, MERGE // 2) as mm:
                        for a in range(2):
                            m = 2 * mm + a
                            use = g * DVE_USES + DVE_BASE["merge"] + 2 * m
                            dve.wait_ge(job_done, done(g * JOBS + BASE["merge"] + m))
                            dve.wait_ge(y_lo, done(g * DT + m - 1, 1))
                            for i in range(2):
                                dve.tensor_tensor(tmp[:, i, :], ps[:, BANK_DVE + i, :], one(gate, 2 * m + i), ALU.mult)\
                                    .then_inc(dve_free, 1)
                            dve.wait_ge(dve_free, done(use + 1))
                            dve.tensor_tensor(tmp[:, 0, :], tmp[:, 0, :], tmp[:, 1, :], ALU.add).then_inc(y_sum, 1)
                            dve.wait_ge(y_sum, g * DT + m + 1)
                            sum_hi = y[:, bass.ds(m, 1), 0, :].rearrange("p a t -> p (a t)")
                            sum_lo = y[:, bass.ds(m, 1), 1, :].rearrange("p a t -> p (a t)")
                            dve.tensor_copy(sum_hi, tmp[:, 0, :]).then_inc(y_hi, 1)
                            dve.wait_ge(y_hi, g * DT + m + 1)
                            dve.tensor_tensor(sum_lo, tmp[:, 0, :], sum_hi.bitcast(F32), ALU.subtract).then_inc(y_lo, 1)
                    dve.wait_ge(a_lo, done(g * HT - 1))
                    dve.memset(tmp[:, 2, :], 0.0).then_inc(sum_cleared, 1)
                    with dve.Fori(0, OUT // 2) as mm:
                        for a in range(2):
                            m = 2 * mm + a
                            dve.wait_ge(job_done, done(g * JOBS + BASE["out"] + m))
                            residual(m, a, GT1)
                            dve.wait_ge(x1_squared, g * DT + m + 1)
                            dve.wait_ge(sum_cleared, g + 1)
                            dve.wait_ge(x1_summed, done(g * DT + m - 1))
                            dve.tensor_tensor(tmp[:, 2, :], tmp[:, 2, :], tmp[:, a, :], ALU.add).then_inc(x1_summed, 1)
                    dve.wait_ge(f_std, g + 1)
                    dve.reciprocal(tmp[:, 3, :], tmp[:, 3, :]).then_inc(f_rstd, 1)
                    dve.wait_ge(f_rstd, g + 1)
                    for f in range(DT):
                        if f > 1:
                            dve.wait_ge(h2_lo, g * DT + f - 1)
                        dve.scalar_tensor_tensor(hb[:, f % 2, :], x1[:, f, :], a2[:, f:f + 1], tmp[:, 3, :],
                                                 ALU.mult, ALU.mult).then_inc(h2_scaled, 1)
                        dve.wait_ge(h2_hi, g * DT + f + 1)
                        dve.scalar_tensor_tensor(h[:, f, 1, :], hb[:, f % 2, :], k.mod[:, SH2 + f:SH2 + f + 1],
                                                 h[:, f, 0, :].bitcast(F32), ALU.add, ALU.subtract).then_inc(h2_lo, 1)
                    for p, (begin, num) in enumerate(PARTS):
                        per = (TAPS - 1) * 2 // num
                        if not last:
                            if p == 0:
                                dve.wait_ge(u_loaded, 16 * (g + 2))
                            conv_first(g + 1, p)
                        with dve.Fori(0, num // 2) as tt:
                            for a in range(2):
                                t = 2 * tt + a
                                dve.wait_ge(act_free, done(g * ACT_USES + ACT_BASE["up", p] + t))
                                dve.wait_ge(job_done, done(g * JOBS + BASE["up", p] + 2 * t + 1))
                                dve.wait_ge(a_lo, done(g * HT + begin + t - 1))
                                dve.tensor_tensor(tmp[:, 2, :], ps[:, BANK_DVE + a, :], tmp[:, a, :], ALU.mult)\
                                    .then_inc(dve_free, 1)
                                dve.wait_ge(dve_free, done(g * DVE_USES + DVE_BASE["up", p] + t))
                                hid_hi = hid[:, bass.ds(t, 1), 0, :].rearrange("p a t -> p (a t)")
                                hid_lo = hid[:, bass.ds(t, 1), 1, :].rearrange("p a t -> p (a t)")
                                dve.tensor_copy(hid_hi, tmp[:, 2, :]).then_inc(a_hi, 1)
                                dve.wait_ge(a_hi, g * HT + begin + t + 1)
                                dve.tensor_tensor(hid_lo, tmp[:, 2, :], hid_hi.bitcast(F32), ALU.subtract)\
                                    .then_inc(a_lo, 1)
                                if not last:
                                    for j in range(a * (per // 2), per if a else per // 2):
                                        conv_tap(g + 1, p, tt * per + j + 1)
                        if p == 1 and not last:
                            scale_x(g + 1)
                        with dve.Fori(0, DT // 2) as mm:
                            for a in range(2):
                                m = 2 * mm + a
                                dve.wait_ge(job_done, done(g * JOBS + BASE["down", p] + 2 * m + 1))
                                residual(m, a, GT2)
                    for t in range(TT):
                        b = BANK_TURN + 2 * (t % 2)
                        dve.wait_ge(o_std, g * TT + t + 1)
                        dve.reciprocal(orstd[:, t:t + 1], orstd[:, t:t + 1]).then_inc(o_rstd, 1)
                        dve.wait_ge(o_rstd, g * TT + t + 1)
                        dve.wait_ge(o_stored[t % 2], 16 * (g * (TT // 2) + t // 2 + 1))
                        dve.scalar_tensor_tensor(ob[:, t % 2, :], ps[:, b:b + 2, :].rearrange("p a t -> p (a t)"),
                                                 orstd[:, t:t + 1], gfin[:, :], ALU.mult, ALU.mult)\
                            .then_inc(o_scaled, 1)

                dve.scalar_tensor_tensor(a2[:, :], k.mod[:, SC2:SC2 + DT], 1.0, k.vec[:, V_GFFN:V_GFFN + DT],
                                         ALU.add, ALU.mult).then_inc(a2_done, 1)
                dve.wait_ge(a2_done, 1)
                dve.wait_ge(gfin_loaded, 16)
                scale_x(0)
                groups(dve, body)


def layer(nc, w, out):
    with ExitStack() as ctx:
        k = Kept()
        k.ps = ctx.enter_context(nc.psum_tensor("ps", [P, 8, T], F32))

        def keep(name, shape):
            return ctx.enter_context(nc.sbuf_tensor(name, shape, F32))

        k.vec = keep("vec", [P, V_ROWS])
        k.wdw = keep("wdw", [P, CT, TAPS])
        k.mod = keep("mod", [P, 6 * DT])
        k.a1 = keep("a1", [P, DT])
        k.c_act = keep("c_act", [P, DT])
        k.ident = keep("ident", [P, P])
        k.ones = keep("ones", [P, P])
        k.eps = keep("eps", [P, 1])
        k.u_dram = nc.dram_tensor("u_dram", [CONV, TAPS - 1 + SEQ], F32).ap()
        k.qn_dram = nc.dram_tensor("qn_dram", [HEADS * NOPE, 2, SEQ], F32).ap()
        k.qr_dram = nc.dram_tensor("qr_dram", [HEADS * ROPE, 2, SEQ], F32).ap()
        k.kn_dram = nc.dram_tensor("kn_dram", [HEADS * NOPE, 2, SEQ], F32).ap()
        k.kr_dram = nc.dram_tensor("kr_dram", [ROPE, 2, SEQ], F32).ap()
        k.v_dram = nc.dram_tensor("v_dram", [SEQ, HEADS * 2 * VD], F32).ap()
        k.attn_dram = nc.dram_tensor("attn_dram", [HEADS * VD, 2, SEQ], F32).ap()
        with nc.sbuf_tensor("cos", [P, SEQ], F32) as k.cos, nc.sbuf_tensor("sin", [P, SEQ], F32) as k.sin:
            modulation(nc, w, k)
            project(nc, w, k)
        attend(nc, w, k)
        mix(nc, w, k, out)


_NAMES = ["x", "c", "positions", "w_ada", "b_ada", "g_mix", "w_in", "g_q", "w_uq", "g_kv", "w_ukv", "w_o_attn",
          "w_dw", "b_dw", "g_cn", "b_cn", "w_pw2", "w_out", "g_ffn", "w_gu", "w_down", "g_final"]


def kernel(**inputs):
    import numpy as _np
    import concourse.bacc as _bacc
    from concourse import mybir as _mybir
    from concourse.bass_utils import run_bass_kernel_spmd as _run

    nc = _bacc.Bacc("TRN2", target_bir_lowering=False, num_devices=1)
    row = _np.arange(P) % ROPE
    freq = ROPE_THETA ** (-2.0 * (row % (ROPE // 2)) / ROPE)
    rope_const = _np.stack([freq, _np.where(row < ROPE // 2, -1.0, 1.0)], axis=1).astype(_np.float32)
    arrays, w = {}, {}
    for name in _NAMES + ["rope_const"]:
        a = _np.ascontiguousarray(inputs[name]) if name in inputs else rope_const
        arrays[f"in_{name}"] = a
        w[name] = nc.dram_tensor(f"in_{name}", a.shape, _mybir.dt.from_np(a.dtype), kind="ExternalInput").ap()
    out = nc.dram_tensor("out", (1, SEQ, D), F32, kind="ExternalOutput").ap()
    layer(nc, w, out)
    r = _run(nc, [arrays], core_ids=[0])
    return r.results[0]["out"]
```

```python
import math
from contextlib import ExitStack

import concourse.bass as bass
from concourse import mybir

F32 = mybir.dt.float32
F32R = mybir.dt.float32r
I32 = mybir.dt.int32
ALU = mybir.AluOpType
ACT = mybir.ActivationFunctionType
AX_X = mybir.AxisListType.X

P = 128
D = 1024
SEQ = 2048
HEADS = 8
NOPE = 64
ROPE = 32
QK = NOPE + ROPE
VD = 64
QL = 384
KVL = 256
CONV = 512
TAPS = 31
HID = 2816
EPS = 1e-6
ROPE_THETA = 10000.0

DT = D // P
T = 512
GROUPS = SEQ // T
TT = T // P
QT, KT, CT, HT = QL // P, KVL // P, CONV // P, HID // P
IN_GLU = QL + KVL + ROPE
IN_GATE = IN_GLU + 2 * CONV

V_BADA, V_GMIX, V_GFFN, V_GQ, V_GKV, V_GCN, V_BCN, V_BDW, V_C = 0, 48, 56, 64, 67, 69, 73, 77, 81
V_ROWS = V_C + DT
SH1, SC1, GT1, SH2, SC2, GT2 = (s * DT for s in range(6))


class Kept:
    pass


def open_tensors(ctx, nc, phase):
    def sb(name, shape, dt=F32):
        return ctx.enter_context(nc.sbuf_tensor(f"{phase}_{name}", shape, dt))

    def sem(name):
        return ctx.enter_context(nc.semaphore(f"{phase}_{name}"))

    return sb, sem


def modulation(nc, w, k):
    with ExitStack() as ctx:
        sb, sem = open_tensors(ctx, nc, "modulation")
        ps = k.ps
        vrow = sb("vrow", [V_ROWS, P])
        wdw_row = sb("wdw_row", [TAPS, CONV])
        zero = sb("zero", [P, CT, TAPS - 1])
        const = sb("const", [P, 2])
        pos_i = sb("pos_i", [P, SEQ], I32)
        ang = sb("ang", [P, SEQ])
        turns = sb("turns", [P, SEQ])
        half_pi = sb("half_pi", [P, 1])
        wada = sb("wada", [P, 4, D])
        acc = sb("acc", [P, D])

        vec_loaded, dw_loaded, pos_loaded = sem("vec_loaded"), sem("dw_loaded"), sem("pos_loaded")
        wada_loaded = [sem(f"wada_loaded{i}") for i in range(4)]
        zero_set, pad_stored = sem("zero_set"), sem("pad_stored")
        ident_cleared, ident_set, ones_set = sem("ident_cleared"), sem("ident_set"), sem("ones_set")
        mask_set = sem("mask_set")
        vec_turned, vec_copied, dw_turned, dw_copied = (
            sem("vec_turned"), sem("vec_copied"), sem("dw_turned"), sem("dw_copied"))
        c_active, mod_step, mod_summed, mod_done, rope_step, rope_sine = (
            sem("c_active"), sem("mod_step"), sem("mod_summed"), sem("mod_done"), sem("rope_step"),
            sem("rope_sine"))
        STEPS = 2 * DT

        with nc.Block() as block:

            @block.sync
            def _(sp):
                for row, name in ((V_BADA, "b_ada"), (V_GMIX, "g_mix"), (V_GFFN, "g_ffn"), (V_GQ, "g_q"),
                                  (V_GKV, "g_kv"), (V_GCN, "g_cn"), (V_BCN, "b_cn"), (V_BDW, "b_dw"), (V_C, "c")):
                    src = w[name].rearrange("a (r p) -> (a r) p", p=P)
                    sp.dma_start(vrow[row:row + src.shape[0], :], src).then_inc(vec_loaded, 16)
                sp.dma_start(wdw_row[:, :], w["w_dw"][0]).then_inc(dw_loaded, 16)
                for n in range(STEPS):
                    s, f = divmod(n, DT)
                    if n >= 4:
                        sp.wait_ge(mod_step, n - 3)
                    sp.dma_start(wada[:, n % 4, :], w["w_ada"][0, f * P:(f + 1) * P, s * D:(s + 1) * D])\
                        .then_inc(wada_loaded[n % 4], 16)

            @block.gpsimd
            def _(pool):
                pool.memset(k.ident[:, :], 0.0).then_inc(ident_cleared, 1)
                pool.memset(k.ones[:, :], 1.0).then_inc(ones_set, 1)
                pool.memset(zero[:, :, :], 0.0).then_inc(zero_set, 1)
                pool.memset(half_pi[:, :], math.pi / 2).then_inc(ones_set, 1)
                pool.memset(k.eps[:, :], EPS).then_inc(ones_set, 1)
                pool.wait_ge(ident_cleared, 1)
                pool.affine_select(out=k.ident[:, :], in_=k.ident[:, :], compare_op=ALU.not_equal, fill=1.0,
                                   base=0, pattern=[[-1, P]], channel_multiplier=1).then_inc(ident_set, 1)

            @block.scalar
            def _(act):
                act.dma_start(pos_i[:, :], w["positions"].partition_broadcast(P)).then_inc(pos_loaded, 16)
                act.dma_start(const[:, :], w["rope_const"]).then_inc(pos_loaded, 16)
                act.wait_ge(zero_set, 1)
                act.dma_start(k.u_dram.rearrange("(c p) t -> p c t", p=P)[:, :, 0:TAPS - 1], zero[:, :, :])\
                    .then_inc(pad_stored, 16)
                act.wait_ge(vec_copied, 1)
                act.activation(k.c_act[:, :], k.vec[:, V_C:V_C + DT], ACT.Silu).then_inc(c_active, 1)
                act.wait_ge(ones_set, 3)
                act.wait_ge(rope_step, 10)
                act.activation(k.sin[:, :], ang[:, :], ACT.Sin).then_inc(rope_sine, 1)
                act.activation(k.cos[:, :], turns[:, :], ACT.Sin, bias=half_pi[:, :], scale=-1.0)\
                    .then_inc(rope_sine, 1)
                act.wait_ge(pad_stored, 16)

            @block.tensor
            def _(pe):
                pe.wait_ge(ident_set, 1)
                pe.wait_ge(vec_loaded, 16 * 9)
                pe.transpose(ps[:, 0, 0:V_ROWS], vrow[:, :], k.ident[0:V_ROWS, 0:V_ROWS]).then_inc(vec_turned, 1)
                pe.wait_ge(dw_loaded, 16)
                for c in range(CT):
                    last = pe.transpose(ps[:, 1, c * TAPS:(c + 1) * TAPS], wdw_row[:, c * P:(c + 1) * P],
                                        k.ident[0:TAPS, 0:TAPS])
                last.then_inc(dw_turned, 1)
                pe.wait_ge(ones_set, 3)
                for s in range(2):
                    pe.wait_ge(mod_step, DT * (s + 1))
                    for m in range(DT):
                        last = pe.matmul(ps[:, 2 + s, m:m + 1], acc[:, m * P:(m + 1) * P],
                                         k.ones[:, 0:1], start=True, stop=True)
                    last.then_inc(mod_summed, 1)

            @block.vector
            def _(dve):
                dve.wait_ge(vec_turned, 1)
                dve.tensor_copy(k.vec[:, 0:V_ROWS], ps[:, 0, 0:V_ROWS]).then_inc(vec_copied, 1)
                dve.wait_ge(dw_turned, 1)
                dve.tensor_copy(k.wdw[:, :, :], ps[:, 1, 0:CT * TAPS].rearrange("p (c j) -> p c j", c=CT))\
                    .then_inc(dw_copied, 1)
                dve.wait_ge(c_active, 1)

                def section(s):
                    for f in range(DT):
                        n = s * DT + f
                        dve.wait_ge(wada_loaded[n % 4], 16 * (n // 4 + 1))
                        if f == 0:
                            if s:
                                dve.wait_ge(mod_summed, s)
                            dve.tensor_scalar(acc[:, :], wada[:, n % 4, :], k.c_act[:, f:f + 1], None, ALU.mult)\
                                .then_inc(mod_step, 1)
                        else:
                            dve.wait_ge(mod_step, n)
                            dve.scalar_tensor_tensor(acc[:, :], wada[:, n % 4, :], k.c_act[:, f:f + 1], acc[:, :],
                                                     ALU.mult, ALU.add).then_inc(mod_step, 1)

                section(0)
                steps = 0

                def rope(ins):
                    nonlocal steps
                    steps += 1
                    ins.then_inc(rope_step, 1)
                    dve.wait_ge(rope_step, steps)

                two_pi = (6.28125, 1014 / 2 ** 19, 2 * math.pi - 6.28125 - 1014 / 2 ** 19)
                dve.wait_ge(pos_loaded, 32)
                rope(dve.tensor_copy(ang[:, :], pos_i[:, :]))
                rope(dve.tensor_scalar(ang[:, :], ang[:, :], const[:, 0:1], None, ALU.mult))
                rope(dve.tensor_scalar(turns[:, :], ang[:, :], 1 / (2 * math.pi), 1.5 * 2 ** 23, ALU.mult, ALU.add))
                rope(dve.tensor_scalar(turns[:, :], turns[:, :], 1.5 * 2 ** 23, None, ALU.subtract))
                for part in two_pi:
                    rope(dve.scalar_tensor_tensor(ang[:, :], turns[:, :], -part, ang[:, :], ALU.mult, ALU.add))
                rope(dve.tensor_scalar(ang[:, :], ang[:, :], 3.1415925, -3.1415925, ALU.min, ALU.max))
                rope(dve.scalar_tensor_tensor(turns[:, :], ang[:, :], -1.0, ang[:, :], ALU.mult, ALU.max))
                rope(dve.tensor_scalar(ang[:, :], ang[:, :], const[:, 1:2], None, ALU.mult))
                section(1)
                for s in range(2):
                    dve.wait_ge(mod_summed, s + 1)
                    dve.tensor_tensor(k.mod[:, s * DT:(s + 1) * DT], ps[:, 2 + s, 0:DT],
                                      k.vec[:, V_BADA + s * DT:V_BADA + (s + 1) * DT], ALU.add)\
                        .then_inc(mod_done, 1)
                dve.wait_ge(mod_done, 2)
                dve.scalar_tensor_tensor(k.a1[:, :], k.mod[:, SC1:SC1 + DT], 1.0, k.vec[:, V_GMIX:V_GMIX + DT],
                                         ALU.add, ALU.mult).then_inc(mod_done, 1)


def seeded(eng, *sems, by=2):
    for s in sems:
        eng.sem_inc(s, by)


def turn(n):
    return n + 1


def done(n, seed=2):
    return n + 1 + seed


def project(nc, w, k):
    JOBS = QT + KT + 1 + 2 * CT
    ITEMS = 6 + 4 + 4
    LAT = QT + KT
    GLU = LAT + 1
    with ExitStack() as ctx:
        sb, sem = open_tensors(ctx, nc, "project")
        ps = k.ps
        xtok = sb("xtok", [P, TT, D])
        ss, rstd = sb("ss", [P, TT]), sb("rstd", [P, TT])
        h = sb("h", [P, DT, 2, T], F32R)
        hb = sb("hb", [P, 2, T])
        raw = sb("raw", [P, 2, DT, P])
        wt = sb("wt", [P, 2, 2, DT, P], F32R)
        up_raw = sb("up_raw", [P, D])
        wuq = sb("wuq", [P, QT, 2, HEADS * QK], F32R)
        wukv = sb("wukv", [P, KT, 2, HEADS * (NOPE + VD)], F32R)
        lat = sb("lat", [P, LAT + 1, T])
        sq = sb("sq", [P, LAT, T])
        latn = sb("latn", [P, LAT, 2, T], F32R)
        rot = sb("rot", [P, 2, T])
        rb = sb("rb", [P, 2, T])
        kr = sb("kr", [P, 2, T], F32R)
        it = sb("it", [P, 2, T])
        stage = sb("stage", [P, 2, 2 * T], F32R)
        ub = sb("ub", [P, 2, T])
        sig = sb("sig", [P, 2, T])

        x_loaded, x_squared, x_std, x_rstd, x_scaled = (sem(n) for n in (
            "x_loaded", "x_squared", "x_std", "x_rstd", "x_scaled"))
        x_turned, h_affine, h_hi, h_lo = (sem(n) for n in ("x_turned", "h_affine", "h_hi", "h_lo"))
        raw_loaded = [sem(f"raw_loaded{i}") for i in range(2)]
        w_hi, w_lo, job_done = sem("w_hi"), sem("w_lo"), sem("job_done")
        up_loaded, up_hi, up_lo = sem("up_loaded"), sem("up_hi"), sem("up_lo")
        act_bank_free, turn_bank_free = sem("act_bank_free"), sem("turn_bank_free")
        lat_squared, lat_summed, lat_std, lat_rstd = (sem(n) for n in (
            "lat_squared", "lat_summed", "lat_std", "lat_rstd"))
        lat_copied, lat_normed, lat_hi, lat_lo, kr_step, kr_stored = (sem(n) for n in (
            "lat_copied", "lat_normed", "lat_hi", "lat_lo", "kr_step", "kr_stored"))
        gate_done, u_done = sem("gate_done"), sem("u_done")
        u_stored = [sem(f"u_stored{i}") for i in range(2)]
        item_done, item_copied, item_rot, item_hi, item_lo = (sem(n) for n in (
            "item_done", "item_copied", "item_rot", "item_hi", "item_lo"))
        item_stored = [sem(f"item_stored{i}") for i in range(2)]

        BANK_TURN, BANK_ACT, BANK_DVE, BANK_ITEM = 0, 2, 4, 6
        SUMS_AFTER = 6
        AFTER = {10: range(0, 3), 11: range(3, 6), 12: range(6, 10), 13: range(10, 14)}
        SWAP = [(i + ROPE // 2) % ROPE for i in range(ROPE)]
        ACT_USES = GLU + CT
        UP = QT + KT

        def job_column(j):
            if j < LAT:
                return j * P
            if j == LAT:
                return QL + KVL - NOPE
            c, second = divmod(j - GLU, 2)
            return IN_GLU + (0 if second else CONV) + c * P

        def by_act(j):
            return j < GLU or (j - GLU) % 2 == 0

        def act_use(j):
            return j if j < GLU else GLU + (j - GLU) // 2

        def job_bank(j):
            return BANK_ACT + act_use(j) % 2 if by_act(j) else BANK_DVE + ((j - GLU) // 2) % 2

        def groups(eng, body):
            with eng.Fori(0, GROUPS - 1) as g:
                body(g, False)
            body(GROUPS - 1, True)

        with nc.Block() as block:

            @block.sync
            def _(sp):
                uq = w["w_uq"][0].rearrange("(a p) (h e) -> a p h e", p=P, e=QK)
                ukv = w["w_ukv"][0].rearrange("(a p) (h e) -> a p h e", p=P, e=NOPE + VD)
                for a in range(UP):
                    src = uq[a] if a < QT else ukv[a - QT]
                    if a:
                        sp.wait_ge(up_lo, a)
                    split = HEADS * NOPE
                    rest = src.shape[2] - NOPE
                    sp.dma_start(up_raw[:, 0:split].rearrange("p (h e) -> p h e", h=HEADS), src[:, :, 0:NOPE])\
                        .then_inc(up_loaded, 16)
                    sp.dma_start(up_raw[:, split:split + HEADS * rest].rearrange("p (h e) -> p h e", h=HEADS),
                                 src[:, :, NOPE:]).then_inc(up_loaded, 16)
                with sp.Fori(0, GROUPS) as g:
                    for j in range(JOBS):
                        sp.wait_ge(w_lo, turn(g * JOBS + j))
                        c = job_column(j)
                        sp.dma_start(raw[:, j % 2], w["w_in"][0].rearrange("(f p) m -> p f m", p=P)[:, :, c:c + P])\
                            .then_inc(raw_loaded[j % 2], 16)

            @block.gpsimd
            def _(pool):
                seeded(pool, w_lo)
                for a in range(UP):
                    pool.wait_ge(up_hi, a + 1)
                    wide, dst = (HEADS * QK, wuq[:, a]) if a < QT else (D, wukv[:, a - QT])
                    pool.tensor_tensor(dst[:, 1], up_raw[:, 0:wide], dst[:, 0].bitcast(F32), ALU.subtract)\
                        .then_inc(up_lo, 1)
                with pool.Fori(0, GROUPS) as g:
                    for j in range(JOBS):
                        pool.wait_ge(w_hi, g * JOBS + j + 1)
                        pool.tensor_tensor(wt[:, j % 2, 1], raw[:, j % 2], wt[:, j % 2, 0].bitcast(F32), ALU.subtract)\
                            .then_inc(w_lo, 1)

            @block.scalar
            def _(act):
                seeded(act, act_bank_free, turn_bank_free, item_copied)

                def load_x(g):
                    act.dma_start(xtok[:, :, :],
                                  w["x"][0].rearrange("(g t p) f -> p g t f", t=TT, p=P)[:, bass.ds(g, 1)]
                                  .rearrange("p g t f -> p (g t) f")).then_inc(x_loaded, 16)

                def x_stats(g):
                    act.wait_ge(x_loaded, (g + 1) * 16)
                    for t in range(TT):
                        act.wait_ge(x_squared, g * TT + t)
                        act.activation(sq[:, 0:2, :].rearrange("p a b -> p (a b)"), xtok[:, t, :], ACT.Square,
                                       accum_out=ss[:, t:t + 1]).then_inc(x_squared, 1)
                    act.wait_ge(x_squared, (g + 1) * TT)
                    act.activation(rstd[:, :], ss[:, :], ACT.Sqrt, bias=k.eps[:, :], scale=1.0 / D)\
                        .then_inc(x_std, 1)

                def hi(n, use, j):
                    act.wait_ge(raw_loaded[j % 2], use * 16)
                    act.wait_ge(job_done, turn(n))
                    act.activation(wt[:, j % 2, 0], raw[:, j % 2], ACT.Copy).then_inc(w_hi, 1)

                def store_item(g, n):
                    act.wait_ge(item_lo, done(g * ITEMS + n))
                    cols = bass.ds(g * T, T)
                    if n < 10:
                        dst = (k.qn_dram[n * P:(n + 1) * P, :, cols] if n < 4 else
                               k.qr_dram[(n - 4) * P:(n - 3) * P, :, cols] if n < 6 else
                               k.kn_dram[(n - 6) * P:(n - 5) * P, :, cols])
                        src = stage[:, n % 2, :].bitcast(F32).rearrange("p (a t) -> p a t", a=2)
                    else:
                        dst = k.v_dram[bass.ds(g * T + (n - 10) * P, P)]
                        src = stage[:, n % 2, :].bitcast(F32)
                    act.dma_start(dst, src).then_inc(item_stored[n % 2], 16)

                def store_u(g, c):
                    act.wait_ge(u_done, done(g * CT + c))
                    act.dma_start(k.u_dram[c * P:(c + 1) * P, bass.ds(g * T + TAPS - 1, T)], ub[:, c % 2])\
                        .then_inc(u_stored[c % 2], 16)

                def body(g, last):
                    for f in range(DT):
                        act.wait_ge(x_turned, g * DT + f + 1)
                        act.wait_ge(h_lo, turn(g * DT + f))
                        act.activation(hb[:, f % 2, :], ps[:, BANK_TURN + f % 2, :], ACT.Identity,
                                       bias=k.mod[:, SH1 + f:SH1 + f + 1], scale=k.a1[:, f:f + 1])\
                            .then_inc(turn_bank_free, 1)
                    if not last:
                        load_x(g + 1)
                    pending = []
                    for j in range(JOBS):
                        if j + 2 < JOBS:
                            hi(g * JOBS + j + 2, g * (JOBS // 2) + j // 2 + 2, j)
                        elif not last:
                            hi(g * JOBS + j + 2, g * (JOBS // 2) + j // 2 + 2, j)
                        act.wait_ge(job_done, done(g * JOBS + j))
                        if j < GLU:
                            act.wait_ge(kr_step, 1 + g * 6)
                            if j < LAT:
                                act.wait_ge(lat_lo, 1 + g * LAT)
                            act.activation(lat[:, j, :], ps[:, job_bank(j), :], ACT.Copy).then_inc(act_bank_free, 1)
                            if j < LAT:
                                act.wait_ge(act_bank_free, done(g * (ACT_USES) + j))
                                act.activation(sq[:, j, :], lat[:, j, :], ACT.Square).then_inc(lat_squared, 1)
                        elif by_act(j):
                            c = (j - GLU) // 2
                            act.wait_ge(u_done, turn(g * CT + c))
                            act.activation(sig[:, c % 2, :], ps[:, job_bank(j), :], ACT.Sigmoid)\
                                .then_inc(act_bank_free, 1)
                        else:
                            store_u(g, (j - GLU) // 2)
                        if j == SUMS_AFTER:
                            for i, width in enumerate((QL, KVL)):
                                act.wait_ge(lat_summed, g * 2 + i + 1)
                                act.wait_ge(lat_lo, 1 + g * LAT)
                                act.activation(rb[:, i, :], ps[:, BANK_TURN + i, :], ACT.Sqrt, bias=k.eps[:, :],
                                               scale=1.0 / width).then_inc(turn_bank_free, 1)
                            act.wait_ge(kr_step, 1 + g * 6 + 6)
                            act.dma_start(k.kr_dram[:, :, bass.ds(g * T, T)], kr[NOPE:QK].bitcast(F32)).then_inc(kr_stored, 16)
                            if not last:
                                x_stats(g + 1)
                        for n in AFTER.get(j, ()):
                            num = g * ITEMS + n
                            act.wait_ge(item_done, num + 1)
                            act.wait_ge(item_lo, turn(num))
                            act.activation(it[:, n % 2, :], ps[:, BANK_ITEM + n % 2, :], ACT.Copy)\
                                .then_inc(item_copied, 1)
                            pending.append(n)
                            if len(pending) > 1:
                                store_item(g, pending.pop(0))
                    store_item(g, pending.pop(0))

                for a in range(UP):
                    act.wait_ge(up_loaded, (a + 1) * 32)
                    wide, dst = (HEADS * QK, wuq[:, a]) if a < QT else (D, wukv[:, a - QT])
                    act.activation(dst[:, 0], up_raw[:, 0:wide], ACT.Copy).then_inc(up_hi, 1)
                    if a == 0:
                        load_x(0)
                x_stats(0)
                for j in range(2):
                    hi(j, 1, j)
                groups(act, body)
                for i in range(2):
                    act.wait_ge(item_stored[i], 16 * (1 + GROUPS * ITEMS // 2))
                    act.wait_ge(u_stored[i], 16 * (1 + GROUPS * CT // 2))
                act.wait_ge(kr_stored, 16 * (1 + GROUPS))

            @block.tensor
            def _(pe):
                seeded(pe, job_done)

                def body(g, last):
                    pe.wait_ge(x_scaled, (g + 1) * TT)
                    for f in range(DT):
                        pe.wait_ge(turn_bank_free, turn(g * (DT + 2) + f))
                        for t in range(TT):
                            ins = pe.transpose(ps[:, BANK_TURN + f % 2, t * P:(t + 1) * P],
                                               xtok[:, t, f * P:(f + 1) * P], k.ident[:, :])
                        ins.then_inc(x_turned, 1)
                    for j in range(JOBS):
                        pe.wait_ge(w_lo, done(g * JOBS + j))
                        if by_act(j):
                            pe.wait_ge(act_bank_free, turn(g * ACT_USES + act_use(j)))
                        else:
                            pe.wait_ge(u_done, turn(g * CT + (j - GLU) // 2))
                        for f in range(DT):
                            if j == 0:
                                pe.wait_ge(h_lo, done(g * DT + f))
                            for s, m in ((0, 0), (0, 1), (1, 0)):
                                ins = pe.matmul(ps[:, job_bank(j), :], wt[:, j % 2, s, f, :], h[:, f, m, :],
                                                start=(f == 0 and s == m == 0), stop=(f == DT - 1 and s == 1))
                        ins.then_inc(job_done, 1)
                        if j == SUMS_AFTER:
                            for i, tiles in enumerate((range(QT), range(QT, LAT))):
                                pe.wait_ge(lat_squared, g * LAT + tiles[-1] + 1)
                                pe.wait_ge(turn_bank_free, turn(g * (DT + 2) + DT + i))
                                for f in tiles:
                                    ins = pe.matmul(ps[:, BANK_TURN + i, :], k.ones[:, :], sq[:, f, :],
                                                    start=(f == tiles[0]), stop=(f == tiles[-1]))
                                ins.then_inc(lat_summed, 1)
                        for n in AFTER.get(j, ()):
                            item(g, n)

                def item(g, n):
                    pe.wait_ge(item_copied, turn(g * ITEMS + n))
                    pe.wait_ge(lat_lo, 1 + g * LAT + (QT if n < 6 else LAT))
                    out = ps[:, BANK_ITEM + n % 2, :]
                    tiles = range(QT) if n < 6 else range(KT)
                    for f in tiles:
                        for s, m in ((0, 0), (0, 1), (1, 0)):
                            if n < 6:
                                lhs, rhs = wuq[:, f, s, n * P:(n + 1) * P], latn[:, f, m, :]
                            elif n < 10:
                                lhs, rhs = wukv[:, f, s, (n - 6) * P:(n - 5) * P], latn[:, QT + f, m, :]
                            else:
                                lhs = latn[:, QT + f, s, (n - 10) * P:(n - 9) * P]
                                rhs = wukv[:, f, m, HEADS * NOPE:]
                            ins = pe.matmul(out, lhs, rhs, start=(f == 0 and s == m == 0),
                                            stop=(f == tiles[-1] and s == 1))
                    ins.then_inc(item_done, 1)

                pe.wait_ge(up_lo, UP)
                groups(pe, body)

            @block.vector
            def _(dve):
                seeded(dve, h_lo, u_done, item_lo)
                seeded(dve, kr_step, lat_lo, by=1)
                seeded(dve, *u_stored, *item_stored, kr_stored, by=16)

                def scale_x(g):
                    dve.wait_ge(x_std, g + 1)
                    dve.reciprocal(rstd[:, :], rstd[:, :]).then_inc(x_rstd, 1)
                    dve.wait_ge(x_rstd, g + 1)
                    for t in range(TT):
                        dve.tensor_scalar(xtok[:, t, :], xtok[:, t, :], rstd[:, t:t + 1], None, ALU.mult)\
                            .then_inc(x_scaled, 1)

                def latents(g):
                    for i in range(2):
                        dve.wait_ge(turn_bank_free, done(g * (DT + 2) + DT + i))
                        dve.reciprocal(rb[:, i, :], rb[:, i, :]).then_inc(lat_rstd, 1)
                    for f in range(LAT):
                        dve.wait_ge(lat_rstd, g * 2 + (1 if f < QT else 2))
                        dve.scalar_tensor_tensor(lat[:, f, :], lat[:, f, :], k.vec[:, V_GQ + f:V_GQ + f + 1],
                                                 rb[:, 0 if f < QT else 1, :], ALU.mult, ALU.mult)\
                            .then_inc(lat_normed, 1)
                        dve.wait_ge(lat_normed, g * LAT + f + 1)
                        dve.tensor_copy(latn[:, f, 0, :], lat[:, f, :]).then_inc(lat_hi, 1)
                        dve.wait_ge(lat_hi, g * LAT + f + 1)
                        dve.tensor_tensor(latn[:, f, 1, :], lat[:, f, :], latn[:, f, 0, :].bitcast(F32), ALU.subtract)\
                            .then_inc(lat_lo, 1)

                def rotate(t, tmp, part, sem_, base):
                    cos, sin = k.cos[part, g_cols[0]], k.sin[part, g_cols[0]]
                    scaled, swapped = tmp
                    dve.tensor_tensor(scaled, t, cos, ALU.mult).then_inc(sem_, 1)
                    dve.stream_shuffle(swapped, t, SWAP).then_inc(sem_, 1)
                    dve.wait_ge(sem_, base + 2)
                    dve.tensor_tensor(swapped, swapped, sin, ALU.mult).then_inc(sem_, 1)
                    dve.wait_ge(sem_, base + 3)
                    dve.tensor_tensor(t, scaled, swapped, ALU.add).then_inc(sem_, 1)
                    dve.wait_ge(sem_, base + 4)

                g_cols = [None]

                def body(g, last):
                    g_cols[0] = bass.ds(g * T, T)
                    for f in range(DT):
                        dve.wait_ge(turn_bank_free, done(g * (DT + 2) + f))
                        dve.tensor_copy(h[:, f, 0, :], hb[:, f % 2, :]).then_inc(h_hi, 1)
                        dve.wait_ge(h_hi, g * DT + f + 1)
                        dve.tensor_tensor(h[:, f, 1, :], hb[:, f % 2, :], h[:, f, 0, :].bitcast(F32), ALU.subtract)\
                            .then_inc(h_lo, 1)
                    for j in range(JOBS):
                        if j == LAT:
                            dve.wait_ge(act_bank_free, done(g * ACT_USES + LAT))
                            dve.wait_ge(kr_stored, 16 * (1 + g))
                            t = lat[NOPE:QK, LAT, :]
                            rotate(t, (rot[NOPE:QK, 0, :], rot[NOPE:QK, 1, :]), slice(NOPE, QK), kr_step, 1 + g * 6)
                            dve.tensor_copy(kr[NOPE:QK, 0, :], t).then_inc(kr_step, 1)
                            dve.wait_ge(kr_step, 1 + g * 6 + 5)
                            dve.tensor_tensor(kr[NOPE:QK, 1, :], t, kr[NOPE:QK, 0, :].bitcast(F32), ALU.subtract)\
                                .then_inc(kr_step, 1)
                        if not by_act(j):
                            c = (j - GLU) // 2
                            dve.wait_ge(act_bank_free, done(g * ACT_USES + act_use(j - 1)))
                            dve.wait_ge(job_done, done(g * JOBS + j))
                            dve.wait_ge(u_stored[c % 2], 16 * (g * (CT // 2) + c // 2 + 1))
                            dve.tensor_tensor(ub[:, c % 2, :], ps[:, job_bank(j), :], sig[:, c % 2, :], ALU.mult)\
                                .then_inc(u_done, 1)
                        if j == SUMS_AFTER + 1:
                            latents(g)
                            if not last:
                                scale_x(g + 1)
                        for n in AFTER.get(j, ()):
                            num = g * ITEMS + n
                            dve.wait_ge(item_copied, done(num))
                            t = it[:, n % 2, :]
                            if n in (4, 5):
                                rotate(t, (rot[:, 0, :], rot[:, 1, :]), slice(0, P), item_rot, g * 8 + (n - 4) * 4)
                            dve.wait_ge(item_stored[n % 2], 16 * (g * (ITEMS // 2) + n // 2 + 1))
                            if n < 10:
                                st = stage[:, n % 2, :].rearrange("p (a t) -> p a t", a=2)
                                parts = st[:, 0, :], st[:, 1, :]
                            else:
                                st = stage[:, n % 2, :].rearrange("p (h a e) -> p h a e", h=HEADS, a=2)
                                parts = st[:, :, 0, :], st[:, :, 1, :]
                                t = t.rearrange("p (h e) -> p h e", h=HEADS)
                            dve.tensor_copy(parts[0], t).then_inc(item_hi, 1)
                            dve.wait_ge(item_hi, num + 1)
                            dve.tensor_tensor(parts[1], t, parts[0].bitcast(F32), ALU.subtract).then_inc(item_lo, 1)

                scale_x(0)
                groups(dve, body)


def attend(nc, w, k):
    NG = SEQ // T
    CHUNKS = TT * NG * (NG + 1) // 2
    UNITS = CHUNKS
    BLOCKS = SEQ // P
    STEPS = 4
    upto = [TT * n * (n + 1) // 2 for n in range(NG + 2)]
    SCALE = float(QK) ** -0.5
    with ExitStack() as ctx:
        sb, sem = open_tensors(ctx, nc, "attend")
        ps = k.ps
        key = sb("key", [P, 2, 2, SEQ], F32R)
        qry = sb("qry", [P, 2, 2, SEQ], F32R)
        val = sb("val", [P, 2, BLOCKS, 2 * VD], F32R)
        prob = sb("prob", [P, STEPS, T])
        pt = sb("pt", [P, STEPS, 2, T], F32R)
        total = sb("total", [P, 2, T])
        zero = sb("zero", [P, T])
        rows = sb("rows", [P, 2, SEQ])
        eye = sb("eye", [P, P], F32R)
        mask, mask_t = sb("mask", [P, P], F32R), sb("mask_t", [P, P], F32R)
        mask_f = sb("mask_f", [P, 2, P])
        cmax, bmax = sb("cmax", [P, TT, NG]), sb("bmax", [P, TT])
        nmax = sb("nmax", [P, TT, P])
        rsum = sb("rsum", [P, TT])
        diag = sb("diag", [P, TT, P])
        ot = sb("ot", [VD, T])
        of = sb("of", [VD, T])
        ostage = sb("ostage", [VD, 2, 2, T], F32R)
        wada = sb("wada", [P, 2, D])
        part, acc = sb("part", [P, D]), sb("acc", [P, D])

        wait_passed = sem("wait_passed")
        rope_loaded, const_cleared, const_made, consts_set = (
            sem(n) for n in ("rope_loaded", "const_cleared", "const_made", "consts_set"))
        head_loaded = [sem(f"head_loaded{i}") for i in range(2)]
        chunk_done, chunk_max, block_max, max_negated = (
            sem(n) for n in ("chunk_done", "chunk_max", "block_max", "max_negated"))
        row_turned, row_hi, row_lo = sem("row_turned"), sem("row_hi"), sem("row_lo")
        score_done, exp_done, prob_hi, prob_lo, prob_summed, unit_done = (sem(n) for n in (
            "score_done", "exp_done", "prob_hi", "prob_lo", "prob_summed", "unit_done"))
        sums_done, recip_done, diag_done, spread_done = (
            sem(n) for n in ("sums_done", "recip_done", "diag_done", "spread_done"))
        out_moved, out_summed, out_scaled, out_hi, out_lo = (
            sem(n) for n in ("out_moved", "out_summed", "out_scaled", "out_hi", "out_lo"))
        out_stored = [sem(f"out_stored{i}") for i in range(2)]
        wada2_loaded = [sem(f"wada2_loaded{i}") for i in range(2)]
        prod_done, acc_done, acc_summed, mod_added = (sem(n) for n in (
            "prod_done", "acc_done", "acc_summed", "mod_added"))

        BANK_CHUNK, BANK_SCORE, BANK_OUT, BANK_ROW, BANK_SUM = 0, 2, 4, 6, 7

        def maxima(n):
            return [("chunk", n, b, c) for b in range(TT) for c in range((n % NG) + 1)]

        def events(s, first, last):
            at = {u: n for n in range(NG) for u in range(upto[n], upto[n + 1])}
            at[-2] = at[-1] = -1
            if first:
                yield from maxima(0)
                yield ("combine", 0)
                yield ("row", 0)
            chunks, slots = {}, {}
            for n in range(NG):
                if last and n == NG - 1:
                    continue
                num = upto[n + 1] - upto[n]
                todo = maxima(n + 1)
                use = max(3, num - 3)
                for i, chunk in enumerate(todo):
                    slots.setdefault(upto[n] + i * use // len(todo), []).append(chunk)
                slots.setdefault(upto[n] + use - 1, []).append(("combine", n + 1))
                slots.setdefault(upto[n] + use, []).insert(0, ("row", n + 1))
            for u in range(UNITS + (2 if last else 0)):
                if u <= UNITS and not (first and u == 0):
                    yield ("split", at[u - 1], u - 1)
                if u < UNITS:
                    yield ("score", at[u], u)
                some = slots.get(u, [])
                yield from some[:1]
                if not (first and u < 2):
                    yield ("product", at[u - 2], u - 2)
                yield from some[1:]
                if s == 0 and u % 4 == 0 and u // 4 < DT:
                    yield ("mod_load", u // 4)
                if first and u < 2:
                    continue
                n = at[u - 2]
                if u - 1 == upto[n + 1]:
                    yield ("sums", n)
                if u - 2 == upto[n] and not (first and n == 0):
                    yield ("out", n - 1)
                if s == 0 and u % 4 == 3 and 0 < u // 4 <= DT:
                    yield ("mod_step", u // 4 - 1)
                if s == 1 and u == 8:
                    yield ("mod",)
            if last:
                yield ("out", NG - 1)

        def heads(eng, body):
            body(0, 0, 0, list(events(0, True, False)), False)
            body(0, 1, 1, list(events(1, False, False)), False)
            with eng.Fori(1, HEADS // 2 - 1) as pair:
                for s in range(2):
                    body(pair, s, pair * 2 + s, list(events(s, False, False)), False)
            last = HEADS // 2 - 1
            body(last, 0, HEADS - 2, list(events(0, False, False)), False)
            body(last, 1, HEADS - 1, list(events(1, False, True)), True)

        def width(n, b, c):
            return T if c < n % NG else (b + 1) * P

        def first_query(n, kb):
            return max(0, kb - TT * n) * P

        def place(s, n):
            return (s if 0 <= n < NG else 1 - s), n % NG

        def unit(n, u):
            kb = u - upto[n] if n >= 0 else u + TT * NG
            return kb, first_query(n % NG, kb), kb == TT * (n % NG + 1) - 1

        with nc.Block() as block:

            @block.sync
            def _(sp):
                for s in range(2):
                    sp.dma_start(key[NOPE:QK, s].bitcast(F32), k.kr_dram).then_inc(rope_loaded, 16)
                with sp.Fori(0, HEADS // 2) as pair:
                    for s in range(2):
                        head = pair * 2 + s
                        sp.wait_ge(out_summed, head * NG + NG)
                        cols = bass.ds(head * NOPE, NOPE)
                        sp.dma_start(key[0:NOPE, s].bitcast(F32), k.kn_dram[cols]).then_inc(head_loaded[s], 16)
                        sp.dma_start(qry[0:NOPE, s].bitcast(F32), k.qn_dram[cols]).then_inc(head_loaded[s], 16)
                        sp.dma_start(qry[NOPE:QK, s].bitcast(F32), k.qr_dram[bass.ds(head * ROPE, ROPE)])\
                            .then_inc(head_loaded[s], 16)
                        sp.dma_start(val[:, s].bitcast(F32), k.v_dram.rearrange("(b p) c -> p b c", p=P)
                                     [:, :, bass.ds(head * 2 * VD, 2 * VD)])\
                            .then_inc(head_loaded[s], 16)

            @block.gpsimd
            def _(pool):
                seeded(pool, acc_done)
                seeded(pool, prob_summed, by=STEPS)
                pool.memset(mask_f[:, :, :], 0.0).then_inc(const_cleared, 1)
                pool.memset(zero[:, :], 0.0).then_inc(const_cleared, 1)
                pool.memset(nmax[:, :, :], 0.0).then_inc(const_cleared, 1)
                pool.memset(rows[:, 0, :], 1.0).then_inc(const_cleared, 1)
                pool.memset(rows[:, 1, :], 0.0).then_inc(const_cleared, 1)
                pool.wait_ge(const_cleared, 5)
                for i, sign in ((0, -1), (1, 1)):
                    pool.affine_select(out=mask_f[:, i, :], in_=mask_f[:, i, :], compare_op=ALU.is_ge, fill=-1e30,
                                       base=0, pattern=[[sign, P]], channel_multiplier=-sign).then_inc(const_made, 1)

                def body(pair, s, head, order, last):
                    for kind, *what in order:
                        if kind == "split":
                            n, u = what
                            kb, q0, _ = unit(n, u)
                            num = head * UNITS + u
                            pool.wait_ge(exp_done, done(num))
                            if kb == 0:
                                pool.wait_ge(sums_done, head * NG + n + 1)
                            else:
                                pool.wait_ge(prob_summed, done(num - 1, STEPS))
                            dst = total[:, n % 2, q0:]
                            pool.tensor_tensor(dst, prob[:, u % STEPS, q0:], zero[:, q0:] if kb == 0 else dst, ALU.add)\
                                .then_inc(prob_summed, 1)
                        elif kind == "mod_step":
                            f, = what
                            num = pair * DT + f
                            pool.wait_ge(prod_done, done(num))
                            if f:
                                pool.wait_ge(acc_done, done(num - 1))
                                pool.tensor_tensor(acc[:, :], acc[:, :], part[:, :], ALU.add).then_inc(acc_done, 1)
                            else:
                                pool.sem_inc(acc_done, 1)

                heads(pool, body)

            @block.scalar
            def _(act):
                seeded(act, exp_done, prod_done)
                act.activation(eye[:, :], k.ident[:, :], ACT.Copy).then_inc(consts_set, 1)
                act.wait_ge(const_made, 2)
                act.activation(mask[:, :], mask_f[:, 0, :], ACT.Copy).then_inc(consts_set, 1)
                act.activation(mask_t[:, :], mask_f[:, 1, :], ACT.Copy).then_inc(consts_set, 1)
                for s in range(2):
                    for i in range(2):
                        act.activation(key[QK:QK + 1, s, i, :], rows[QK:QK + 1, i, :], ACT.Copy).then_inc(consts_set, 1)

                def store(head, n):
                    row = head * VD if n >= 0 else (head - 1) * VD
                    n0 = n % NG
                    act.wait_ge(out_lo, done(head * NG + n, 1))
                    act.dma_start(k.attn_dram[bass.ds(row, VD), :, n0 * T:(n0 + 1) * T],
                                  ostage[:, n % 2].bitcast(F32)).then_inc(out_stored[n % 2], 16)

                def body(pair, s, head, order, last):
                    unstored = None
                    for kind, *what in order:
                        if kind == "score":
                            n, u = what
                            num = head * UNITS + u
                            kb, q0, _ = unit(n, u)
                            act.wait_ge(score_done, num + 1)
                            act.wait_ge(prob_summed, turn(num))
                            act.wait_ge(prob_lo, turn(num))
                            act.activation(prob[:, u % STEPS, q0:], ps[:, BANK_SCORE + u % 2, q0:], ACT.Exp,
                                           scale=SCALE).then_inc(exp_done, 1)
                        elif kind == "split":
                            n, u = what
                            num = head * UNITS + u
                            kb, q0, _ = unit(n, u)
                            act.wait_ge(exp_done, done(num))
                            act.wait_ge(unit_done, turn(num))
                            act.activation(pt[:, u % STEPS, 0, q0:], prob[:, u % STEPS, q0:], ACT.Copy)\
                                .then_inc(prob_hi, 1)
                        elif kind == "row":
                            n, = what
                            buf, n0 = place(s, n)
                            act.wait_ge(row_turned, done(head * NG + n, 1))
                            act.activation(qry[QK:QK + 1, buf, 0, n0 * T:(n0 + 1) * T], ps[QK:QK + 1, BANK_ROW, :],
                                           ACT.Copy).then_inc(row_hi, 1)
                            if unstored is not None:
                                store(head, unstored)
                                unstored = None
                        elif kind == "sums":
                            n, = what
                            buf, n0 = place(s, n)
                            act.wait_ge(unit_done, done(head * UNITS + (upto[n + 1] if n >= 0 else 0) - 1, STEPS))
                            act.wait_ge(out_summed, head * NG + n + 8)
                            act.activation(ot[:, :], ps[VD:P, BANK_OUT + n % 2, :], ACT.Copy).then_inc(out_moved, 1)
                        elif kind == "out":
                            if unstored is not None:
                                store(head, unstored)
                            unstored, = what
                        elif kind == "mod_load":
                            f, = what
                            act.wait_ge(prod_done, done(pair * DT + f - 2))
                            act.dma_start(wada[:, f % 2],
                                          w["w_ada"][0, f * P:(f + 1) * P, bass.ds((pair + 2) * D, D)])\
                                .then_inc(wada2_loaded[f % 2], 16)
                        elif kind == "mod_step":
                            f, = what
                            num = pair * DT + f
                            act.wait_ge(wada2_loaded[f % 2], 16 * (pair * (DT // 2) + f // 2 + 1))
                            act.wait_ge(acc_done, done(num - 1))
                            act.wait_ge(acc_summed, 1 + pair)
                            act.activation((part if f else acc)[:, :], wada[:, f % 2], ACT.Identity,
                                           scale=k.c_act[:, f:f + 1]).then_inc(prod_done, 1)
                    if unstored is not None:
                        store(head, unstored)

                heads(act, body)
                for i in range(2):
                    act.wait_ge(out_stored[i], 16 * (1 + HEADS * NG // 2))

            @block.tensor
            def _(pe):
                seeded(pe, unit_done, by=STEPS)
                seeded(pe, sums_done)
                seeded(pe, acc_summed, row_turned, spread_done, by=1)
                pe.wait_ge(consts_set, 7)
                pe.wait_ge(rope_loaded, 32)

                def body(pair, s, head, order, last):
                    for kind, *what in order:
                        if kind == "chunk":
                            n, b, c = what
                            buf, n0 = place(s, n)
                            if n == NG and b == 0:
                                pe.wait_ge(head_loaded[buf], 64 * (pair + 1 + s))
                            i = n0 * TT + b
                            wd = width(n, b, c)
                            at = upto[n] + b * (n0 + 1) + c
                            bank = BANK_CHUNK + at % 2
                            pe.wait_ge(chunk_max, turn(head * CHUNKS + at))
                            for q, m in ((0, 0), (0, 1), (1, 0)):
                                ins = pe.matmul(ps[:, bank, 0:wd], qry[0:QK, buf, q, i * P:(i + 1) * P],
                                                key[0:QK, buf, m, c * T:c * T + wd], start=(q == m == 0),
                                                stop=(q == 1 and c < n0))
                            if c == n0:
                                ins = pe.matmul(ps[:, bank, wd - P:wd], eye[:, :], mask[:, :], start=False, stop=True)
                            ins.then_inc(chunk_done, 1)
                        elif kind == "row":
                            n, = what
                            pe.wait_ge(max_negated, head * NG + n + 1)
                            pe.wait_ge(out_scaled, head * NG + n + 1)
                            for b in range(TT):
                                ins = pe.transpose(ps[:, BANK_ROW, b * P:(b + 1) * P], nmax[:, b, :], k.ident[:, :])
                            ins.then_inc(row_turned, 1)
                        elif kind == "score":
                            n, u = what
                            kb, q0, _ = unit(n, u)
                            diagonal = kb >= TT * n
                            bank = BANK_SCORE + u % 2
                            if kb == 0:
                                pe.wait_ge(row_lo, head * NG + n + 1)
                            pe.wait_ge(exp_done, turn(head * UNITS + u))
                            for q, m in ((0, 0), (0, 1), (1, 0)):
                                ins = pe.matmul(ps[:, bank, q0:], key[0:QK + 1, s, q, kb * P:(kb + 1) * P],
                                                qry[0:QK + 1, s, m, n * T + q0:(n + 1) * T], start=(q == m == 0),
                                                stop=(q == 1 and not diagonal))
                            if diagonal:
                                ins = pe.matmul(ps[:, bank, q0:q0 + P], eye[:, :], mask_t[:, :], start=False, stop=True)
                            ins.then_inc(score_done, 1)
                        elif kind == "product":
                            n, u = what
                            buf, n0 = place(s, n)
                            kb, q0, final = unit(n, u)
                            if kb == 0:
                                pe.wait_ge(out_summed, head * NG + n + 7)
                            pe.wait_ge(prob_lo, done(head * UNITS + u, STEPS))
                            for m in range(2):
                                ins = pe.matmul(ps[:, BANK_OUT + n % 2, q0:], val[:, buf, kb, :],
                                                pt[:, u % STEPS, m, q0:], start=(kb == 0 and m == 0),
                                                stop=(final and m == 1))
                            ins.then_inc(unit_done, 1)
                        elif kind == "sums":
                            n, = what
                            end = upto[n + 1] if n >= 0 else 0
                            pe.wait_ge(prob_summed, done(head * UNITS + end - 1, STEPS))
                            pe.wait_ge(recip_done, done(head * NG + n - 1, 1))
                            pe.wait_ge(mod_added, pair + (1 if s == 0 or n < 0 or n == 0 else 2))
                            for b in range(TT):
                                ins = pe.matmul(ps[:, BANK_SUM, b:b + 1], total[:, n % 2, b * P:(b + 1) * P],
                                                k.ones[:, 0:1], start=True, stop=True)
                            ins.then_inc(sums_done, 1)
                        elif kind == "out":
                            n, = what
                            pe.wait_ge(diag_done, TT * (head * NG + n + 1))
                            pe.wait_ge(row_lo, head * NG + n + (1 if last and n == NG - 1 else 2))
                            pe.matmul(ps[0:VD, BANK_ROW, :], k.ones[:, 0:VD], diag[:, :, :].rearrange("p b q -> p (b q)"),
                                      start=True, stop=True).then_inc(spread_done, 1)
                        elif kind == "mod":
                            pe.wait_ge(acc_done, done(pair * DT + DT - 1))
                            pe.wait_ge(recip_done, done(head * NG, 1))
                            for m in range(DT):
                                ins = pe.matmul(ps[:, BANK_SUM, m:m + 1], acc[:, m * P:(m + 1) * P], k.ones[:, 0:1],
                                                start=True, stop=True)
                            ins.then_inc(acc_summed, 1)

                pe.wait_ge(head_loaded[0], 64)
                heads(pe, body)

            @block.vector
            def _(dve):
                seeded(dve, out_summed, by=8)
                seeded(dve, chunk_max, out_scaled)
                seeded(dve, prob_lo, by=STEPS)
                seeded(dve, mod_added, recip_done, out_lo, by=1)
                seeded(dve, *out_stored, by=16)
                dve.wait_ge(const_cleared, 5)

                def body(pair, s, head, order, last):
                    for kind, *what in order:
                        if kind == "chunk":
                            n, b, c = what
                            at = upto[n] + b * (n % NG + 1) + c
                            wd = width(n, b, c)
                            dve.wait_ge(chunk_done, head * CHUNKS + at + 1)
                            dve.reduce_max(cmax[:, b, c:c + 1], ps[:, BANK_CHUNK + at % 2, 0:wd], AX_X)\
                                .then_inc(chunk_max, 1)
                        elif kind == "combine":
                            n, = what
                            dve.wait_ge(chunk_max, done(head * CHUNKS + upto[n] + TT * (n % NG + 1) - 1))
                            dve.wait_ge(row_turned, head * NG + n + 1)
                            dve.reduce_max(bmax[:, :], cmax[:, :, 0:n % NG + 1], AX_X).then_inc(block_max, 1)
                            dve.wait_ge(block_max, head * NG + n + 1)
                            dve.tensor_scalar(nmax[:, :, QK], bmax[:, :], -1.0, None, ALU.mult).then_inc(max_negated, 1)
                        elif kind == "row":
                            n, = what
                            buf, n0 = place(s, n)
                            cols = slice(n0 * T, (n0 + 1) * T)
                            dve.wait_ge(row_hi, head * NG + n + 1)
                            dve.tensor_tensor(qry[QK:QK + 1, buf, 1, cols], ps[QK:QK + 1, BANK_ROW, :],
                                              qry[QK:QK + 1, buf, 0, cols].bitcast(F32), ALU.subtract)\
                                .then_inc(row_lo, 1)
                        elif kind == "split":
                            n, u = what
                            num = head * UNITS + u
                            _, q0, _ = unit(n, u)
                            dve.wait_ge(prob_hi, num + 1)
                            dve.tensor_tensor(pt[:, u % STEPS, 1, q0:], prob[:, u % STEPS, q0:],
                                              pt[:, u % STEPS, 0, q0:].bitcast(F32), ALU.subtract).then_inc(prob_lo, 1)
                        elif kind == "sums":
                            n, = what
                            num = head * NG + n
                            dve.wait_ge(sums_done, done(num))
                            dve.wait_ge(spread_done, num + 1)
                            dve.reciprocal(rsum[:, :], ps[:, BANK_SUM, 0:TT]).then_inc(recip_done, 1)
                            dve.wait_ge(recip_done, done(num, 1))
                            for b in range(TT):
                                dve.tensor_scalar(diag[:, b, :], k.ident[:, :], rsum[:, b:b + 1], None, ALU.mult)\
                                    .then_inc(diag_done, 1)
                        elif kind == "out":
                            n, = what
                            num = head * NG + n
                            dve.wait_ge(out_moved, num + 1)
                            dve.wait_ge(out_lo, num + 1)
                            dve.tensor_tensor(of[:, :], ps[0:VD, BANK_OUT + n % 2, :], ot[:, :], ALU.add)\
                                .then_inc(out_summed, 1)
                            dve.wait_ge(out_summed, num + 1 + 8)
                            dve.wait_ge(spread_done, done(num, 1))
                            dve.tensor_tensor(of[:, :], of[:, :], ps[0:VD, BANK_ROW, :], ALU.mult).then_inc(out_scaled, 1)
                            dve.wait_ge(out_scaled, done(num))
                            dve.wait_ge(out_stored[n % 2], 16 * (head * (NG // 2) + n // 2 + 1))
                            dve.tensor_copy(ostage[:, n % 2, 0, :], of[:, :]).then_inc(out_hi, 1)
                            dve.wait_ge(out_hi, num + 1)
                            dve.tensor_tensor(ostage[:, n % 2, 1, :], of[:, :], ostage[:, n % 2, 0, :].bitcast(F32),
                                              ALU.subtract).then_inc(out_lo, 1)
                        elif kind == "mod":
                            dve.wait_ge(acc_summed, 1 + pair + 1)
                            cols = bass.ds((pair + 2) * DT, DT)
                            dve.tensor_tensor(k.mod[:, cols], ps[:, BANK_SUM, 0:DT], k.vec[:, cols], ALU.add)\
                                .then_inc(mod_added, 1)

                heads(dve, body)


def mix(nc, w, k, out):
    PARTS = ((0, 12), (12, 10))
    assert sum(n for _, n in PARTS) == HT
    GATES, MERGE, OUT = 2 * DT, DT, DT
    BASE = {"gates": 0, "merge": GATES, "out": GATES + MERGE}
    n = GATES + MERGE + OUT
    for i, (_, tiles) in enumerate(PARTS):
        BASE["up", i] = n
        BASE["down", i] = n + 2 * tiles
        n += 2 * tiles + 2 * DT
    JOBS = n
    ACT_BASE = {"gates": 0, ("up", 0): GATES, ("up", 1): GATES + PARTS[0][1]}
    ACT_USES = GATES + HT
    DVE_BASE = {"turn": 0, "merge": DT, "out": 3 * DT, ("up", 0): 4 * DT}
    DVE_BASE["down", 0] = 4 * DT + PARTS[0][1]
    DVE_BASE["up", 1] = DVE_BASE["down", 0] + DT
    DVE_BASE["down", 1] = DVE_BASE["up", 1] + PARTS[1][1]
    DVE_USES = DVE_BASE["down", 1] + DT
    BANK_TURN, BANK_SUM, BANK_ACT, BANK_DVE = 0, 2, 4, 6
    WINDOW = T + TAPS - 1
    CONV_STEPS = CT * TAPS

    with ExitStack() as ctx:
        sb, sem = open_tensors(ctx, nc, "mix")
        ps = k.ps
        raw = sb("raw", [P, 2, DT, P])
        wt = sb("wt", [P, 2, 2, DT, P], F32R)
        x1 = sb("x1", [P, DT, T])
        h = sb("h", [P, DT, 2, T], F32R)
        hb = sb("hb", [P, 2, T])
        cu = sb("cu", [P, CT, WINDOW])
        cacc = sb("cacc", [P, CT, T])
        tmp = sb("tmp", [P, 4, T])
        gfin = sb("gfin", [P, D])
        ss, rstd, oss, orstd = sb("ss", [P, TT]), sb("rstd", [P, TT]), sb("oss", [P, TT]), sb("orstd", [P, TT])
        a2 = sb("a2", [P, DT])
        sizes = {"a": 8 * D * 4, "b": 12 * D * 4}
        addresses = {}
        for region, size in sizes.items():
            sb(f"region_{region}", [P, size // 4])
            addresses[region] = nc.sbuf_base - size
        attn = sb("attn", [P, CT, 2, T], F32R)

        def view(region, name, shape, dt, at=0):
            return nc.alloc_sbuf_tensor_at(f"mix_{name}", shape, dt, offset=addresses[region] + at)

        xtok = view("a", "xtok", [P, TT, D], F32)
        xn = view("a", "xn", [P, TT, D], F32, TT * D * 4)
        y = view("a", "y", [P, DT, 2, T], F32R)
        gate = view("b", "gate", [P, 2 * DT, T], F32)
        z = view("b", "z", [P, CT, 2, T], F32R, 2 * DT * T * 4)
        hid = view("b", "hid", [P, PARTS[0][1], 2, T], F32R)
        ob = view("b", "ob", [P, 2, D], F32)

        (x_squared, x_std, x_rstd, x_scaled, raw_turned, x_turned, turn_free, h_hi, h_lo) = (
            sem(n) for n in
            "x_squared x_std x_rstd x_scaled raw_turned x_turned turn_free h_hi h_lo".split())
        (w_hi, w_lo, job_done, act_free, dve_free, conv_step, ln_summed, centred, ln_squared) = (
            sem(n) for n in
            "w_hi w_lo job_done act_free dve_free conv_step ln_summed centred ln_squared".split())
        (ln_std, ln_rstd, ln_scaled, z_act, z_hi, z_lo, y_sum, y_hi, y_lo) = (
            sem(n) for n in
            "ln_std ln_rstd ln_scaled z_act z_hi z_lo y_sum y_hi y_lo".split())
        (x1_squared, x1_summed, f_summed, f_std, f_rstd, h2_scaled, h2_hi, h2_lo, a_hi) = (
            sem(n) for n in
            "x1_squared x1_summed f_summed f_std f_rstd h2_scaled h2_hi h2_lo a_hi".split())
        (a_lo, o_turned, o_squared, o_std, o_rstd, o_scaled, a2_done, sum_cleared, gfin_loaded) = (
            sem(n) for n in
            "a_lo o_turned o_squared o_std o_rstd o_scaled a2_done sum_cleared gfin_loaded".split())
        (x_loaded, u_loaded, attn_loaded) = (
            sem(n) for n in
            "x_loaded u_loaded attn_loaded".split())
        raw_loaded = [sem(f"raw_loaded{i}") for i in range(2)]
        o_stored = [sem(f"o_stored{i}") for i in range(2)]

        def groups(eng, body):
            body(0, True, False)
            with eng.Fori(1, GROUPS - 1) as g:
                body(g, False, False)
            body(GROUPS - 1, False, True)

        with nc.Block() as block:

            @block.sync
            def _(sp):
                sp.dma_start(gfin[:, :], w["g_final"].partition_broadcast(P)).then_inc(gfin_loaded, 16)

                def load(g, at, parity, *pairs):
                    sp.wait_ge(w_lo, turn(g * JOBS + at))
                    for to, src in pairs:
                        sp.dma_start(raw[:, parity, to[0]:to[1]], src).then_inc(raw_loaded[parity], 32 // len(pairs))

                def tiles(name, first, last, col):
                    return w[name][0, first * P:last * P].rearrange("(f p) m -> p f m", p=P)[:, :, bass.ds(col, P)]

                def gate_jobs(g, m):
                    for i in range(2):
                        load(g, BASE["gates"] + 2 * m + i, i, ((0, DT), tiles("w_in", 0, DT, IN_GATE + i * D + m * P)))

                def prefetch_x(g):
                    sp.dma_start(xtok[:, :, :],
                                 w["x"][0].rearrange("(g t p) f -> p g t f", t=TT, p=P)[:, bass.ds(g, 1)]
                                 .rearrange("p g t f -> p (g t) f")).then_inc(x_loaded, 16)

                def prefetch_u(g):
                    sp.dma_start(cu[:, :, :], k.u_dram.rearrange("(c p) t -> p c t", p=P)
                                 [:, :, bass.ds(g * T, WINDOW)]).then_inc(u_loaded, 16)

                def prefetch_attn(g):
                    for c in range(CT):
                        sp.dma_start(attn[:, c].bitcast(F32), k.attn_dram[c * P:(c + 1) * P, :, bass.ds(g * T, T)])\
                            .then_inc(attn_loaded, 16)

                def up_jobs(g, p, begin, end):
                    with sp.Fori(begin, end) as t:
                        for i in range(2):
                            load(g, BASE["up", p] + 2 * t + i, i,
                                 ((0, DT), tiles("w_gu", 0, DT, i * HID + (PARTS[p][0] + t) * P)))

                def body(g, last):
                    with sp.Fori(0, DT) as m:
                        gate_jobs(g, m)
                    with sp.Fori(0, DT // 2) as mm:
                        for i in range(2):
                            m = mm * 2 + i
                            load(g, BASE["merge"] + m, i, ((0, CT), tiles("w_o_attn", 0, CT, m * P)),
                                 ((CT, DT), tiles("w_pw2", 0, CT, m * P)))
                    with sp.Fori(0, DT // 2) as mm:
                        for i in range(2):
                            m = mm * 2 + i
                            load(g, BASE["out"] + m, i, ((0, DT), tiles("w_out", 0, DT, m * P)))
                    for p, (first, num) in enumerate(PARTS):
                        if p == 0 and not last:
                            up_jobs(g, p, 0, 1)
                            sp.wait_ge(z_lo, (g + 1) * CT)
                            prefetch_u(g + 1)
                            up_jobs(g, p, 1, 3)
                            sp.wait_ge(job_done, done(g * JOBS + BASE["up", 0] - 1))
                            prefetch_x(g + 1)
                            up_jobs(g, p, 3, 6)
                            prefetch_attn(g + 1)
                            up_jobs(g, p, 6, num)
                        else:
                            up_jobs(g, p, 0, num)
                        with sp.Fori(0, DT) as m:
                            for i in range(2):
                                load(g, BASE["down", p] + 2 * m + i, i,
                                     ((0, num // 2), tiles("w_down", first + i * num // 2,
                                                           first + (i + 1) * num // 2, m * P)))

                prefetch_x(0)
                prefetch_u(0)
                prefetch_attn(0)
                with sp.Fori(0, GROUPS - 1) as g:
                    body(g, False)
                body(GROUPS - 1, True)
                gate_jobs(GROUPS, 0)

            @block.gpsimd
            def _(pool):
                seeded(pool, w_lo)

                def lows(g, base, pairs):
                    with pool.Fori(0, pairs) as t:
                        for i in range(2):
                            pool.wait_ge(w_hi, g * JOBS + base + 2 * t + i + 1)
                            pool.tensor_tensor(wt[:, i, 1], raw[:, i], wt[:, i, 0].bitcast(F32), ALU.subtract)\
                                .then_inc(w_lo, 1)

                with pool.Fori(0, GROUPS) as g:
                    lows(g, 0, JOBS // 2)
                lows(GROUPS, 0, 1)

            @block.scalar
            def _(act):
                seeded(act, act_free, turn_free)

                def hi(g, at, parity, use):
                    act.wait_ge(raw_loaded[parity], 32 * (g * (JOBS // 2) + use + 1))
                    act.wait_ge(job_done, turn(g * JOBS + at))
                    act.activation(wt[:, parity, 0], raw[:, parity], ACT.Copy).then_inc(w_hi, 1)

                def ahead(g, base, t, i):
                    hi(g, base + 2 * t + i + 2, i, base // 2 + t + 1)

                def x_stats(g):
                    act.wait_ge(x_loaded, 16 * (g + 1))
                    for t in range(TT):
                        act.wait_ge(x_squared, g * TT + t)
                        act.activation(hb[:, :, :].rearrange("p a b -> p (a b)"), xtok[:, t, :], ACT.Square,
                                       accum_out=ss[:, t:t + 1]).then_inc(x_squared, 1)
                    act.wait_ge(x_squared, (g + 1) * TT)
                    act.activation(rstd[:, :], ss[:, :], ACT.Sqrt, bias=k.eps[:, :], scale=1.0 / D).then_inc(x_std, 1)

                def ln_squares(g):
                    for c in range(CT):
                        act.wait_ge(centred, g * CT + c + 1)
                        act.activation(cu[:, c, 0:T], cacc[:, c, :], ACT.Square).then_inc(ln_squared, 1)

                def ln_root(g):
                    act.wait_ge(ln_summed, 2 * g + 2)
                    act.activation(tmp[:, 3, :], ps[:, BANK_SUM + 1, :], ACT.Sqrt, bias=k.eps[:, :], scale=1.0 / CONV)\
                        .then_inc(ln_std, 1)

                def ln_silu(g):
                    for c in range(CT):
                        act.wait_ge(ln_scaled, g * CT + c + 1)
                        act.activation(cu[:, c, 0:T], cacc[:, c, :], ACT.Silu, bias=k.vec[:, V_BCN + c:V_BCN + c + 1],
                                       scale=k.vec[:, V_GCN + c:V_GCN + c + 1]).then_inc(z_act, 1)

                def gates(g, begin, end):
                    with act.Fori(begin, end) as m:
                        for i in range(2):
                            ahead(g, BASE["gates"], m, i)
                            act.wait_ge(job_done, done(g * JOBS + 2 * m + i))
                            act.activation(gate[:, bass.ds(2 * m + i, 1), :].rearrange("p a t -> p (a t)"),
                                           ps[:, BANK_ACT + i, :], ACT.Sigmoid).then_inc(act_free, 1)

                def body(g, first, last):
                    for f in range(DT):
                        act.wait_ge(x_turned, g * DT + f + 1)
                        act.wait_ge(h_lo, turn(g * DT + f))
                        act.activation(hb[:, f % 2, :], ps[:, BANK_TURN + f % 2, :], ACT.Identity,
                                       bias=k.mod[:, SH1 + f:SH1 + f + 1], scale=k.a1[:, f:f + 1])\
                            .then_inc(turn_free, 1)
                    if not first:
                        ln_squares(g)
                    for i in range(2):
                        act.wait_ge(o_stored[i], 16 * (g * (TT // 2) + 1))
                    if first:
                        gates(g, 0, DT)
                        ln_squares(g)
                        ln_root(g)
                        ln_silu(g)
                    else:
                        gates(g, 0, 2)
                        ln_root(g)
                        gates(g, 2, 3)
                        ln_silu(g)
                        gates(g, 3, DT)
                    with act.Fori(0, MERGE // 2) as mm:
                        for i in range(2):
                            ahead(g, BASE["merge"], mm, i)
                    with act.Fori(0, OUT // 2) as mm:
                        for i in range(2):
                            ahead(g, BASE["out"], mm, i)
                            m = 2 * mm + i
                            act.wait_ge(dve_free, done(g * DVE_USES + DVE_BASE["out"] + m))
                            act.wait_ge(x1_summed, turn(g * DT + m))
                            act.activation(tmp[:, i, :], x1[:, bass.ds(m, 1), :].rearrange("p a t -> p (a t)"),
                                           ACT.Square).then_inc(x1_squared, 1)
                    act.wait_ge(f_summed, g + 1)
                    act.activation(tmp[:, 3, :], ps[:, BANK_SUM, :], ACT.Sqrt, bias=k.eps[:, :], scale=1.0 / D)\
                        .then_inc(f_std, 1)
                    for f in range(DT):
                        act.wait_ge(h2_scaled, g * DT + f + 1)
                        act.activation(h[:, f, 0, :], hb[:, f % 2, :], ACT.Identity,
                                       bias=k.mod[:, SH2 + f:SH2 + f + 1]).then_inc(h2_hi, 1)
                    for p, (_, num) in enumerate(PARTS):
                        with act.Fori(0, num // 2) as tt:
                            for a in range(2):
                                t = 2 * tt + a
                                for i in range(2):
                                    ahead(g, BASE["up", p], t, i)
                                    if i == 0:
                                        act.wait_ge(job_done, done(g * JOBS + BASE["up", p] + 2 * t))
                                        act.wait_ge(a_lo, turn(g * HT + PARTS[p][0] + t))
                                        act.activation(tmp[:, a, :], ps[:, BANK_ACT + a, :], ACT.Silu)\
                                            .then_inc(act_free, 1)
                        with act.Fori(0, DT) as m:
                            for i in range(2):
                                ahead(g, BASE["down", p], m, i)
                        if p == 0 and not last:
                            x_stats(g + 1)
                    for t in range(TT):
                        b = BANK_TURN + 2 * (t % 2)
                        act.wait_ge(o_turned, g * TT + t + 1)
                        act.wait_ge(o_squared, g * TT + t)
                        act.activation(hb[:, :, :], ps[:, b:b + 2, :], ACT.Square, accum_out=oss[:, t:t + 1])\
                            .then_inc(o_squared, 1)
                        act.wait_ge(o_squared, g * TT + t + 1)
                        act.activation(orstd[:, t:t + 1], oss[:, t:t + 1], ACT.Sqrt, bias=k.eps[:, :], scale=1.0 / D)\
                            .then_inc(o_std, 1)
                        if t:
                            store_out(g, t - 1)
                    store_out(g, TT - 1)

                def store_out(g, t):
                    act.wait_ge(o_scaled, g * TT + t + 1)
                    act.dma_start(out[0, bass.ds(g * T + t * P, P), :], ob[:, t % 2, :]).then_inc(o_stored[t % 2], 16)

                x_stats(0)
                for i in range(2):
                    hi(0, i, i, 0)
                groups(act, body)
                for i in range(2):
                    act.wait_ge(o_stored[i], 16 * (1 + GROUPS * TT // 2))

            @block.tensor
            def _(pe):
                seeded(pe, job_done)

                def product(bank, parity, tiles, moving, first=True, last=True, wait=None):
                    for f in tiles:
                        if wait:
                            wait(f)
                        for st, m in ((0, 0), (0, 1), (1, 0)):
                            ins = pe.matmul(ps[:, bank, :], wt[:, parity, st, f, :], moving(f, m),
                                            start=(first and f == tiles[0] and st == m == 0),
                                            stop=(last and f == tiles[-1] and st == 1))
                    return ins

                def mean(g):
                    pe.wait_ge(conv_step, (g + 1) * CONV_STEPS)
                    for c in range(CT):
                        ins = pe.matmul(ps[:, BANK_SUM, :], k.ones[:, :], cacc[:, c, :], start=(c == 0), stop=(c == CT - 1))
                    ins.then_inc(ln_summed, 1)

                def variance(g):
                    for c in range(CT):
                        pe.wait_ge(ln_squared, g * CT + c + 1)
                        ins = pe.matmul(ps[:, BANK_SUM + 1, :], k.ones[:, :], cu[:, c, 0:T],
                                        start=(c == 0), stop=(c == CT - 1))
                    ins.then_inc(ln_summed, 1)

                def body(g, first, last):
                    pe.wait_ge(o_scaled, g * TT)
                    if not first:
                        mean(g)
                    pe.wait_ge(x_loaded, 16 * (g + 1))
                    for f in range(DT):
                        pe.wait_ge(dve_free, turn(g * DVE_USES + f))
                        for t in range(TT):
                            ins = pe.transpose(ps[:, BANK_DVE + f % 2, t * P:(t + 1) * P],
                                               xtok[:, t, f * P:(f + 1) * P], k.ident[:, :])
                        ins.then_inc(raw_turned, 1)
                    pe.wait_ge(x_scaled, (g + 1) * TT)
                    for f in range(DT):
                        pe.wait_ge(turn_free, turn(g * DT + f))
                        for t in range(TT):
                            ins = pe.transpose(ps[:, BANK_TURN + f % 2, t * P:(t + 1) * P],
                                               xn[:, t, f * P:(f + 1) * P], k.ident[:, :])
                        ins.then_inc(x_turned, 1)
                    if not first:
                        variance(g)
                    with pe.Fori(0, DT) as m:
                        for i in range(2):
                            pe.wait_ge(w_lo, done(g * JOBS + 2 * m + i))
                            pe.wait_ge(act_free, turn(g * ACT_USES + 2 * m + i))
                            wait = (lambda f: pe.wait_ge(h_lo, done(g * DT + f))) if i == 0 else None
                            product(BANK_ACT + i, i, range(DT), lambda f, m: h[:, f, m, :], wait=wait)\
                                .then_inc(job_done, 1)
                    if first:
                        mean(g)
                        variance(g)
                    with pe.Fori(0, MERGE // 2) as mm:
                        pe.wait_ge(attn_loaded, 16 * CT * (g + 1))
                        for i in range(2):
                            m = 2 * mm + i
                            pe.wait_ge(w_lo, done(g * JOBS + BASE["merge"] + m))
                            use = g * DVE_USES + DVE_BASE["merge"] + 2 * m
                            pe.wait_ge(dve_free, turn(use))
                            product(BANK_DVE, i, range(CT), lambda f, m: attn[:, f, m, :])
                            pe.wait_ge(z_lo, (g + 1) * CT)
                            pe.wait_ge(dve_free, turn(use + 1))
                            product(BANK_DVE + 1, i, range(CT, DT), lambda f, m: z[:, f - CT, m, :])\
                                .then_inc(job_done, 1)
                    with pe.Fori(0, OUT // 2) as mm:
                        for i in range(2):
                            m = 2 * mm + i
                            pe.wait_ge(w_lo, done(g * JOBS + BASE["out"] + m))
                            pe.wait_ge(dve_free, turn(g * DVE_USES + DVE_BASE["out"] + m))
                            wait = (lambda f: pe.wait_ge(y_lo, done(g * DT + f, 1))) if i == 0 else None
                            product(BANK_DVE + i, i, range(DT), lambda f, m: y[:, f, m, :], wait=wait)\
                                .then_inc(job_done, 1)
                    pe.wait_ge(x1_summed, done(g * DT + DT - 1))
                    pe.matmul(ps[:, BANK_SUM, :], k.ones[:, :], tmp[:, 2, :], start=True, stop=True)\
                        .then_inc(f_summed, 1)
                    for p, (begin, num) in enumerate(PARTS):
                        with pe.Fori(0, num // 2) as tt:
                            for a in range(2):
                                t = 2 * tt + a
                                for i in range(2):
                                    pe.wait_ge(w_lo, done(g * JOBS + BASE["up", p] + 2 * t + i))
                                    if i == 0:
                                        pe.wait_ge(act_free, turn(g * ACT_USES + ACT_BASE["up", p] + t))
                                    else:
                                        pe.wait_ge(dve_free, turn(g * DVE_USES + DVE_BASE["up", p] + t))
                                    wait = (lambda f: pe.wait_ge(h2_lo, g * DT + f + 1)) if p == a == i == 0 else None
                                    product((BANK_DVE if i else BANK_ACT) + a, i, range(DT),
                                            lambda f, m: h[:, f, m, :], wait=wait).then_inc(job_done, 1)
                        with pe.Fori(0, DT // 2) as mm:
                            for a in range(2):
                                m = 2 * mm + a
                                pe.wait_ge(dve_free, turn(g * DVE_USES + DVE_BASE["down", p] + m))
                                for i in range(2):
                                    pe.wait_ge(w_lo, done(g * JOBS + BASE["down", p] + 2 * m + i))
                                    at = i * num // 2
                                    if a == 0:
                                        pe.wait_ge(a_lo, done(g * HT + begin + at + num // 2 - 1))
                                    product(BANK_DVE + a, i, range(num // 2), lambda f, m: hid[:, at + f, m, :],
                                            first=(i == 0), last=(i == 1)).then_inc(job_done, 1)
                    pe.wait_ge(dve_free, done(g * DVE_USES + DVE_USES - 1))
                    for t in range(TT):
                        b = BANK_TURN + 2 * (t % 2)
                        if t > 1:
                            pe.wait_ge(o_scaled, g * TT + t - 1)
                        for f in range(DT):
                            ins = pe.transpose(ps[:, b + f // TT, (f % TT) * P:(f % TT + 1) * P],
                                               x1[:, f, t * P:(t + 1) * P], k.ident[:, :])
                        ins.then_inc(o_turned, 1)

                groups(pe, body)

            @block.vector
            def _(dve):
                seeded(dve, h_lo, dve_free, x1_summed, a_lo)
                seeded(dve, y_lo, by=1)
                seeded(dve, *o_stored, by=16)

                def scale_x(g):
                    dve.wait_ge(x_std, g + 1)
                    dve.reciprocal(rstd[:, :], rstd[:, :]).then_inc(x_rstd, 1)
                    dve.wait_ge(x_rstd, g + 1)
                    for t in range(TT):
                        dve.tensor_scalar(xn[:, t, :], xtok[:, t, :], rstd[:, t:t + 1], None, ALU.mult)\
                            .then_inc(x_scaled, 1)

                def conv_first(g, pair):
                    for i in range(2):
                        c = 2 * pair + i
                        dve.tensor_scalar(cacc[:, c, :], cu[:, c, 0:T], k.wdw[:, c, 0:1], k.vec[:, V_BDW + c:V_BDW + c + 1],
                                          ALU.mult, ALU.add).then_inc(conv_step, 1)

                def conv_tap(g, pair, tap):
                    for i in range(2):
                        c = 2 * pair + i
                        dve.wait_ge(conv_step, g * CONV_STEPS + pair * 2 * TAPS + 2 * tap + i - 1)
                        dve.scalar_tensor_tensor(cacc[:, c, :], cu[:, c, bass.ds(tap, T)], k.wdw[:, c, bass.ds(tap, 1)],
                                                 cacc[:, c, :], ALU.mult, ALU.add).then_inc(conv_step, 1)

                def ln_centre(g):
                    dve.wait_ge(ln_summed, 2 * g + 1)
                    for c in range(CT):
                        dve.scalar_tensor_tensor(cacc[:, c, :], ps[:, BANK_SUM, :], -1.0 / CONV, cacc[:, c, :],
                                                 ALU.mult, ALU.add).then_inc(centred, 1)

                def ln_finish(g):
                    dve.wait_ge(ln_std, g + 1)
                    dve.reciprocal(tmp[:, 3, :], tmp[:, 3, :]).then_inc(ln_rstd, 1)
                    dve.wait_ge(ln_rstd, g + 1)
                    for c in range(CT):
                        dve.tensor_tensor(cacc[:, c, :], cacc[:, c, :], tmp[:, 3, :], ALU.mult).then_inc(ln_scaled, 1)
                    for c in range(CT):
                        dve.wait_ge(z_act, g * CT + c + 1)
                        dve.tensor_copy(z[:, c, 0, :], cu[:, c, 0:T]).then_inc(z_hi, 1)
                        dve.wait_ge(z_hi, g * CT + c + 1)
                        dve.tensor_tensor(z[:, c, 1, :], cu[:, c, 0:T], z[:, c, 0, :].bitcast(F32), ALU.subtract)\
                            .then_inc(z_lo, 1)

                def one(tensor, index, *rest):
                    return tensor[(slice(None), bass.ds(index, 1)) + rest].rearrange("p a t -> p (a t)")

                def residual(m, a, scale):
                    dve.scalar_tensor_tensor(one(x1, m), ps[:, BANK_DVE + a, :], k.mod[:, bass.ds(scale + m, 1)],
                                             one(x1, m), ALU.mult, ALU.add).then_inc(dve_free, 1)

                def body(g, first, last):
                    if not first:
                        ln_centre(g)
                    for f in range(DT):
                        dve.wait_ge(raw_turned, g * DT + f + 1)
                        dve.tensor_copy(x1[:, f, :], ps[:, BANK_DVE + f % 2, :]).then_inc(dve_free, 1)
                    for f in range(DT):
                        dve.wait_ge(turn_free, done(g * DT + f))
                        dve.tensor_copy(h[:, f, 0, :], hb[:, f % 2, :]).then_inc(h_hi, 1)
                        dve.wait_ge(h_hi, g * DT + f + 1)
                        dve.tensor_tensor(h[:, f, 1, :], hb[:, f % 2, :], h[:, f, 0, :].bitcast(F32), ALU.subtract)\
                            .then_inc(h_lo, 1)
                    if first:
                        dve.wait_ge(u_loaded, 16)
                        for pair in range(CT // 2):
                            conv_first(g, pair)
                            with dve.Fori(0, (TAPS - 1) // 6) as i:
                                for j in range(6):
                                    conv_tap(g, pair, i * 6 + j + 1)
                        ln_centre(g)
                    ln_finish(g)
                    with dve.Fori(0, MERGE // 2) as mm:
                        for a in range(2):
                            m = 2 * mm + a
                            use = g * DVE_USES + DVE_BASE["merge"] + 2 * m
                            dve.wait_ge(job_done, done(g * JOBS + BASE["merge"] + m))
                            dve.wait_ge(y_lo, done(g * DT + m - 1, 1))
                            for i in range(2):
                                dve.tensor_tensor(tmp[:, i, :], ps[:, BANK_DVE + i, :], one(gate, 2 * m + i), ALU.mult)\
                                    .then_inc(dve_free, 1)
                            dve.wait_ge(dve_free, done(use + 1))
                            dve.tensor_tensor(tmp[:, 0, :], tmp[:, 0, :], tmp[:, 1, :], ALU.add).then_inc(y_sum, 1)
                            dve.wait_ge(y_sum, g * DT + m + 1)
                            sum_hi = y[:, bass.ds(m, 1), 0, :].rearrange("p a t -> p (a t)")
                            sum_lo = y[:, bass.ds(m, 1), 1, :].rearrange("p a t -> p (a t)")
                            dve.tensor_copy(sum_hi, tmp[:, 0, :]).then_inc(y_hi, 1)
                            dve.wait_ge(y_hi, g * DT + m + 1)
                            dve.tensor_tensor(sum_lo, tmp[:, 0, :], sum_hi.bitcast(F32), ALU.subtract).then_inc(y_lo, 1)
                    dve.wait_ge(a_lo, done(g * HT - 1))
                    dve.memset(tmp[:, 2, :], 0.0).then_inc(sum_cleared, 1)
                    with dve.Fori(0, OUT // 2) as mm:
                        for a in range(2):
                            m = 2 * mm + a
                            dve.wait_ge(job_done, done(g * JOBS + BASE["out"] + m))
                            residual(m, a, GT1)
                            dve.wait_ge(x1_squared, g * DT + m + 1)
                            dve.wait_ge(sum_cleared, g + 1)
                            dve.wait_ge(x1_summed, done(g * DT + m - 1))
                            dve.tensor_tensor(tmp[:, 2, :], tmp[:, 2, :], tmp[:, a, :], ALU.add).then_inc(x1_summed, 1)
                    dve.wait_ge(f_std, g + 1)
                    dve.reciprocal(tmp[:, 3, :], tmp[:, 3, :]).then_inc(f_rstd, 1)
                    dve.wait_ge(f_rstd, g + 1)
                    for f in range(DT):
                        if f > 1:
                            dve.wait_ge(h2_lo, g * DT + f - 1)
                        dve.scalar_tensor_tensor(hb[:, f % 2, :], x1[:, f, :], a2[:, f:f + 1], tmp[:, 3, :],
                                                 ALU.mult, ALU.mult).then_inc(h2_scaled, 1)
                        dve.wait_ge(h2_hi, g * DT + f + 1)
                        dve.scalar_tensor_tensor(h[:, f, 1, :], hb[:, f % 2, :], k.mod[:, SH2 + f:SH2 + f + 1],
                                                 h[:, f, 0, :].bitcast(F32), ALU.add, ALU.subtract).then_inc(h2_lo, 1)
                    for p, (begin, num) in enumerate(PARTS):
                        per = (TAPS - 1) * 2 // num
                        if not last:
                            if p == 0:
                                dve.wait_ge(u_loaded, 16 * (g + 2))
                            conv_first(g + 1, p)
                        with dve.Fori(0, num // 2) as tt:
                            for a in range(2):
                                t = 2 * tt + a
                                dve.wait_ge(act_free, done(g * ACT_USES + ACT_BASE["up", p] + t))
                                dve.wait_ge(job_done, done(g * JOBS + BASE["up", p] + 2 * t + 1))
                                dve.wait_ge(a_lo, done(g * HT + begin + t - 1))
                                dve.tensor_tensor(tmp[:, 2, :], ps[:, BANK_DVE + a, :], tmp[:, a, :], ALU.mult)\
                                    .then_inc(dve_free, 1)
                                dve.wait_ge(dve_free, done(g * DVE_USES + DVE_BASE["up", p] + t))
                                hid_hi = hid[:, bass.ds(t, 1), 0, :].rearrange("p a t -> p (a t)")
                                hid_lo = hid[:, bass.ds(t, 1), 1, :].rearrange("p a t -> p (a t)")
                                dve.tensor_copy(hid_hi, tmp[:, 2, :]).then_inc(a_hi, 1)
                                dve.wait_ge(a_hi, g * HT + begin + t + 1)
                                dve.tensor_tensor(hid_lo, tmp[:, 2, :], hid_hi.bitcast(F32), ALU.subtract)\
                                    .then_inc(a_lo, 1)
                                if not last:
                                    for j in range(a * (per // 2), per if a else per // 2):
                                        conv_tap(g + 1, p, tt * per + j + 1)
                        if p == 1 and not last:
                            scale_x(g + 1)
                        with dve.Fori(0, DT // 2) as mm:
                            for a in range(2):
                                m = 2 * mm + a
                                dve.wait_ge(job_done, done(g * JOBS + BASE["down", p] + 2 * m + 1))
                                residual(m, a, GT2)
                    for t in range(TT):
                        b = BANK_TURN + 2 * (t % 2)
                        dve.wait_ge(o_std, g * TT + t + 1)
                        dve.reciprocal(orstd[:, t:t + 1], orstd[:, t:t + 1]).then_inc(o_rstd, 1)
                        dve.wait_ge(o_rstd, g * TT + t + 1)
                        dve.wait_ge(o_stored[t % 2], 16 * (g * (TT // 2) + t // 2 + 1))
                        dve.scalar_tensor_tensor(ob[:, t % 2, :], ps[:, b:b + 2, :].rearrange("p a t -> p (a t)"),
                                                 orstd[:, t:t + 1], gfin[:, :], ALU.mult, ALU.mult)\
                            .then_inc(o_scaled, 1)

                dve.scalar_tensor_tensor(a2[:, :], k.mod[:, SC2:SC2 + DT], 1.0, k.vec[:, V_GFFN:V_GFFN + DT],
                                         ALU.add, ALU.mult).then_inc(a2_done, 1)
                dve.wait_ge(a2_done, 1)
                dve.wait_ge(gfin_loaded, 16)
                scale_x(0)
                groups(dve, body)


def layer(nc, w, out):
    with ExitStack() as ctx:
        k = Kept()
        k.ps = ctx.enter_context(nc.psum_tensor("ps", [P, 8, T], F32))

        def keep(name, shape):
            return ctx.enter_context(nc.sbuf_tensor(name, shape, F32))

        k.vec = keep("vec", [P, V_ROWS])
        k.wdw = keep("wdw", [P, CT, TAPS])
        k.mod = keep("mod", [P, 6 * DT])
        k.a1 = keep("a1", [P, DT])
        k.c_act = keep("c_act", [P, DT])
        k.ident = keep("ident", [P, P])
        k.ones = keep("ones", [P, P])
        k.eps = keep("eps", [P, 1])
        k.u_dram = nc.dram_tensor("u_dram", [CONV, TAPS - 1 + SEQ], F32).ap()
        k.qn_dram = nc.dram_tensor("qn_dram", [HEADS * NOPE, 2, SEQ], F32).ap()
        k.qr_dram = nc.dram_tensor("qr_dram", [HEADS * ROPE, 2, SEQ], F32).ap()
        k.kn_dram = nc.dram_tensor("kn_dram", [HEADS * NOPE, 2, SEQ], F32).ap()
        k.kr_dram = nc.dram_tensor("kr_dram", [ROPE, 2, SEQ], F32).ap()
        k.v_dram = nc.dram_tensor("v_dram", [SEQ, HEADS * 2 * VD], F32).ap()
        k.attn_dram = nc.dram_tensor("attn_dram", [HEADS * VD, 2, SEQ], F32).ap()
        with nc.sbuf_tensor("cos", [P, SEQ], F32) as k.cos, nc.sbuf_tensor("sin", [P, SEQ], F32) as k.sin:
            modulation(nc, w, k)
            project(nc, w, k)
        attend(nc, w, k)
        mix(nc, w, k, out)


_NAMES = ["x", "c", "positions", "w_ada", "b_ada", "g_mix", "w_in", "g_q", "w_uq", "g_kv", "w_ukv", "w_o_attn",
          "w_dw", "b_dw", "g_cn", "b_cn", "w_pw2", "w_out", "g_ffn", "w_gu", "w_down", "g_final"]


def kernel(**inputs):
    import numpy as _np
    import concourse.bacc as _bacc
    from concourse import mybir as _mybir
    from concourse.bass_utils import run_bass_kernel_spmd as _run

    nc = _bacc.Bacc("TRN2", target_bir_lowering=False, num_devices=1)
    row = _np.arange(P) % ROPE
    freq = ROPE_THETA ** (-2.0 * (row % (ROPE // 2)) / ROPE)
    rope_const = _np.stack([freq, _np.where(row < ROPE // 2, -1.0, 1.0)], axis=1).astype(_np.float32)
    arrays, w = {}, {}
    for name in _NAMES + ["rope_const"]:
        a = _np.ascontiguousarray(inputs[name]) if name in inputs else rope_const
        arrays[f"in_{name}"] = a
        w[name] = nc.dram_tensor(f"in_{name}", a.shape, _mybir.dt.from_np(a.dtype), kind="ExternalInput").ap()
    out = nc.dram_tensor("out", (1, SEQ, D), F32, kind="ExternalOutput").ap()
    layer(nc, w, out)
    r = _run(nc, [arrays], core_ids=[0])
    return r.results[0]["out"]
```

```python
import math
from contextlib import ExitStack

import concourse.bass as bass
from concourse import mybir

F32 = mybir.dt.float32
F32R = mybir.dt.float32r
I32 = mybir.dt.int32
ALU = mybir.AluOpType
ACT = mybir.ActivationFunctionType
AX_X = mybir.AxisListType.X

P = 128
D = 1024
SEQ = 2048
HEADS = 8
NOPE = 64
ROPE = 32
QK = NOPE + ROPE
VD = 64
QL = 384
KVL = 256
CONV = 512
TAPS = 31
HID = 2816
EPS = 1e-6
ROPE_THETA = 10000.0

DT = D // P
T = 512
GROUPS = SEQ // T
TT = T // P
QT, KT, CT, HT = QL // P, KVL // P, CONV // P, HID // P
IN_GLU = QL + KVL + ROPE
IN_GATE = IN_GLU + 2 * CONV

V_BADA, V_GMIX, V_GFFN, V_GQ, V_GKV, V_GCN, V_BCN, V_BDW, V_C = 0, 48, 56, 64, 67, 69, 73, 77, 81
V_ROWS = V_C + DT
SH1, SC1, GT1, SH2, SC2, GT2 = (s * DT for s in range(6))


class Kept:
    pass


def open_tensors(ctx, nc, phase):
    def sb(name, shape, dt=F32):
        return ctx.enter_context(nc.sbuf_tensor(f"{phase}_{name}", shape, dt))

    def sem(name):
        return ctx.enter_context(nc.semaphore(f"{phase}_{name}"))

    return sb, sem


def modulation(nc, w, k):
    with ExitStack() as ctx:
        sb, sem = open_tensors(ctx, nc, "modulation")
        ps = k.ps
        vrow = sb("vrow", [V_ROWS, P])
        wdw_row = sb("wdw_row", [TAPS, CONV])
        zero = sb("zero", [P, CT, TAPS - 1])
        const = sb("const", [P, 2])
        pos_i = sb("pos_i", [P, SEQ], I32)
        ang = sb("ang", [P, SEQ])
        turns = sb("turns", [P, SEQ])
        half_pi = sb("half_pi", [P, 1])
        wada = sb("wada", [P, 4, D])
        mod_row = sb("mod_row", [1, 2, D])
        up_raw = sb("up_raw", [P, 2, D])
        squares = sb("squares", [P, D])

        x_loaded, x_squared, x_std, x_rstd, x_scaled = k.x_progress
        up_loaded, up_hi, up_lo = [sem(f"up_loaded{i}") for i in range(2)], sem("up_hi"), sem("up_lo")
        vec_loaded, dw_loaded, pos_loaded = sem("vec_loaded"), sem("dw_loaded"), sem("pos_loaded")
        wada_loaded = [sem(f"wada_loaded{i}") for i in range(4)]
        zero_set, pad_stored = sem("zero_set"), sem("pad_stored")
        ident_cleared, ident_set, ones_set = sem("ident_cleared"), sem("ident_set"), sem("ones_set")

        vec_turned, vec_copied, dw_turned, dw_copied = (
            sem("vec_turned"), sem("vec_copied"), sem("dw_turned"), sem("dw_copied"))
        mod_moved = sem("mod_moved")
        c_active, mod_step, mod_summed, mod_done, rope_step, rope_sine = (
            sem("c_active"), sem("mod_step"), sem("mod_summed"), sem("mod_done"), sem("rope_step"),
            sem("rope_sine"))
        STEPS = 2 * DT
        UP = QT + KT

        def split_of(a):
            return (HEADS * QK, k.wuq[:, a]) if a < QT else (D, k.wukv[:, a - QT])

        with nc.Block() as block:

            @block.sync
            def _(sp):
                for row, name in ((V_BADA, "b_ada"), (V_GMIX, "g_mix"), (V_GFFN, "g_ffn"), (V_GQ, "g_q"),
                                  (V_GKV, "g_kv"), (V_GCN, "g_cn"), (V_BCN, "b_cn"), (V_BDW, "b_dw"), (V_C, "c")):
                    src = w[name].rearrange("a (r p) -> (a r) p", p=P)
                    sp.dma_start(vrow[row:row + src.shape[0], :], src).then_inc(vec_loaded, 16)
                sp.dma_start(wdw_row[:, :], w["w_dw"][0]).then_inc(dw_loaded, 16)
                for n in range(STEPS):
                    s, f = divmod(n, DT)
                    if n >= 4:
                        sp.wait_ge(mod_step, n - 3)
                    sp.dma_start(wada[:, n % 4, :], w["w_ada"][0, f * P:(f + 1) * P, s * D:(s + 1) * D])\
                        .then_inc(wada_loaded[n % 4], 16)

            @block.gpsimd
            def _(pool):
                pool.memset(k.ident[:, :], 0.0).then_inc(ident_cleared, 1)
                pool.memset(k.ones[:, :], 1.0).then_inc(ones_set, 1)
                pool.memset(zero[:, :, :], 0.0).then_inc(zero_set, 1)
                pool.memset(half_pi[:, :], math.pi / 2).then_inc(ones_set, 1)
                pool.memset(k.eps[:, :], EPS).then_inc(ones_set, 1)
                pool.wait_ge(ident_cleared, 1)
                pool.affine_select(out=k.ident[:, :], in_=k.ident[:, :], compare_op=ALU.not_equal, fill=1.0,
                                   base=0, pattern=[[-1, P]], channel_multiplier=1).then_inc(ident_set, 1)
                for a in range(UP):
                    pool.wait_ge(up_hi, a + 1)
                    wide, dst = split_of(a)
                    pool.tensor_tensor(dst[:, 1], up_raw[:, a % 2, 0:wide], dst[:, 0].bitcast(F32), ALU.subtract)\
                        .then_inc(up_lo, 1)

            @block.scalar
            def _(act):
                act.dma_start(pos_i[:, :], w["positions"].partition_broadcast(P)).then_inc(pos_loaded, 16)
                act.dma_start(const[:, :], w["rope_const"]).then_inc(pos_loaded, 16)
                act.dma_start(k.tokens[:, :, :], w["x"][0, 0:T].rearrange("(t p) f -> p t f", p=P))\
                    .then_inc(x_loaded, 16)
                uq = w["w_uq"][0].rearrange("(a p) (h e) -> a p h e", p=P, e=QK)
                ukv = w["w_ukv"][0].rearrange("(a p) (h e) -> a p h e", p=P, e=NOPE + VD)
                def load_up(a):
                    src = uq[a] if a < QT else ukv[a - QT]
                    if a > 1:
                        act.wait_ge(up_lo, a - 1)
                    split = HEADS * NOPE
                    rest = src.shape[2] - NOPE
                    act.dma_start(up_raw[:, a % 2, 0:split].rearrange("p (h e) -> p h e", h=HEADS), src[:, :, 0:NOPE])\
                        .then_inc(up_loaded[a % 2], 16)
                    act.dma_start(up_raw[:, a % 2, split:split + HEADS * rest].rearrange("p (h e) -> p h e", h=HEADS),
                                 src[:, :, NOPE:]).then_inc(up_loaded[a % 2], 16)
                load_up(0)
                load_up(1)
                act.wait_ge(zero_set, 1)
                act.dma_start(k.u_dram.rearrange("(c p) t -> p c t", p=P)[:, :, 0:TAPS - 1], zero[:, :, :])\
                    .then_inc(pad_stored, 16)
                act.wait_ge(vec_copied, 1)
                act.activation(k.c_act[:, :], k.vec[:, V_C:V_C + DT], ACT.Silu).then_inc(c_active, 1)
                act.wait_ge(ones_set, 3)
                for a in range(UP):
                    act.wait_ge(up_loaded[a % 2], (a // 2 + 1) * 32)
                    wide, dst = split_of(a)
                    act.activation(dst[:, 0], up_raw[:, a % 2, 0:wide], ACT.Copy).then_inc(up_hi, 1)
                    if a == 1:
                        act.wait_ge(x_loaded, 16)
                        for t in range(TT):
                            if t:
                                act.wait_ge(x_squared, t)
                            act.activation(squares[:, :], k.tokens[:, t, :], ACT.Square, accum_out=k.ss[:, t:t + 1])\
                                .then_inc(x_squared, 1)
                        act.wait_ge(x_squared, TT)
                        act.activation(k.rstd[:, :], k.ss[:, :], ACT.Sqrt, bias=k.eps[:, :], scale=1.0 / D)\
                            .then_inc(x_std, 1)
                    if a + 2 < UP:
                        load_up(a + 2)
                for s in range(2):
                    act.wait_ge(mod_step, DT * (s + 1))
                    act.activation(mod_row[0:1, s, :].rearrange("p (a t) -> p a t", a=2),
                                   ps[0:1, 2 + 2 * s:4 + 2 * s, :], ACT.Copy).then_inc(mod_moved, 1)
                act.wait_ge(rope_step, 10)
                act.activation(k.sin[:, :], ang[:, :], ACT.Sin).then_inc(rope_sine, 1)
                act.activation(k.cos[:, :], turns[:, :], ACT.Sin, bias=half_pi[:, :], scale=-1.0)\
                    .then_inc(rope_sine, 1)
                act.wait_ge(pad_stored, 16)

            @block.tensor
            def _(pe):
                pe.wait_ge(ident_set, 1)
                pe.wait_ge(vec_loaded, 16 * 9)
                pe.transpose(ps[:, 0, 0:V_ROWS], vrow[:, :], k.ident[0:V_ROWS, 0:V_ROWS]).then_inc(vec_turned, 1)
                pe.wait_ge(dw_loaded, 16)
                for c in range(CT):
                    last = pe.transpose(ps[:, 1, c * TAPS:(c + 1) * TAPS], wdw_row[:, c * P:(c + 1) * P],
                                        k.ident[0:TAPS, 0:TAPS])
                last.then_inc(dw_turned, 1)
                pe.wait_ge(c_active, 1)
                for n in range(STEPS):
                    s, f = divmod(n, DT)
                    pe.wait_ge(wada_loaded[n % 4], 16 * (n // 4 + 1))
                    for half in range(2):
                        last = pe.matmul(ps[0:1, 2 + 2 * s + half, :], k.c_act[:, f:f + 1],
                                         wada[:, n % 4, half * T:(half + 1) * T], start=(f == 0), stop=(f == DT - 1))
                    last.then_inc(mod_step, 1)
                for s in range(2):
                    pe.wait_ge(mod_moved, s + 1)
                    for m in range(DT):
                        last = pe.transpose(ps[:, 6 + s, m:m + 1], mod_row[0:1, s, m * P:(m + 1) * P],
                                            k.ident[0:1, 0:1])
                    last.then_inc(mod_summed, 1)

            @block.vector
            def _(dve):
                dve.wait_ge(vec_turned, 1)
                dve.tensor_copy(k.vec[:, 0:V_ROWS], ps[:, 0, 0:V_ROWS]).then_inc(vec_copied, 1)
                dve.wait_ge(dw_turned, 1)
                dve.tensor_copy(k.wdw[:, :, :], ps[:, 1, 0:CT * TAPS].rearrange("p (c j) -> p c j", c=CT))\
                    .then_inc(dw_copied, 1)

                steps = 0

                def rope(ins):
                    nonlocal steps
                    steps += 1
                    ins.then_inc(rope_step, 1)
                    dve.wait_ge(rope_step, steps)

                two_pi = (6.28125, 1014 / 2 ** 19, 2 * math.pi - 6.28125 - 1014 / 2 ** 19)
                dve.wait_ge(pos_loaded, 32)
                rope(dve.tensor_copy(ang[:, :], pos_i[:, :]))
                rope(dve.tensor_scalar(ang[:, :], ang[:, :], const[:, 0:1], None, ALU.mult))
                rope(dve.tensor_scalar(turns[:, :], ang[:, :], 1 / (2 * math.pi), 1.5 * 2 ** 23, ALU.mult, ALU.add))
                rope(dve.tensor_scalar(turns[:, :], turns[:, :], 1.5 * 2 ** 23, None, ALU.subtract))
                for part in two_pi:
                    rope(dve.scalar_tensor_tensor(ang[:, :], turns[:, :], -part, ang[:, :], ALU.mult, ALU.add))
                rope(dve.tensor_scalar(ang[:, :], ang[:, :], 3.1415925, -3.1415925, ALU.min, ALU.max))
                rope(dve.scalar_tensor_tensor(turns[:, :], ang[:, :], -1.0, ang[:, :], ALU.mult, ALU.max))
                rope(dve.tensor_scalar(ang[:, :], ang[:, :], const[:, 1:2], None, ALU.mult))
                dve.wait_ge(x_std, 1)
                dve.reciprocal(k.rstd[:, :], k.rstd[:, :]).then_inc(x_rstd, 1)
                dve.wait_ge(x_rstd, 1)
                for t in range(TT):
                    dve.tensor_scalar(k.tokens[:, t, :], k.tokens[:, t, :], k.rstd[:, t:t + 1], None, ALU.mult)\
                        .then_inc(x_scaled, 1)
                for s in range(2):
                    dve.wait_ge(mod_summed, s + 1)
                    dve.tensor_tensor(k.mod[:, s * DT:(s + 1) * DT], ps[:, 6 + s, 0:DT],
                                      k.vec[:, V_BADA + s * DT:V_BADA + (s + 1) * DT], ALU.add)\
                        .then_inc(mod_done, 1)
                dve.wait_ge(mod_done, 2)
                dve.scalar_tensor_tensor(k.a1[:, :], k.mod[:, SC1:SC1 + DT], 1.0, k.vec[:, V_GMIX:V_GMIX + DT],
                                         ALU.add, ALU.mult).then_inc(mod_done, 1)


def seeded(eng, *sems, by=2):
    for s in sems:
        eng.sem_inc(s, by)


def turn(n):
    return n + 1


def done(n, seed=2):
    return n + 1 + seed


def project(nc, w, k):
    JOBS = QT + KT + 1 + 2 * CT
    ITEMS = 6 + 4 + 4
    LAT = QT + KT
    GLU = LAT + 1
    with ExitStack() as ctx:
        sb, sem = open_tensors(ctx, nc, "project")
        ps = k.ps
        xtok, ss, rstd, wuq, wukv = k.tokens, k.ss, k.rstd, k.wuq, k.wukv
        h = sb("h", [P, DT, 2, T], F32R)
        hb = sb("hb", [P, 2, T])
        raw = sb("raw", [P, 2, DT, P])
        wt = sb("wt", [P, 2, 2, DT, P], F32R)
        lat = sb("lat", [P, LAT + 1, T])
        sq = sb("sq", [P, LAT, T])
        latn = sb("latn", [P, LAT, 2, T], F32R)
        rot = sb("rot", [P, 2, T])
        rb = sb("rb", [P, 2, T])
        kr = sb("kr", [P, 2, T], F32R)
        it = sb("it", [P, 2, T])
        stage = sb("stage", [P, 2, 2 * T], F32R)
        ub = sb("ub", [P, 2, T])
        sig = sb("sig", [P, 2, T])

        x_loaded, x_squared, x_std, x_rstd, x_scaled = k.x_progress
        x_turned, h_hi, h_lo = (sem(n) for n in ("x_turned", "h_hi", "h_lo"))
        raw_loaded = [sem(f"raw_loaded{i}") for i in range(2)]
        w_hi, w_lo, job_done = sem("w_hi"), sem("w_lo"), sem("job_done")
        act_bank_free, turn_bank_free = sem("act_bank_free"), sem("turn_bank_free")
        lat_squared, lat_summed, lat_std, lat_rstd = (sem(n) for n in (
            "lat_squared", "lat_summed", "lat_std", "lat_rstd"))
        lat_normed, lat_hi, lat_lo, kr_step, kr_stored = (sem(n) for n in (
            "lat_normed", "lat_hi", "lat_lo", "kr_step", "kr_stored"))
        u_done = sem("u_done")
        u_stored = [sem(f"u_stored{i}") for i in range(2)]
        item_done, item_copied, item_rot, item_hi, item_lo = (sem(n) for n in (
            "item_done", "item_copied", "item_rot", "item_hi", "item_lo"))
        item_stored = [sem(f"item_stored{i}") for i in range(2)]

        BANK_TURN, BANK_ACT, BANK_DVE, BANK_ITEM = 0, 2, 4, 6
        SUMS_AFTER = 6
        AFTER = {9: range(0, 3), 10: range(3, 6), 11: range(6, 9), 12: range(9, 13), 13: range(13, 14)}
        SWAP = [(i + ROPE // 2) % ROPE for i in range(ROPE)]
        ACT_USES = GLU + CT

        def job_column(j):
            if j < LAT:
                return j * P
            if j == LAT:
                return QL + KVL - NOPE
            c, second = divmod(j - GLU, 2)
            return IN_GLU + (0 if second else CONV) + c * P

        def by_act(j):
            return j < GLU or (j - GLU) % 2 == 0

        def act_use(j):
            return j if j < GLU else GLU + (j - GLU) // 2

        def job_bank(j):
            return BANK_ACT + act_use(j) % 2 if by_act(j) else BANK_DVE + ((j - GLU) // 2) % 2

        def groups(eng, body):
            with eng.Fori(0, GROUPS - 1) as g:
                body(g, False)
            body(GROUPS - 1, True)

        with nc.Block() as block:

            @block.sync
            def _(sp):
                with sp.Fori(0, GROUPS) as g:
                    for j in range(JOBS):
                        sp.wait_ge(w_lo, turn(g * JOBS + j))
                        c = job_column(j)
                        sp.dma_start(raw[:, j % 2], w["w_in"][0].rearrange("(f p) m -> p f m", p=P)[:, :, c:c + P])\
                            .then_inc(raw_loaded[j % 2], 16)

            @block.gpsimd
            def _(pool):
                seeded(pool, w_lo)
                with pool.Fori(0, GROUPS) as g:
                    for j in range(JOBS):
                        pool.wait_ge(w_hi, g * JOBS + j + 1)
                        pool.tensor_tensor(wt[:, j % 2, 1], raw[:, j % 2], wt[:, j % 2, 0].bitcast(F32), ALU.subtract)\
                            .then_inc(w_lo, 1)

            @block.scalar
            def _(act):
                seeded(act, act_bank_free, turn_bank_free, item_copied)

                def load_x(g):
                    act.dma_start(xtok[:, :, :],
                                  w["x"][0].rearrange("(g t p) f -> p g t f", t=TT, p=P)[:, bass.ds(g, 1)]
                                  .rearrange("p g t f -> p (g t) f")).then_inc(x_loaded, 16)

                def x_stats(g):
                    act.wait_ge(x_loaded, (g + 1) * 16)
                    for t in range(TT):
                        act.wait_ge(x_squared, g * TT + t)
                        act.activation(sq[:, 0:2, :].rearrange("p a b -> p (a b)"), xtok[:, t, :], ACT.Square,
                                       accum_out=ss[:, t:t + 1]).then_inc(x_squared, 1)
                    act.wait_ge(x_squared, (g + 1) * TT)
                    act.activation(rstd[:, :], ss[:, :], ACT.Sqrt, bias=k.eps[:, :], scale=1.0 / D)\
                        .then_inc(x_std, 1)

                def hi(n, use, j):
                    act.wait_ge(raw_loaded[j % 2], use * 16)
                    act.wait_ge(job_done, turn(n))
                    act.activation(wt[:, j % 2, 0], raw[:, j % 2], ACT.Copy).then_inc(w_hi, 1)

                def store_item(g, n):
                    act.wait_ge(item_lo, done(g * ITEMS + n))
                    cols = bass.ds(g * T, T)
                    if n < 10:
                        dst = (k.qn_dram[n * P:(n + 1) * P, :, cols] if n < 4 else
                               k.qr_dram[(n - 4) * P:(n - 3) * P, :, cols] if n < 6 else
                               k.kn_dram[(n - 6) * P:(n - 5) * P, :, cols])
                        src = stage[:, n % 2, :].bitcast(F32).rearrange("p (a t) -> p a t", a=2)
                    else:
                        dst = k.v_dram[bass.ds(g * T + (n - 10) * P, P)]
                        src = stage[:, n % 2, :].bitcast(F32)
                    act.dma_start(dst, src).then_inc(item_stored[n % 2], 16)

                def store_u(g, c):
                    act.wait_ge(u_done, done(g * CT + c))
                    act.dma_start(k.u_dram[c * P:(c + 1) * P, bass.ds(g * T + TAPS - 1, T)], ub[:, c % 2])\
                        .then_inc(u_stored[c % 2], 16)

                def body(g, last):
                    for f in range(DT):
                        act.wait_ge(x_turned, g * DT + f + 1)
                        act.wait_ge(h_lo, turn(g * DT + f))
                        act.activation(hb[:, f % 2, :], ps[:, BANK_TURN + f % 2, :], ACT.Identity,
                                       bias=k.mod[:, SH1 + f:SH1 + f + 1], scale=k.a1[:, f:f + 1])\
                            .then_inc(turn_bank_free, 1)
                    if not last:
                        load_x(g + 1)
                    pending = []
                    for j in range(JOBS):
                        if j + 2 < JOBS:
                            hi(g * JOBS + j + 2, g * (JOBS // 2) + j // 2 + 2, j)
                        elif not last:
                            hi(g * JOBS + j + 2, g * (JOBS // 2) + j // 2 + 2, j)
                        act.wait_ge(job_done, done(g * JOBS + j))
                        if j < GLU:
                            act.wait_ge(kr_step, 1 + g * 6)
                            if j < LAT:
                                act.wait_ge(lat_lo, 1 + g * LAT)
                            act.activation(lat[:, j, :], ps[:, job_bank(j), :], ACT.Copy).then_inc(act_bank_free, 1)
                            if j < LAT:
                                act.wait_ge(act_bank_free, done(g * (ACT_USES) + j))
                                act.activation(sq[:, j, :], lat[:, j, :], ACT.Square).then_inc(lat_squared, 1)
                        elif by_act(j):
                            c = (j - GLU) // 2
                            act.wait_ge(u_done, turn(g * CT + c))
                            act.activation(sig[:, c % 2, :], ps[:, job_bank(j), :], ACT.Sigmoid)\
                                .then_inc(act_bank_free, 1)
                        else:
                            store_u(g, (j - GLU) // 2)
                        if j == SUMS_AFTER:
                            for i, width in enumerate((QL, KVL)):
                                act.wait_ge(lat_summed, g * 2 + i + 1)
                                act.wait_ge(lat_lo, 1 + g * LAT)
                                act.activation(rb[:, i, :], ps[:, BANK_TURN + i, :], ACT.Sqrt, bias=k.eps[:, :],
                                               scale=1.0 / width).then_inc(turn_bank_free, 1)
                            act.wait_ge(kr_step, 1 + g * 6 + 6)
                            act.dma_start(k.kr_dram[:, :, bass.ds(g * T, T)], kr[NOPE:QK].bitcast(F32)).then_inc(kr_stored, 16)
                            if not last:
                                x_stats(g + 1)
                        for n in AFTER.get(j, ()):
                            num = g * ITEMS + n
                            act.wait_ge(item_done, num + 1)
                            act.wait_ge(item_lo, turn(num))
                            act.activation(it[:, n % 2, :], ps[:, BANK_ITEM + n % 2, :], ACT.Copy)\
                                .then_inc(item_copied, 1)
                            pending.append(n)
                            if len(pending) > 1:
                                store_item(g, pending.pop(0))
                    store_item(g, pending.pop(0))

                for j in range(2):
                    hi(j, 1, j)
                groups(act, body)
                for i in range(2):
                    act.wait_ge(item_stored[i], 16 * (1 + GROUPS * ITEMS // 2))
                    act.wait_ge(u_stored[i], 16 * (1 + GROUPS * CT // 2))
                act.wait_ge(kr_stored, 16 * (1 + GROUPS))

            @block.tensor
            def _(pe):
                seeded(pe, job_done)

                def body(g, last):
                    pe.wait_ge(x_scaled, (g + 1) * TT)
                    for f in range(DT):
                        pe.wait_ge(turn_bank_free, turn(g * (DT + 2) + f))
                        for t in range(TT):
                            ins = pe.transpose(ps[:, BANK_TURN + f % 2, t * P:(t + 1) * P],
                                               xtok[:, t, f * P:(f + 1) * P], k.ident[:, :])
                        ins.then_inc(x_turned, 1)
                    for j in range(JOBS):
                        pe.wait_ge(w_lo, done(g * JOBS + j))
                        if by_act(j):
                            pe.wait_ge(act_bank_free, turn(g * ACT_USES + act_use(j)))
                        else:
                            pe.wait_ge(u_done, turn(g * CT + (j - GLU) // 2))
                        for f in range(DT):
                            if j == 0:
                                pe.wait_ge(h_lo, done(g * DT + f))
                            for s, m in ((0, 0), (0, 1), (1, 0)):
                                ins = pe.matmul(ps[:, job_bank(j), :], wt[:, j % 2, s, f, :], h[:, f, m, :],
                                                start=(f == 0 and s == m == 0), stop=(f == DT - 1 and s == 1))
                        ins.then_inc(job_done, 1)
                        if j == SUMS_AFTER:
                            for i, tiles in enumerate((range(QT), range(QT, LAT))):
                                pe.wait_ge(lat_squared, g * LAT + tiles[-1] + 1)
                                pe.wait_ge(turn_bank_free, turn(g * (DT + 2) + DT + i))
                                for f in tiles:
                                    ins = pe.matmul(ps[:, BANK_TURN + i, :], k.ones[:, :], sq[:, f, :],
                                                    start=(f == tiles[0]), stop=(f == tiles[-1]))
                                ins.then_inc(lat_summed, 1)
                        for n in AFTER.get(j, ()):
                            item(g, n)

                def item(g, n):
                    pe.wait_ge(item_copied, turn(g * ITEMS + n))
                    pe.wait_ge(lat_lo, 1 + g * LAT + (QT if n < 6 else LAT))
                    out = ps[:, BANK_ITEM + n % 2, :]
                    tiles = range(QT) if n < 6 else range(KT)
                    for f in tiles:
                        for s, m in ((0, 0), (0, 1), (1, 0)):
                            if n < 6:
                                lhs, rhs = wuq[:, f, s, n * P:(n + 1) * P], latn[:, f, m, :]
                            elif n < 10:
                                lhs, rhs = wukv[:, f, s, (n - 6) * P:(n - 5) * P], latn[:, QT + f, m, :]
                            else:
                                lhs = latn[:, QT + f, s, (n - 10) * P:(n - 9) * P]
                                rhs = wukv[:, f, m, HEADS * NOPE:]
                            ins = pe.matmul(out, lhs, rhs, start=(f == 0 and s == m == 0),
                                            stop=(f == tiles[-1] and s == 1))
                    ins.then_inc(item_done, 1)

                groups(pe, body)

            @block.vector
            def _(dve):
                seeded(dve, h_lo, u_done, item_lo)
                seeded(dve, kr_step, lat_lo, by=1)
                seeded(dve, *u_stored, *item_stored, kr_stored, by=16)

                def scale_x(g):
                    dve.wait_ge(x_std, g + 1)
                    dve.reciprocal(rstd[:, :], rstd[:, :]).then_inc(x_rstd, 1)
                    dve.wait_ge(x_rstd, g + 1)
                    for t in range(TT):
                        dve.tensor_scalar(xtok[:, t, :], xtok[:, t, :], rstd[:, t:t + 1], None, ALU.mult)\
                            .then_inc(x_scaled, 1)

                def latents(g):
                    for i in range(2):
                        dve.wait_ge(turn_bank_free, done(g * (DT + 2) + DT + i))
                        dve.reciprocal(rb[:, i, :], rb[:, i, :]).then_inc(lat_rstd, 1)
                    for f in range(LAT):
                        dve.wait_ge(lat_rstd, g * 2 + (1 if f < QT else 2))
                        dve.scalar_tensor_tensor(lat[:, f, :], lat[:, f, :], k.vec[:, V_GQ + f:V_GQ + f + 1],
                                                 rb[:, 0 if f < QT else 1, :], ALU.mult, ALU.mult)\
                            .then_inc(lat_normed, 1)
                        dve.wait_ge(lat_normed, g * LAT + f + 1)
                        dve.tensor_copy(latn[:, f, 0, :], lat[:, f, :]).then_inc(lat_hi, 1)
                        dve.wait_ge(lat_hi, g * LAT + f + 1)
                        dve.tensor_tensor(latn[:, f, 1, :], lat[:, f, :], latn[:, f, 0, :].bitcast(F32), ALU.subtract)\
                            .then_inc(lat_lo, 1)

                def rotate(t, tmp, part, sem_, base):
                    cos, sin = k.cos[part, g_cols[0]], k.sin[part, g_cols[0]]
                    scaled, swapped = tmp
                    dve.tensor_tensor(scaled, t, cos, ALU.mult).then_inc(sem_, 1)
                    dve.stream_shuffle(swapped, t, SWAP).then_inc(sem_, 1)
                    dve.wait_ge(sem_, base + 2)
                    dve.tensor_tensor(swapped, swapped, sin, ALU.mult).then_inc(sem_, 1)
                    dve.wait_ge(sem_, base + 3)
                    dve.tensor_tensor(t, scaled, swapped, ALU.add).then_inc(sem_, 1)
                    dve.wait_ge(sem_, base + 4)

                g_cols = [None]

                def body(g, last):
                    g_cols[0] = bass.ds(g * T, T)
                    for f in range(DT):
                        dve.wait_ge(turn_bank_free, done(g * (DT + 2) + f))
                        dve.tensor_copy(h[:, f, 0, :], hb[:, f % 2, :]).then_inc(h_hi, 1)
                        dve.wait_ge(h_hi, g * DT + f + 1)
                        dve.tensor_tensor(h[:, f, 1, :], hb[:, f % 2, :], h[:, f, 0, :].bitcast(F32), ALU.subtract)\
                            .then_inc(h_lo, 1)
                    for j in range(JOBS):
                        if j == LAT:
                            dve.wait_ge(act_bank_free, done(g * ACT_USES + LAT))
                            dve.wait_ge(kr_stored, 16 * (1 + g))
                            t = lat[NOPE:QK, LAT, :]
                            rotate(t, (rot[NOPE:QK, 0, :], rot[NOPE:QK, 1, :]), slice(NOPE, QK), kr_step, 1 + g * 6)
                            dve.tensor_copy(kr[NOPE:QK, 0, :], t).then_inc(kr_step, 1)
                            dve.wait_ge(kr_step, 1 + g * 6 + 5)
                            dve.tensor_tensor(kr[NOPE:QK, 1, :], t, kr[NOPE:QK, 0, :].bitcast(F32), ALU.subtract)\
                                .then_inc(kr_step, 1)
                        if not by_act(j):
                            c = (j - GLU) // 2
                            dve.wait_ge(act_bank_free, done(g * ACT_USES + act_use(j - 1)))
                            dve.wait_ge(job_done, done(g * JOBS + j))
                            dve.wait_ge(u_stored[c % 2], 16 * (g * (CT // 2) + c // 2 + 1))
                            dve.tensor_tensor(ub[:, c % 2, :], ps[:, job_bank(j), :], sig[:, c % 2, :], ALU.mult)\
                                .then_inc(u_done, 1)
                        if j == SUMS_AFTER + 1:
                            latents(g)
                            if not last:
                                scale_x(g + 1)
                        for n in AFTER.get(j, ()):
                            num = g * ITEMS + n
                            dve.wait_ge(item_copied, done(num))
                            t = it[:, n % 2, :]
                            if n in (4, 5):
                                rotate(t, (rot[:, 0, :], rot[:, 1, :]), slice(0, P), item_rot, g * 8 + (n - 4) * 4)
                            dve.wait_ge(item_stored[n % 2], 16 * (g * (ITEMS // 2) + n // 2 + 1))
                            if n < 10:
                                st = stage[:, n % 2, :].rearrange("p (a t) -> p a t", a=2)
                                parts = st[:, 0, :], st[:, 1, :]
                            else:
                                st = stage[:, n % 2, :].rearrange("p (h a e) -> p h a e", h=HEADS, a=2)
                                parts = st[:, :, 0, :], st[:, :, 1, :]
                                t = t.rearrange("p (h e) -> p h e", h=HEADS)
                            dve.tensor_copy(parts[0], t).then_inc(item_hi, 1)
                            dve.wait_ge(item_hi, num + 1)
                            dve.tensor_tensor(parts[1], t, parts[0].bitcast(F32), ALU.subtract).then_inc(item_lo, 1)

                groups(dve, body)


def attend(nc, w, k):
    NG = SEQ // T
    CHUNKS = TT * NG * (NG + 1) // 2
    UNITS = CHUNKS
    BLOCKS = SEQ // P
    STEPS = 4
    AHEAD = 20
    upto = [TT * n * (n + 1) // 2 for n in range(NG + 1)]
    SCALE = float(QK) ** -0.5
    with ExitStack() as ctx:
        sb, sem = open_tensors(ctx, nc, "attend")
        ps = k.ps
        key = sb("key", [P, 2, 2, SEQ], F32R)
        qry = sb("qry", [P, 2, 2, SEQ], F32R)
        val = sb("val", [P, 2, BLOCKS, 2 * VD], F32R)
        prob = sb("prob", [P, STEPS, T])
        pt = sb("pt", [P, STEPS, 2, T], F32R)
        total = sb("total", [P, 2, T])
        zero = sb("zero", [P, T])
        rows = sb("rows", [P, 2, SEQ])
        eye = sb("eye", [P, P], F32R)
        mask, mask_t = sb("mask", [P, P], F32R), sb("mask_t", [P, P], F32R)
        mask_f = sb("mask_f", [P, 2, P])
        cmax, bmax = sb("cmax", [P, TT, NG]), sb("bmax", [P, TT])
        nmax = sb("nmax", [P, TT, P])
        rsum = sb("rsum", [P, TT])
        diag = sb("diag", [P, TT, P])
        ss, rstd, squares = sb("ss", [P, TT]), sb("rstd", [P, TT]), sb("squares", [P, D])
        ot = sb("ot", [VD, T])
        of = sb("of", [VD, T])
        ostage = sb("ostage", [VD, 2, 2, T], F32R)
        wada = sb("wada", [P, 2, D])
        part, acc = sb("part", [P, D]), sb("acc", [P, D])

        x_loaded, x_squared, x_std, x_rstd, x_scaled = k.late_x_progress
        first_loaded = sem("first_loaded")
        rope_loaded, const_cleared, const_made, consts_set = (
            sem(n) for n in ("rope_loaded", "const_cleared", "const_made", "consts_set"))
        head_loaded, val_loaded = ([sem(f"{n}_loaded{i}") for i in range(2)] for n in ("head", "val"))
        chunk_done, chunk_max, block_max, max_negated = (
            sem(n) for n in ("chunk_done", "chunk_max", "block_max", "max_negated"))
        row_turned, row_hi, row_lo = sem("row_turned"), sem("row_hi"), sem("row_lo")
        score_done, exp_done, prob_hi, prob_lo, prob_summed, unit_done = (sem(n) for n in (
            "score_done", "exp_done", "prob_hi", "prob_lo", "prob_summed", "unit_done"))
        sums_done, recip_done, diag_done, spread_done = (
            sem(n) for n in ("sums_done", "recip_done", "diag_done", "spread_done"))
        out_moved, out_summed, out_scaled, out_hi, out_lo = (
            sem(n) for n in ("out_moved", "out_summed", "out_scaled", "out_hi", "out_lo"))
        out_stored = [sem(f"out_stored{i}") for i in range(2)]
        wada2_loaded = [sem(f"wada2_loaded{i}") for i in range(2)]
        prod_done, acc_done, acc_summed, mod_added = (sem(n) for n in (
            "prod_done", "acc_done", "acc_summed", "mod_added"))

        BANK_CHUNK, BANK_SCORE, BANK_OUT, BANK_ROW, BANK_SUM = 0, 2, 4, 6, 7

        def chunk_base(n):
            return n // NG * CHUNKS + upto[n % NG]

        def maxima(after):
            slots = {}
            for n in range(after):
                for i in range(TT * (n % NG + 1)):
                    at = chunk_base(n) + i - AHEAD
                    slots.setdefault(at, []).append(("chunk", n, i // (n % NG + 1), i % (n % NG + 1)))
                slots.setdefault(at, []).append(("combine", n))
                slots.setdefault(at + 1, []).append(("row", n))
            return slots

        def events(s, first, last):
            at = {u: n for n in range(NG) for u in range(upto[n], upto[n + 1])}
            at[-2] = at[-1] = -1
            slots = maxima(NG if last else 2 * NG)
            if first:
                for u in range(-AHEAD, 0):
                    yield from slots.get(u, ())
            for u in range(UNITS + (2 if last else 0)):
                if u <= UNITS and not (first and u == 0):
                    yield ("split", at[u - 1], u - 1)
                if u < UNITS:
                    yield ("score", at[u], u)
                some = slots.get(u, [])
                yield from some
                if not (first and u < 2):
                    yield ("product", at[u - 2], u - 2)
                if s == 0 and u % 4 == 0 and u // 4 < DT:
                    yield ("mod_load", u // 4)
                if first and u < 2:
                    continue
                n = at[u - 2]
                if u - 2 == upto[n] and not (first and n == 0):
                    yield ("sums", n - 1)
                if u - 3 == upto[n] and not (first and n == 0):
                    yield ("out", n - 1)
                if s == 0 and u % 4 == 3 and 0 < u // 4 <= DT:
                    yield ("mod_step", u // 4 - 1)
                if s == 1 and u == 8:
                    yield ("mod",)
            if last:
                yield ("sums", NG - 1)
                yield ("out", NG - 1)

        def with_order(order):
            row, out = None, None
            ordered = []
            for event in order:
                if event[0] == "row":
                    ordered.append(event + (out,))
                    row = event[1]
                elif event[0] == "out":
                    ordered.append(event + (row,))
                    out = event[1]
                else:
                    ordered.append(event)
            return ordered

        def heads(eng, body):
            body(0, 0, 0, with_order(events(0, True, False)), False)
            body(0, 1, 1, with_order(events(1, False, False)), False)
            with eng.Fori(1, HEADS // 2 - 1) as pair:
                for s in range(2):
                    body(pair, s, pair * 2 + s, with_order(events(s, False, False)), False)
            last = HEADS // 2 - 1
            body(last, 0, HEADS - 2, with_order(events(0, False, False)), False)
            body(last, 1, HEADS - 1, with_order(events(1, False, True)), True)

        def first_head(head):
            return isinstance(head, int) and head == 0

        rows_of_head = [e[1] for e in events(0, False, False) if e[0] == "row"]
        last_row = rows_of_head[-1] - NG
        last_out = NG - 2 - NG

        def width(n, b, c):
            return T if c < n % NG else (b + 1) * P

        def first_query(n, kb):
            return max(0, kb - TT * n) * P

        def place(s, n):
            return (s if 0 <= n < NG else 1 - s), n % NG

        def unit(n, u):
            kb = u - upto[n] if n >= 0 else u + TT * NG
            return kb, first_query(n % NG, kb), kb == TT * (n % NG + 1) - 1

        with nc.Block() as block:

            @block.sync
            def _(sp):
                for s in range(2):
                    sp.dma_start(key[NOPE:QK, s].bitcast(F32), k.kr_dram).then_inc(rope_loaded, 16)

                def load_head(head, s):
                    sp.wait_ge(out_summed, head * NG + NG)
                    rows_n, rows_r = bass.ds(head * NOPE, NOPE), bass.ds(head * ROPE, ROPE)
                    parts = [(slice(0, SEQ), head_loaded[s])]
                    if first_head(head):
                        parts = [(slice(0, T), first_loaded), (slice(T, SEQ), head_loaded[s])]
                    for cols, loaded in parts:
                        sp.dma_start(key[0:NOPE, s, :, cols].bitcast(F32), k.kn_dram[rows_n, :, cols])\
                            .then_inc(loaded, 16)
                        sp.dma_start(qry[0:NOPE, s, :, cols].bitcast(F32), k.qn_dram[rows_n, :, cols])\
                            .then_inc(loaded, 16)
                        sp.dma_start(qry[NOPE:QK, s, :, cols].bitcast(F32), k.qr_dram[rows_r, :, cols])\
                            .then_inc(loaded, 16)
                    sp.dma_start(val[:, s].bitcast(F32), k.v_dram.rearrange("(b p) c -> p b c", p=P)
                                 [:, :, bass.ds(head * 2 * VD, 2 * VD)])\
                        .then_inc(val_loaded[s], 16)

                load_head(0, 0)
                load_head(1, 1)
                sp.dma_start(k.xtok[:, :, :], w["x"][0, 0:T].rearrange("(t p) f -> p t f", p=P)).then_inc(x_loaded, 16)
                with sp.Fori(1, HEADS // 2) as pair:
                    for s in range(2):
                        load_head(pair * 2 + s, s)

            @block.gpsimd
            def _(pool):
                seeded(pool, acc_done)
                seeded(pool, prob_summed, by=STEPS)
                pool.memset(mask_f[:, :, :], 0.0).then_inc(const_cleared, 1)
                pool.memset(zero[:, :], 0.0).then_inc(const_cleared, 1)
                pool.memset(nmax[:, :, :], 0.0).then_inc(const_cleared, 1)
                pool.memset(rows[:, 0, :], 1.0).then_inc(const_cleared, 1)
                pool.memset(rows[:, 1, :], 0.0).then_inc(const_cleared, 1)
                pool.wait_ge(const_cleared, 5)
                for i, sign in ((0, -1), (1, 1)):
                    pool.affine_select(out=mask_f[:, i, :], in_=mask_f[:, i, :], compare_op=ALU.is_ge, fill=-1e30,
                                       base=0, pattern=[[sign, P]], channel_multiplier=-sign).then_inc(const_made, 1)

                def body(pair, s, head, order, last):
                    for kind, *what in order:
                        if kind == "split":
                            n, u = what
                            kb, q0, _ = unit(n, u)
                            num = head * UNITS + u
                            pool.wait_ge(exp_done, done(num))
                            if kb == 0:
                                pool.wait_ge(sums_done, head * NG + n + 1)
                            else:
                                pool.wait_ge(prob_summed, done(num - 1, STEPS))
                            dst = total[:, n % 2, q0:]
                            pool.tensor_tensor(dst, prob[:, u % STEPS, q0:], zero[:, q0:] if kb == 0 else dst, ALU.add)\
                                .then_inc(prob_summed, 1)
                        elif kind == "mod_step":
                            f, = what
                            num = pair * DT + f
                            pool.wait_ge(prod_done, done(num))
                            if f:
                                pool.wait_ge(acc_done, done(num - 1))
                                pool.tensor_tensor(acc[:, :], acc[:, :], part[:, :], ALU.add).then_inc(acc_done, 1)
                            else:
                                pool.sem_inc(acc_done, 1)

                heads(pool, body)

            @block.scalar
            def _(act):
                seeded(act, exp_done, prod_done)
                act.activation(eye[:, :], k.ident[:, :], ACT.Copy).then_inc(consts_set, 1)
                act.wait_ge(const_made, 2)
                act.activation(mask[:, :], mask_f[:, 0, :], ACT.Copy).then_inc(consts_set, 1)
                act.activation(mask_t[:, :], mask_f[:, 1, :], ACT.Copy).then_inc(consts_set, 1)
                for s in range(2):
                    for i in range(2):
                        act.activation(key[QK:QK + 1, s, i, :], rows[QK:QK + 1, i, :], ACT.Copy).then_inc(consts_set, 1)

                def x_stats():
                    act.wait_ge(x_loaded, 16)
                    for t in range(TT):
                        if t:
                            act.wait_ge(x_squared, t)
                        act.activation(squares[:, :], k.xtok[:, t, :], ACT.Square, accum_out=ss[:, t:t + 1])\
                            .then_inc(x_squared, 1)
                    act.wait_ge(x_squared, TT)
                    act.activation(rstd[:, :], ss[:, :], ACT.Sqrt, bias=k.eps[:, :], scale=1.0 / D).then_inc(x_std, 1)

                def store(head, n):
                    row = head * VD if n >= 0 else (head - 1) * VD
                    n0 = n % NG
                    act.wait_ge(out_lo, done(head * NG + n, 1))
                    act.dma_start(k.attn_dram[bass.ds(row, VD), :, n0 * T:(n0 + 1) * T],
                                  ostage[:, n % 2].bitcast(F32)).then_inc(out_stored[n % 2], 16)

                def body(pair, s, head, order, last):
                    unstored = None
                    for kind, *what in order:
                        if kind == "score":
                            n, u = what
                            num = head * UNITS + u
                            kb, q0, _ = unit(n, u)
                            act.wait_ge(score_done, num + 1)
                            act.wait_ge(prob_summed, turn(num))
                            act.wait_ge(prob_lo, turn(num))
                            act.activation(prob[:, u % STEPS, q0:], ps[:, BANK_SCORE + u % 2, q0:], ACT.Exp,
                                           scale=SCALE).then_inc(exp_done, 1)
                        elif kind == "split":
                            n, u = what
                            num = head * UNITS + u
                            kb, q0, _ = unit(n, u)
                            if last and u == 26:
                                x_stats()
                            act.wait_ge(exp_done, done(num))
                            act.wait_ge(unit_done, turn(num))
                            act.activation(pt[:, u % STEPS, 0, q0:], prob[:, u % STEPS, q0:], ACT.Copy)\
                                .then_inc(prob_hi, 1)
                        elif kind == "row":
                            n, _ = what
                            buf, n0 = place(s, n)
                            act.wait_ge(row_turned, done(head * NG + n, 1))
                            act.activation(qry[QK:QK + 1, buf, 0, n0 * T:(n0 + 1) * T], ps[QK:QK + 1, BANK_ROW, :],
                                           ACT.Copy).then_inc(row_hi, 1)
                            if unstored is not None:
                                store(head, unstored)
                                unstored = None
                        elif kind == "sums":
                            n, = what
                            buf, n0 = place(s, n)
                            act.wait_ge(unit_done, done(head * UNITS + (upto[n + 1] if n >= 0 else 0) - 1, STEPS))
                            act.wait_ge(out_summed, head * NG + n + 8)
                            act.activation(ot[:, :], ps[VD:P, BANK_OUT + n % 2, :], ACT.Copy).then_inc(out_moved, 1)
                        elif kind == "out":
                            if unstored is not None:
                                store(head, unstored)
                            unstored = what[0]
                        elif kind == "mod_load":
                            f, = what
                            act.wait_ge(prod_done, done(pair * DT + f - 2))
                            act.dma_start(wada[:, f % 2],
                                          w["w_ada"][0, f * P:(f + 1) * P, bass.ds((pair + 2) * D, D)])\
                                .then_inc(wada2_loaded[f % 2], 16)
                        elif kind == "mod_step":
                            f, = what
                            num = pair * DT + f
                            act.wait_ge(wada2_loaded[f % 2], 16 * (pair * (DT // 2) + f // 2 + 1))
                            act.wait_ge(acc_done, done(num - 1))
                            act.wait_ge(acc_summed, 1 + pair)
                            act.activation((part if f else acc)[:, :], wada[:, f % 2], ACT.Identity,
                                           scale=k.c_act[:, f:f + 1]).then_inc(prod_done, 1)
                    if unstored is not None:
                        store(head, unstored)

                heads(act, body)
                for i in range(2):
                    act.wait_ge(out_stored[i], 16 * (1 + HEADS * NG // 2))

            @block.tensor
            def _(pe):
                seeded(pe, unit_done, by=STEPS)
                seeded(pe, sums_done)
                seeded(pe, acc_summed, row_turned, spread_done, by=1)
                pe.wait_ge(consts_set, 7)
                pe.wait_ge(rope_loaded, 32)

                def body(pair, s, head, order, last):
                    for kind, *what in order:
                        if kind == "chunk":
                            n, b, c = what
                            buf, n0 = place(s, n)
                            if first_head(head) and n == 1 and b == 0:
                                pe.wait_ge(head_loaded[0], 48)
                            if n == NG and b == 0:
                                pe.wait_ge(head_loaded[buf], 48 * (pair + 1 + s))
                            i = n0 * TT + b
                            wd = width(n, b, c)
                            at = chunk_base(n) + b * (n0 + 1) + c
                            bank = BANK_CHUNK + at % 2
                            pe.wait_ge(chunk_max, turn(head * CHUNKS + at))
                            for q, m in ((0, 0), (0, 1), (1, 0)):
                                ins = pe.matmul(ps[:, bank, 0:wd], qry[0:QK, buf, q, i * P:(i + 1) * P],
                                                key[0:QK, buf, m, c * T:c * T + wd], start=(q == m == 0),
                                                stop=(q == 1 and c < n0))
                            if c == n0:
                                ins = pe.matmul(ps[:, bank, wd - P:wd], eye[:, :], mask[:, :], start=False, stop=True)
                            ins.then_inc(chunk_done, 1)
                        elif kind == "row":
                            n, out = what
                            pe.wait_ge(max_negated, head * NG + n + 1)
                            if out is None:
                                out = last_out
                            pe.wait_ge(out_scaled, done(head * NG + out))
                            for b in range(TT):
                                ins = pe.transpose(ps[:, BANK_ROW, b * P:(b + 1) * P], nmax[:, b, :], k.ident[:, :])
                            ins.then_inc(row_turned, 1)
                        elif kind == "score":
                            n, u = what
                            kb, q0, _ = unit(n, u)
                            diagonal = kb >= TT * n
                            bank = BANK_SCORE + u % 2
                            if kb == 0:
                                pe.wait_ge(row_lo, head * NG + n + 1)
                            pe.wait_ge(exp_done, turn(head * UNITS + u))
                            for q, m in ((0, 0), (0, 1), (1, 0)):
                                ins = pe.matmul(ps[:, bank, q0:], key[0:QK + 1, s, q, kb * P:(kb + 1) * P],
                                                qry[0:QK + 1, s, m, n * T + q0:(n + 1) * T], start=(q == m == 0),
                                                stop=(q == 1 and not diagonal))
                            if diagonal:
                                ins = pe.matmul(ps[:, bank, q0:q0 + P], eye[:, :], mask_t[:, :], start=False, stop=True)
                            ins.then_inc(score_done, 1)
                        elif kind == "product":
                            n, u = what
                            buf, n0 = place(s, n)
                            kb, q0, final = unit(n, u)
                            if u == 0:
                                pe.wait_ge(val_loaded[s], 16 * (pair + 1))
                            if kb == 0:
                                pe.wait_ge(out_summed, head * NG + n + 7)
                            pe.wait_ge(prob_lo, done(head * UNITS + u, STEPS))
                            for m in range(2):
                                ins = pe.matmul(ps[:, BANK_OUT + n % 2, q0:], val[:, buf, kb, :],
                                                pt[:, u % STEPS, m, q0:], start=(kb == 0 and m == 0),
                                                stop=(final and m == 1))
                            ins.then_inc(unit_done, 1)
                        elif kind == "sums":
                            n, = what
                            end = upto[n + 1] if n >= 0 else 0
                            pe.wait_ge(prob_summed, done(head * UNITS + end - 1, STEPS))
                            pe.wait_ge(recip_done, done(head * NG + n - 1, 1))
                            pe.wait_ge(mod_added, pair + (1 if s == 0 or n < 0 or n == 0 else 2))
                            for b in range(TT):
                                ins = pe.matmul(ps[:, BANK_SUM, b:b + 1], total[:, n % 2, b * P:(b + 1) * P],
                                                k.ones[:, 0:1], start=True, stop=True)
                            ins.then_inc(sums_done, 1)
                        elif kind == "out":
                            n, row = what
                            pe.wait_ge(diag_done, TT * (head * NG + n + 1))
                            pe.wait_ge(row_lo, head * NG + (last_row if row is None else row) + 1)
                            pe.matmul(ps[0:VD, BANK_ROW, :], k.ones[:, 0:VD], diag[:, :, :].rearrange("p b q -> p (b q)"),
                                      start=True, stop=True).then_inc(spread_done, 1)
                        elif kind == "mod":
                            pe.wait_ge(acc_done, done(pair * DT + DT - 1))
                            pe.wait_ge(recip_done, done(head * NG, 1))
                            for m in range(DT):
                                ins = pe.matmul(ps[:, BANK_SUM, m:m + 1], acc[:, m * P:(m + 1) * P], k.ones[:, 0:1],
                                                start=True, stop=True)
                            ins.then_inc(acc_summed, 1)

                pe.wait_ge(first_loaded, 48)
                heads(pe, body)

            @block.vector
            def _(dve):
                seeded(dve, out_summed, by=8)
                seeded(dve, chunk_max, out_scaled)
                seeded(dve, prob_lo, by=STEPS)
                seeded(dve, mod_added, recip_done, out_lo, by=1)
                seeded(dve, *out_stored, by=16)
                dve.wait_ge(const_cleared, 5)

                def scale_x():
                    dve.wait_ge(x_std, 1)
                    dve.reciprocal(rstd[:, :], rstd[:, :]).then_inc(x_rstd, 1)
                    dve.wait_ge(x_rstd, 1)
                    for t in range(TT):
                        dve.tensor_scalar(k.xn[:, t, :], k.xtok[:, t, :], rstd[:, t:t + 1], None, ALU.mult)\
                            .then_inc(x_scaled, 1)

                def body(pair, s, head, order, last):
                    for kind, *what in order:
                        if kind == "chunk":
                            n, b, c = what
                            at = chunk_base(n) + b * (n % NG + 1) + c
                            wd = width(n, b, c)
                            dve.wait_ge(chunk_done, head * CHUNKS + at + 1)
                            dve.reduce_max(cmax[:, b, c:c + 1], ps[:, BANK_CHUNK + at % 2, 0:wd], AX_X)\
                                .then_inc(chunk_max, 1)
                        elif kind == "combine":
                            n, = what
                            dve.wait_ge(chunk_max, done(head * CHUNKS + chunk_base(n) + TT * (n % NG + 1) - 1))
                            dve.wait_ge(row_turned, head * NG + n + 1)
                            dve.reduce_max(bmax[:, :], cmax[:, :, 0:n % NG + 1], AX_X).then_inc(block_max, 1)
                            dve.wait_ge(block_max, head * NG + n + 1)
                            dve.tensor_scalar(nmax[:, :, QK], bmax[:, :], -1.0, None, ALU.mult).then_inc(max_negated, 1)
                        elif kind == "row":
                            n, _ = what
                            buf, n0 = place(s, n)
                            cols = slice(n0 * T, (n0 + 1) * T)
                            dve.wait_ge(row_hi, head * NG + n + 1)
                            dve.tensor_tensor(qry[QK:QK + 1, buf, 1, cols], ps[QK:QK + 1, BANK_ROW, :],
                                              qry[QK:QK + 1, buf, 0, cols].bitcast(F32), ALU.subtract)\
                                .then_inc(row_lo, 1)
                        elif kind == "split":
                            n, u = what
                            num = head * UNITS + u
                            _, q0, _ = unit(n, u)
                            if last and u == 32:
                                scale_x()
                            dve.wait_ge(prob_hi, num + 1)
                            dve.tensor_tensor(pt[:, u % STEPS, 1, q0:], prob[:, u % STEPS, q0:],
                                              pt[:, u % STEPS, 0, q0:].bitcast(F32), ALU.subtract).then_inc(prob_lo, 1)
                        elif kind == "sums":
                            n, = what
                            num = head * NG + n
                            dve.wait_ge(sums_done, done(num))
                            dve.wait_ge(spread_done, num + 1)
                            dve.reciprocal(rsum[:, :], ps[:, BANK_SUM, 0:TT]).then_inc(recip_done, 1)
                            dve.wait_ge(recip_done, done(num, 1))
                            for b in range(TT):
                                dve.tensor_scalar(diag[:, b, :], k.ident[:, :], rsum[:, b:b + 1], None, ALU.mult)\
                                    .then_inc(diag_done, 1)
                        elif kind == "out":
                            n, _ = what
                            num = head * NG + n
                            dve.wait_ge(out_moved, num + 1)
                            dve.wait_ge(out_lo, num + 1)
                            dve.tensor_tensor(of[:, :], ps[0:VD, BANK_OUT + n % 2, :], ot[:, :], ALU.add)\
                                .then_inc(out_summed, 1)
                            dve.wait_ge(out_summed, num + 1 + 8)
                            dve.wait_ge(spread_done, done(num, 1))
                            dve.tensor_tensor(of[:, :], of[:, :], ps[0:VD, BANK_ROW, :], ALU.mult).then_inc(out_scaled, 1)
                            dve.wait_ge(out_scaled, done(num))
                            dve.wait_ge(out_stored[n % 2], 16 * (head * (NG // 2) + n // 2 + 1))
                            dve.tensor_copy(ostage[:, n % 2, 0, :], of[:, :]).then_inc(out_hi, 1)
                            dve.wait_ge(out_hi, num + 1)
                            dve.tensor_tensor(ostage[:, n % 2, 1, :], of[:, :], ostage[:, n % 2, 0, :].bitcast(F32),
                                              ALU.subtract).then_inc(out_lo, 1)
                        elif kind == "mod":
                            dve.wait_ge(acc_summed, 1 + pair + 1)
                            cols = bass.ds((pair + 2) * DT, DT)
                            dve.tensor_tensor(k.mod[:, cols], ps[:, BANK_SUM, 0:DT], k.vec[:, cols], ALU.add)\
                                .then_inc(mod_added, 1)

                heads(dve, body)


def mix(nc, w, k, out):
    PARTS = ((0, 12), (12, 10))
    assert sum(n for _, n in PARTS) == HT
    GATES, MERGE, OUT = 2 * DT, DT, DT
    BASE = {"gates": 0, "merge": GATES, "out": GATES + MERGE}
    n = GATES + MERGE + OUT
    for i, (_, tiles) in enumerate(PARTS):
        BASE["up", i] = n
        BASE["down", i] = n + 2 * tiles
        n += 2 * tiles + 2 * DT
    JOBS = n
    ACT_BASE = {"gates": 0, ("up", 0): GATES, ("up", 1): GATES + PARTS[0][1]}
    ACT_USES = GATES + HT
    DVE_BASE = {"turn": 0, "merge": DT, "out": 3 * DT, ("up", 0): 4 * DT}
    DVE_BASE["down", 0] = 4 * DT + PARTS[0][1]
    DVE_BASE["up", 1] = DVE_BASE["down", 0] + DT
    DVE_BASE["down", 1] = DVE_BASE["up", 1] + PARTS[1][1]
    DVE_USES = DVE_BASE["down", 1] + DT
    BANK_TURN, BANK_SUM, BANK_ACT, BANK_DVE = 0, 2, 4, 6
    WINDOW = T + TAPS - 1
    CONV_STEPS = CT * TAPS

    with ExitStack() as ctx:
        sb, sem = open_tensors(ctx, nc, "mix")
        ps = k.ps
        raw = sb("raw", [P, 2, DT, P])
        wt = sb("wt", [P, 2, 2, DT, P], F32R)
        x1 = sb("x1", [P, DT, T])
        h = sb("h", [P, DT, 2, T], F32R)
        hb = sb("hb", [P, 2, T])
        cu = sb("cu", [P, CT, WINDOW])
        cacc = sb("cacc", [P, CT, T])
        tmp = sb("tmp", [P, 4, T])
        gfin = sb("gfin", [P, D])
        ss, rstd, oss, orstd = sb("ss", [P, TT]), sb("rstd", [P, TT]), sb("oss", [P, TT]), sb("orstd", [P, TT])
        frstd = sb("frstd", [P, TT])
        a2 = sb("a2", [P, DT])
        sizes = {"a": 8 * D * 4, "b": 12 * D * 4}
        addresses = {}
        for region, size in sizes.items():
            if region == "a":
                addresses[region] = k.region_a
            else:
                sb(f"region_{region}", [P, size // 4])
                addresses[region] = nc.sbuf_base - size
        attn = sb("attn", [P, CT, 2, T], F32R)

        def view(region, name, shape, dt, at=0):
            return nc.alloc_sbuf_tensor_at(f"mix_{name}", shape, dt, offset=addresses[region] + at)

        xtok, xn = k.xtok, k.xn
        y = view("a", "y", [P, DT, 2, T], F32R)
        gate = view("b", "gate", [P, 2 * DT, T], F32)
        z = view("b", "z", [P, CT, 2, T], F32R, 2 * DT * T * 4)
        hid = view("b", "hid", [P, PARTS[0][1], 2, T], F32R)
        ob = view("a", "ob", [P, 2, D], F32, TT * D * 4)

        x_loaded, x_squared, x_std, x_rstd, x_scaled = k.late_x_progress
        (raw_turned, x_turned, turn_free, h_hi, h_lo) = (
            sem(n) for n in "raw_turned x_turned turn_free h_hi h_lo".split())
        (w_hi, w_lo, job_done, act_free, dve_free, conv_step, ln_summed, centred, ln_squared) = (
            sem(n) for n in
            "w_hi w_lo job_done act_free dve_free conv_step ln_summed centred ln_squared".split())
        (ln_std, ln_rstd, ln_scaled, z_act, z_hi, z_lo, y_sum, y_hi, y_lo) = (
            sem(n) for n in
            "ln_std ln_rstd ln_scaled z_act z_hi z_lo y_sum y_hi y_lo".split())
        (x1_squared, x1_summed, f_summed, f_std, f_rstd, h2_scaled, h2_hi, h2_lo, a_hi) = (
            sem(n) for n in
            "x1_squared x1_summed f_summed f_std f_rstd h2_scaled h2_hi h2_lo a_hi".split())
        (a_lo, o_turned, o_squared, o_std, o_rstd, o_scaled, a2_done, sum_cleared, gfin_loaded) = (
            sem(n) for n in
            "a_lo o_turned o_squared o_std o_rstd o_scaled a2_done sum_cleared gfin_loaded".split())
        (u_loaded, attn_loaded, f_diag, f_spread) = (
            sem(n) for n in "u_loaded attn_loaded f_diag f_spread".split())
        raw_loaded = [sem(f"raw_loaded{i}") for i in range(2)]
        o_stored = [sem(f"o_stored{i}") for i in range(2)]

        def prefetch_u(g, eng):
            eng.dma_start(cu[:, :, :], k.u_dram.rearrange("(c p) t -> p c t", p=P)
                         [:, :, bass.ds(g * T, WINDOW)]).then_inc(u_loaded, 16)

        def prefetch_attn(g, eng):
            for c in range(CT):
                eng.dma_start(attn[:, c].bitcast(F32), k.attn_dram[c * P:(c + 1) * P, :, bass.ds(g * T, T)])\
                    .then_inc(attn_loaded, 16)

        def groups(eng, body):
            body(0, True, False)
            with eng.Fori(1, GROUPS - 1) as g:
                body(g, False, False)
            body(GROUPS - 1, False, True)

        with nc.Block() as block:

            @block.sync
            def _(sp):
                def load(g, at, parity, *pairs):
                    sp.wait_ge(w_lo, turn(g * JOBS + at))
                    for to, src in pairs:
                        sp.dma_start(raw[:, parity, to[0]:to[1]], src).then_inc(raw_loaded[parity], 32 // len(pairs))

                def tiles(name, first, last, col):
                    return w[name][0, first * P:last * P].rearrange("(f p) m -> p f m", p=P)[:, :, bass.ds(col, P)]

                def gate_jobs(g, m):
                    for i in range(2):
                        load(g, BASE["gates"] + 2 * m + i, i, ((0, DT), tiles("w_in", 0, DT, IN_GATE + i * D + m * P)))

                def prefetch_x(g):
                    sp.dma_start(xtok[:, :, :],
                                 w["x"][0].rearrange("(g t p) f -> p g t f", t=TT, p=P)[:, bass.ds(g, 1)]
                                 .rearrange("p g t f -> p (g t) f")).then_inc(x_loaded, 16)

                def up_jobs(g, p, begin, end):
                    with sp.Fori(begin, end) as t:
                        for i in range(2):
                            load(g, BASE["up", p] + 2 * t + i, i,
                                 ((0, DT), tiles("w_gu", 0, DT, i * HID + (PARTS[p][0] + t) * P)))

                def body(g, last):
                    with sp.Fori(0, DT) as m:
                        gate_jobs(g, m)
                    with sp.Fori(0, DT // 2) as mm:
                        for i in range(2):
                            m = mm * 2 + i
                            load(g, BASE["merge"] + m, i, ((0, CT), tiles("w_o_attn", 0, CT, m * P)),
                                 ((CT, DT), tiles("w_pw2", 0, CT, m * P)))
                    with sp.Fori(0, DT // 2) as mm:
                        for i in range(2):
                            m = mm * 2 + i
                            load(g, BASE["out"] + m, i, ((0, DT), tiles("w_out", 0, DT, m * P)))
                    for p, (first, num) in enumerate(PARTS):
                        if p == 0 and not last:
                            up_jobs(g, p, 0, 1)
                            sp.wait_ge(z_lo, (g + 1) * CT)
                            prefetch_u(g + 1, sp)
                            up_jobs(g, p, 1, 3)
                            sp.wait_ge(job_done, done(g * JOBS + BASE["up", 0] - 1))
                            prefetch_x(g + 1)
                            up_jobs(g, p, 3, 6)
                            prefetch_attn(g + 1, sp)
                            up_jobs(g, p, 6, num)
                        else:
                            up_jobs(g, p, 0, num)
                        with sp.Fori(0, DT) as m:
                            for i in range(2):
                                load(g, BASE["down", p] + 2 * m + i, i,
                                     ((0, num // 2), tiles("w_down", first + i * num // 2,
                                                           first + (i + 1) * num // 2, m * P)))

                with sp.Fori(0, GROUPS - 1) as g:
                    body(g, False)
                body(GROUPS - 1, True)
                gate_jobs(GROUPS, 0)

            @block.gpsimd
            def _(pool):
                seeded(pool, w_lo)

                def lows(g, base, pairs):
                    with pool.Fori(0, pairs) as t:
                        for i in range(2):
                            pool.wait_ge(w_hi, g * JOBS + base + 2 * t + i + 1)
                            pool.tensor_tensor(wt[:, i, 1], raw[:, i], wt[:, i, 0].bitcast(F32), ALU.subtract)\
                                .then_inc(w_lo, 1)

                with pool.Fori(0, GROUPS) as g:
                    lows(g, 0, JOBS // 2)
                lows(GROUPS, 0, 1)

            @block.scalar
            def _(act):
                seeded(act, act_free, turn_free)
                seeded(act, o_squared, by=1)

                def hi(g, at, parity, use):
                    act.wait_ge(raw_loaded[parity], 32 * (g * (JOBS // 2) + use + 1))
                    act.wait_ge(job_done, turn(g * JOBS + at))
                    act.activation(wt[:, parity, 0], raw[:, parity], ACT.Copy).then_inc(w_hi, 1)

                def ahead(g, base, t, i):
                    hi(g, base + 2 * t + i + 2, i, base // 2 + t + 1)

                def x_stats(g):
                    act.wait_ge(x_loaded, 16 * (g + 1))
                    for t in range(TT):
                        act.wait_ge(x_squared, g * TT + t)
                        act.activation(hb[:, :, :].rearrange("p a b -> p (a b)"), xtok[:, t, :], ACT.Square,
                                       accum_out=ss[:, t:t + 1]).then_inc(x_squared, 1)
                    act.wait_ge(x_squared, (g + 1) * TT)
                    act.activation(rstd[:, :], ss[:, :], ACT.Sqrt, bias=k.eps[:, :], scale=1.0 / D).then_inc(x_std, 1)

                def ln_squares(g):
                    for c in range(CT):
                        act.wait_ge(centred, g * CT + c + 1)
                        act.activation(cu[:, c, 0:T], cacc[:, c, :], ACT.Square).then_inc(ln_squared, 1)

                def ln_root(g):
                    act.wait_ge(ln_summed, 2 * g + 2)
                    act.activation(tmp[:, 3, :], ps[:, BANK_SUM + 1, :], ACT.Sqrt, bias=k.eps[:, :], scale=1.0 / CONV)\
                        .then_inc(ln_std, 1)

                def ln_silu(g):
                    for c in range(CT):
                        act.wait_ge(ln_scaled, g * CT + c + 1)
                        act.activation(cu[:, c, 0:T], cacc[:, c, :], ACT.Silu, bias=k.vec[:, V_BCN + c:V_BCN + c + 1],
                                       scale=k.vec[:, V_GCN + c:V_GCN + c + 1]).then_inc(z_act, 1)

                def gates(g, begin, end):
                    with act.Fori(begin, end) as m:
                        for i in range(2):
                            ahead(g, BASE["gates"], m, i)
                            act.wait_ge(job_done, done(g * JOBS + 2 * m + i))
                            act.activation(gate[:, bass.ds(2 * m + i, 1), :].rearrange("p a t -> p (a t)"),
                                           ps[:, BANK_ACT + i, :], ACT.Sigmoid).then_inc(act_free, 1)

                def affine(g, f, half):
                    act.wait_ge(x_turned, g * DT + f + 1)
                    act.wait_ge(h_lo, turn(g * DT + f))
                    act.activation(hb[:, half, :], ps[:, BANK_TURN + half, :], ACT.Identity,
                                   bias=k.mod[:, bass.ds(SH1 + f, 1)], scale=k.a1[:, bass.ds(f, 1)])\
                        .then_inc(turn_free, 1)

                def norm_rows(g, begin, end):
                    act.wait_ge(h_lo, done((g + 1) * DT - 1))
                    for t in range(begin, end):
                        b = BANK_TURN + 2 * (t % 2)
                        act.wait_ge(o_turned, g * TT + t + 1)
                        act.wait_ge(o_squared, done(g * TT + t - 1, 1))
                        act.activation(hb[:, :, :], ps[:, b:b + 2, :], ACT.Square, accum_out=oss[:, t:t + 1])\
                            .then_inc(o_squared, 1)
                        act.wait_ge(o_squared, done(g * TT + t, 1))
                        act.activation(orstd[:, t:t + 1], oss[:, t:t + 1], ACT.Sqrt, bias=k.eps[:, :], scale=1.0 / D)\
                            .then_inc(o_std, 1)
                        if t:
                            store_out(g, t - 1)
                    if end == TT:
                        store_out(g, TT - 1)

                def body(g, first, last):
                    if first:
                        gates(g, 0, DT)
                        ln_squares(g)
                        ln_root(g)
                        ln_silu(g)
                    else:
                        gates(g, 0, 1)
                        norm_rows(g - 1, 0, 2)
                        gates(g, 1, 2)
                        norm_rows(g - 1, 2, TT)
                        gates(g, 2, 4)
                        ln_squares(g)
                        gates(g, 4, 6)
                        ln_root(g)
                        gates(g, 6, 7)
                        ln_silu(g)
                        gates(g, 7, DT)
                    with act.Fori(0, MERGE // 2) as mm:
                        for i in range(2):
                            ahead(g, BASE["merge"], mm, i)
                    with act.Fori(0, OUT // 2) as mm:
                        for i in range(2):
                            ahead(g, BASE["out"], mm, i)
                            m = 2 * mm + i
                            act.wait_ge(dve_free, done(g * DVE_USES + DVE_BASE["out"] + m))
                            act.wait_ge(x1_summed, turn(g * DT + m))
                            act.activation(tmp[:, i, :], x1[:, bass.ds(m, 1), :].rearrange("p a t -> p (a t)"),
                                           ACT.Square).then_inc(x1_squared, 1)
                    act.wait_ge(f_summed, g + 1)
                    act.activation(frstd[:, :], ps[:, BANK_SUM, 0:TT], ACT.Sqrt, bias=k.eps[:, :], scale=1.0 / D)\
                        .then_inc(f_std, 1)
                    for f in range(DT):
                        act.wait_ge(h2_scaled, g * DT + f + 1)
                        act.activation(h[:, f, 0, :], hb[:, f % 2, :], ACT.Identity,
                                       bias=k.mod[:, SH2 + f:SH2 + f + 1]).then_inc(h2_hi, 1)
                    for p, (_, num) in enumerate(PARTS):
                        with act.Fori(0, num // 2) as tt:
                            for a in range(2):
                                t = 2 * tt + a
                                for i in range(2):
                                    ahead(g, BASE["up", p], t, i)
                                    if i == 0:
                                        act.wait_ge(job_done, done(g * JOBS + BASE["up", p] + 2 * t))
                                        act.wait_ge(a_lo, turn(g * HT + PARTS[p][0] + t))
                                        act.activation(tmp[:, a, :], ps[:, BANK_ACT + a, :], ACT.Silu)\
                                            .then_inc(act_free, 1)
                        with act.Fori(0, DT // 2) as mm:
                            for a in range(2):
                                m = 2 * mm + a
                                for i in range(2):
                                    ahead(g, BASE["down", p], m, i)
                                if p == 1 and not last:
                                    affine(g + 1, m, a)
                        if p == 0 and not last:
                            x_stats(g + 1)
                    if last:
                        norm_rows(g, 0, TT)

                def store_out(g, t):
                    act.wait_ge(o_scaled, g * TT + t + 1)
                    act.dma_start(out[0, bass.ds(g * T + t * P, P), :], ob[:, t % 2, :]).then_inc(o_stored[t % 2], 16)

                for f in range(DT):
                    affine(0, f, f % 2)
                    if f == 1:
                        prefetch_u(0, act)
                    if f in (3, 5):
                        i = (f - 3) // 2
                        hi(0, i, i, 0)
                act.dma_start(gfin[:, :], w["g_final"].partition_broadcast(P)).then_inc(gfin_loaded, 16)
                prefetch_attn(0, act)
                groups(act, body)
                for i in range(2):
                    act.wait_ge(o_stored[i], 16 * (1 + GROUPS * TT // 2))

            @block.tensor
            def _(pe):
                seeded(pe, job_done)

                def product(bank, parity, tiles, moving, first=True, last=True, wait=None):
                    for f in tiles:
                        if wait:
                            wait(f)
                        for st, m in ((0, 0), (0, 1), (1, 0)):
                            ins = pe.matmul(ps[:, bank, :], wt[:, parity, st, f, :], moving(f, m),
                                            start=(first and f == tiles[0] and st == m == 0),
                                            stop=(last and f == tiles[-1] and st == 1))
                    return ins

                def mean(g):
                    pe.wait_ge(conv_step, (g + 1) * CONV_STEPS)
                    for c in range(CT):
                        ins = pe.matmul(ps[:, BANK_SUM, :], k.ones[:, :], cacc[:, c, :], start=(c == 0), stop=(c == CT - 1))
                    ins.then_inc(ln_summed, 1)

                def variance(g):
                    for c in range(CT):
                        pe.wait_ge(ln_squared, g * CT + c + 1)
                        ins = pe.matmul(ps[:, BANK_SUM + 1, :], k.ones[:, :], cu[:, c, 0:T],
                                        start=(c == 0), stop=(c == CT - 1))
                    ins.then_inc(ln_summed, 1)

                def raw_x(g):
                    for f in range(DT):
                        pe.wait_ge(dve_free, turn(g * DVE_USES + f))
                        for t in range(TT):
                            ins = pe.transpose(ps[:, BANK_DVE + f % 2, t * P:(t + 1) * P],
                                               xtok[:, t, f * P:(f + 1) * P], k.ident[:, :])
                        ins.then_inc(raw_turned, 1)

                def scaled_x(g, f):
                    pe.wait_ge(turn_free, turn(g * DT + f))
                    for t in range(TT):
                        ins = pe.transpose(ps[:, BANK_TURN + f % 2, t * P:(t + 1) * P],
                                           xn[:, t, f * P:(f + 1) * P], k.ident[:, :])
                    ins.then_inc(x_turned, 1)

                def gates(g, begin, end):
                    with pe.Fori(begin, end) as m:
                        for i in range(2):
                            pe.wait_ge(w_lo, done(g * JOBS + 2 * m + i))
                            pe.wait_ge(act_free, turn(g * ACT_USES + 2 * m + i))
                            wait = (lambda f: pe.wait_ge(h_lo, done(g * DT + f))) if i == 0 else None
                            product(BANK_ACT + i, i, range(DT), lambda f, m: h[:, f, m, :], wait=wait)\
                                .then_inc(job_done, 1)

                def rows(g, begin, end):
                    pe.wait_ge(dve_free, done(g * DVE_USES + DVE_USES - 1))
                    for t in range(begin, end):
                        b = BANK_TURN + 2 * (t % 2)
                        if t > 1:
                            pe.wait_ge(o_scaled, g * TT + t - 1)
                        for f in range(DT):
                            ins = pe.transpose(ps[:, b + f // TT, (f % TT) * P:(f % TT + 1) * P],
                                               x1[:, f, t * P:(t + 1) * P], k.ident[:, :])
                        ins.then_inc(o_turned, 1)

                def down_tile(g, p, begin, num, m, a):
                    pe.wait_ge(dve_free, turn(g * DVE_USES + DVE_BASE["down", p] + m))
                    for i in range(2):
                        pe.wait_ge(w_lo, done(g * JOBS + BASE["down", p] + 2 * m + i))
                        at = i * num // 2
                        if a == 0:
                            pe.wait_ge(a_lo, done(g * HT + begin + at + num // 2 - 1))
                        product(BANK_DVE + a, i, range(num // 2), lambda f, m: hid[:, at + f, m, :],
                                first=(i == 0), last=(i == 1)).then_inc(job_done, 1)

                def body(g, first, last):
                    if first:
                        for f in range(DT):
                            scaled_x(g, f)
                        raw_x(g)
                        gates(g, 0, DT)
                        mean(g)
                        variance(g)
                    else:
                        gates(g, 0, 1)
                        rows(g - 1, 0, 2)
                        gates(g, 1, 2)
                        rows(g - 1, 2, TT)
                        gates(g, 2, 3)
                        raw_x(g)
                        pe.wait_ge(o_scaled, g * TT)
                        mean(g)
                        gates(g, 3, 5)
                        variance(g)
                        gates(g, 5, DT)
                    with pe.Fori(0, MERGE // 2) as mm:
                        pe.wait_ge(attn_loaded, 16 * CT * (g + 1))
                        pe.wait_ge(dve_free, done(g * DVE_USES + DT - 1))
                        pe.wait_ge(act_free, done(g * ACT_USES + GATES - 1))
                        for i in range(2):
                            m = 2 * mm + i
                            pe.wait_ge(w_lo, done(g * JOBS + BASE["merge"] + m))
                            bank = BANK_ACT if i else BANK_DVE
                            pe.wait_ge(dve_free, g * DVE_USES + DVE_BASE["merge"] + 2 * m)
                            product(bank, i, range(CT), lambda f, m: attn[:, f, m, :])
                            pe.wait_ge(z_lo, (g + 1) * CT)
                            product(bank + 1, i, range(CT, DT), lambda f, m: z[:, f - CT, m, :])\
                                .then_inc(job_done, 1)
                    with pe.Fori(0, OUT // 2) as mm:
                        for i in range(2):
                            m = 2 * mm + i
                            pe.wait_ge(w_lo, done(g * JOBS + BASE["out"] + m))
                            pe.wait_ge(dve_free, turn(g * DVE_USES + DVE_BASE["out"] + m))
                            wait = (lambda f: pe.wait_ge(y_lo, done(g * DT + f, 1))) if i == 0 else None
                            product(BANK_DVE + i, i, range(DT), lambda f, m: y[:, f, m, :], wait=wait)\
                                .then_inc(job_done, 1)
                    pe.wait_ge(x1_summed, done(g * DT + DT - 1))
                    for t in range(TT):
                        ins = pe.matmul(ps[:, BANK_SUM, t:t + 1], tmp[:, 2, t * P:(t + 1) * P], k.ones[:, 0:1],
                                        start=True, stop=True)
                    ins.then_inc(f_summed, 1)
                    pe.wait_ge(f_diag, TT * (g + 1))
                    pe.matmul(ps[:, BANK_SUM + 1, :], k.ones[:, :], tmp[:, 3, :], start=True, stop=True)\
                        .then_inc(f_spread, 1)
                    for p, (begin, num) in enumerate(PARTS):
                        with pe.Fori(0, num // 2) as tt:
                            for a in range(2):
                                t = 2 * tt + a
                                for i in range(2):
                                    pe.wait_ge(w_lo, done(g * JOBS + BASE["up", p] + 2 * t + i))
                                    if i == 0:
                                        pe.wait_ge(act_free, turn(g * ACT_USES + ACT_BASE["up", p] + t))
                                    else:
                                        pe.wait_ge(dve_free, turn(g * DVE_USES + DVE_BASE["up", p] + t))
                                    wait = (lambda f: pe.wait_ge(h2_lo, g * DT + f + 1)) if p == a == i == 0 else None
                                    product((BANK_DVE if i else BANK_ACT) + a, i, range(DT),
                                            lambda f, m: h[:, f, m, :], wait=wait).then_inc(job_done, 1)
                        if p == 1 and not last:
                            pe.wait_ge(x_scaled, (g + 2) * TT)
                            for m in range(DT):
                                scaled_x(g + 1, m)
                                down_tile(g, p, begin, num, m, m % 2)
                        else:
                            with pe.Fori(0, DT // 2) as mm:
                                for a in range(2):
                                    down_tile(g, p, begin, num, 2 * mm + a, a)
                    if last:
                        rows(g, 0, TT)

                groups(pe, body)

            @block.vector
            def _(dve):
                seeded(dve, h_lo, dve_free, x1_summed, a_lo)
                seeded(dve, y_lo, by=1)
                seeded(dve, *o_stored, by=16)

                def scale_x(g):
                    dve.wait_ge(x_std, g + 1)
                    dve.reciprocal(rstd[:, :], rstd[:, :]).then_inc(x_rstd, 1)
                    dve.wait_ge(x_rstd, g + 1)
                    for t in range(TT):
                        dve.tensor_scalar(xn[:, t, :], xtok[:, t, :], rstd[:, t:t + 1], None, ALU.mult)\
                            .then_inc(x_scaled, 1)

                def conv_first(g, pair):
                    for i in range(2):
                        c = 2 * pair + i
                        dve.tensor_scalar(cacc[:, c, :], cu[:, c, 0:T], k.wdw[:, c, 0:1], k.vec[:, V_BDW + c:V_BDW + c + 1],
                                          ALU.mult, ALU.add).then_inc(conv_step, 1)

                def conv_tap(g, pair, tap):
                    for i in range(2):
                        c = 2 * pair + i
                        dve.wait_ge(conv_step, g * CONV_STEPS + pair * 2 * TAPS + 2 * tap + i - 1)
                        dve.scalar_tensor_tensor(cacc[:, c, :], cu[:, c, bass.ds(tap, T)], k.wdw[:, c, bass.ds(tap, 1)],
                                                 cacc[:, c, :], ALU.mult, ALU.add).then_inc(conv_step, 1)

                def ln_centre(g):
                    dve.wait_ge(ln_summed, 2 * g + 1)
                    for c in range(CT):
                        dve.scalar_tensor_tensor(cacc[:, c, :], ps[:, BANK_SUM, :], -1.0 / CONV, cacc[:, c, :],
                                                 ALU.mult, ALU.add).then_inc(centred, 1)

                def ln_finish(g):
                    dve.wait_ge(ln_std, g + 1)
                    dve.reciprocal(tmp[:, 3, :], tmp[:, 3, :]).then_inc(ln_rstd, 1)
                    dve.wait_ge(ln_rstd, g + 1)
                    for c in range(CT):
                        dve.tensor_tensor(cacc[:, c, :], cacc[:, c, :], tmp[:, 3, :], ALU.mult).then_inc(ln_scaled, 1)
                    for c in range(CT):
                        dve.wait_ge(z_act, g * CT + c + 1)
                        dve.tensor_copy(z[:, c, 0, :], cu[:, c, 0:T]).then_inc(z_hi, 1)
                        dve.wait_ge(z_hi, g * CT + c + 1)
                        dve.tensor_tensor(z[:, c, 1, :], cu[:, c, 0:T], z[:, c, 0, :].bitcast(F32), ALU.subtract)\
                            .then_inc(z_lo, 1)

                def one(tensor, index, *rest):
                    return tensor[(slice(None), bass.ds(index, 1)) + rest].rearrange("p a t -> p (a t)")

                def residual(m, a, scale):
                    dve.scalar_tensor_tensor(one(x1, m), ps[:, BANK_DVE + a, :], k.mod[:, bass.ds(scale + m, 1)],
                                             one(x1, m), ALU.mult, ALU.add).then_inc(dve_free, 1)

                def split_h(g, f, half):
                    dve.wait_ge(turn_free, done(g * DT + f))
                    hh = h[:, bass.ds(f, 1), :, :].rearrange("p a b t -> p (a b) t")
                    dve.tensor_copy(hh[:, 0, :], hb[:, half, :]).then_inc(h_hi, 1)
                    dve.wait_ge(h_hi, g * DT + f + 1)
                    dve.tensor_tensor(hh[:, 1, :], hb[:, half, :], hh[:, 0, :].bitcast(F32), ALU.subtract)\
                        .then_inc(h_lo, 1)

                def raw_x(g):
                    for f in range(DT):
                        dve.wait_ge(raw_turned, g * DT + f + 1)
                        dve.tensor_copy(x1[:, f, :], ps[:, BANK_DVE + f % 2, :]).then_inc(dve_free, 1)

                def norm_rows(g):
                    dve.wait_ge(gfin_loaded, 16)
                    for t in range(TT):
                        b = BANK_TURN + 2 * (t % 2)
                        dve.wait_ge(o_std, g * TT + t + 1)
                        dve.reciprocal(orstd[:, t:t + 1], orstd[:, t:t + 1]).then_inc(o_rstd, 1)
                        dve.wait_ge(o_rstd, g * TT + t + 1)
                        dve.wait_ge(o_stored[t % 2], 16 * (g * (TT // 2) + t // 2 + 1))
                        dve.scalar_tensor_tensor(ob[:, t % 2, :], ps[:, b:b + 2, :].rearrange("p a t -> p (a t)"),
                                                 orstd[:, t:t + 1], gfin[:, :], ALU.mult, ALU.mult)\
                            .then_inc(o_scaled, 1)

                def body(g, first, last):
                    if not first:
                        norm_rows(g - 1)
                        raw_x(g)
                        ln_centre(g)
                    else:
                        for f in range(DT):
                            split_h(g, f, f % 2)
                        raw_x(g)
                        dve.wait_ge(u_loaded, 16)
                        for pair in range(CT // 2):
                            conv_first(g, pair)
                            with dve.Fori(0, (TAPS - 1) // 6) as i:
                                for j in range(6):
                                    conv_tap(g, pair, i * 6 + j + 1)
                        ln_centre(g)
                    ln_finish(g)
                    with dve.Fori(0, MERGE // 2) as mm:
                        for a in range(2):
                            dve.wait_ge(o_stored[a], 16 * (g * (TT // 2) + 1))
                        for a in range(2):
                            m = 2 * mm + a
                            use = g * DVE_USES + DVE_BASE["merge"] + 2 * m
                            dve.wait_ge(job_done, done(g * JOBS + BASE["merge"] + m))
                            dve.wait_ge(y_lo, done(g * DT + m - 1, 1))
                            for i in range(2):
                                dve.tensor_tensor(tmp[:, i, :], ps[:, (BANK_ACT if a else BANK_DVE) + i, :], one(gate, 2 * m + i), ALU.mult)\
                                    .then_inc(dve_free, 1)
                            dve.wait_ge(dve_free, done(use + 1))
                            dve.tensor_tensor(tmp[:, 0, :], tmp[:, 0, :], tmp[:, 1, :], ALU.add).then_inc(y_sum, 1)
                            dve.wait_ge(y_sum, g * DT + m + 1)
                            sum_hi = y[:, bass.ds(m, 1), 0, :].rearrange("p a t -> p (a t)")
                            sum_lo = y[:, bass.ds(m, 1), 1, :].rearrange("p a t -> p (a t)")
                            dve.tensor_copy(sum_hi, tmp[:, 0, :]).then_inc(y_hi, 1)
                            dve.wait_ge(y_hi, g * DT + m + 1)
                            dve.tensor_tensor(sum_lo, tmp[:, 0, :], sum_hi.bitcast(F32), ALU.subtract).then_inc(y_lo, 1)
                    dve.wait_ge(a_lo, done(g * HT - 1))
                    dve.memset(tmp[:, 2, :], 0.0).then_inc(sum_cleared, 1)
                    with dve.Fori(0, OUT // 2) as mm:
                        for a in range(2):
                            m = 2 * mm + a
                            dve.wait_ge(job_done, done(g * JOBS + BASE["out"] + m))
                            residual(m, a, GT1)
                            dve.wait_ge(x1_squared, g * DT + m + 1)
                            dve.wait_ge(sum_cleared, g + 1)
                            dve.wait_ge(x1_summed, done(g * DT + m - 1))
                            dve.tensor_tensor(tmp[:, 2, :], tmp[:, 2, :], tmp[:, a, :], ALU.add).then_inc(x1_summed, 1)
                    dve.wait_ge(f_std, g + 1)
                    dve.reciprocal(frstd[:, :], frstd[:, :]).then_inc(f_rstd, 1)
                    dve.wait_ge(f_rstd, g + 1)
                    for t in range(TT):
                        dve.tensor_scalar(tmp[:, 3, t * P:(t + 1) * P], k.ident[:, :], frstd[:, t:t + 1], None, ALU.mult)\
                            .then_inc(f_diag, 1)
                    dve.wait_ge(f_spread, g + 1)
                    for f in range(DT + 1):
                        if f < DT:
                            if f > 1:
                                dve.wait_ge(h2_lo, g * DT + f - 1)
                            dve.scalar_tensor_tensor(hb[:, f % 2, :], x1[:, f, :], a2[:, f:f + 1],
                                                     ps[:, BANK_SUM + 1, :], ALU.mult, ALU.mult).then_inc(h2_scaled, 1)
                        if f:
                            e = f - 1
                            dve.wait_ge(h2_hi, g * DT + f)
                            dve.scalar_tensor_tensor(h[:, e, 1, :], hb[:, e % 2, :], k.mod[:, SH2 + e:SH2 + e + 1],
                                                     h[:, e, 0, :].bitcast(F32), ALU.add, ALU.subtract)\
                                .then_inc(h2_lo, 1)
                    for p, (begin, num) in enumerate(PARTS):
                        per = (TAPS - 1) * 2 // num
                        if not last:
                            if p == 0:
                                dve.wait_ge(u_loaded, 16 * (g + 2))
                            else:
                                scale_x(g + 1)
                            conv_first(g + 1, p)
                        with dve.Fori(0, num // 2) as tt:
                            for a in range(2):
                                t = 2 * tt + a
                                dve.wait_ge(act_free, done(g * ACT_USES + ACT_BASE["up", p] + t))
                                dve.wait_ge(job_done, done(g * JOBS + BASE["up", p] + 2 * t + 1))
                                dve.wait_ge(a_lo, done(g * HT + begin + t - 1))
                                dve.tensor_tensor(tmp[:, 2, :], ps[:, BANK_DVE + a, :], tmp[:, a, :], ALU.mult)\
                                    .then_inc(dve_free, 1)
                                dve.wait_ge(dve_free, done(g * DVE_USES + DVE_BASE["up", p] + t))
                                hid_hi = hid[:, bass.ds(t, 1), 0, :].rearrange("p a t -> p (a t)")
                                hid_lo = hid[:, bass.ds(t, 1), 1, :].rearrange("p a t -> p (a t)")
                                dve.tensor_copy(hid_hi, tmp[:, 2, :]).then_inc(a_hi, 1)
                                dve.wait_ge(a_hi, g * HT + begin + t + 1)
                                dve.tensor_tensor(hid_lo, tmp[:, 2, :], hid_hi.bitcast(F32), ALU.subtract)\
                                    .then_inc(a_lo, 1)
                                if not last:
                                    for j in range(a * (per // 2), per if a else per // 2):
                                        conv_tap(g + 1, p, tt * per + j + 1)
                        with dve.Fori(0, DT // 2) as mm:
                            for a in range(2):
                                m = 2 * mm + a
                                dve.wait_ge(job_done, done(g * JOBS + BASE["down", p] + 2 * m + 1))
                                residual(m, a, GT2)
                                if p == 1 and not last:
                                    split_h(g + 1, m, a)
                    if last:
                        norm_rows(g)

                dve.scalar_tensor_tensor(a2[:, :], k.mod[:, SC2:SC2 + DT], 1.0, k.vec[:, V_GFFN:V_GFFN + DT],
                                         ALU.add, ALU.mult).then_inc(a2_done, 1)
                dve.wait_ge(a2_done, 1)
                groups(dve, body)


def layer(nc, w, out):
    with ExitStack() as ctx:
        k = Kept()
        k.ps = ctx.enter_context(nc.psum_tensor("ps", [P, 8, T], F32))

        def keep(name, shape):
            return ctx.enter_context(nc.sbuf_tensor(name, shape, F32))

        k.vec = keep("vec", [P, V_ROWS])
        k.wdw = keep("wdw", [P, CT, TAPS])
        k.mod = keep("mod", [P, 6 * DT])
        k.a1 = keep("a1", [P, DT])
        k.c_act = keep("c_act", [P, DT])
        k.ident = keep("ident", [P, P])
        k.ones = keep("ones", [P, P])
        k.eps = keep("eps", [P, 1])
        k.u_dram = nc.dram_tensor("u_dram", [CONV, TAPS - 1 + SEQ], F32).ap()
        k.qn_dram = nc.dram_tensor("qn_dram", [HEADS * NOPE, 2, SEQ], F32).ap()
        k.qr_dram = nc.dram_tensor("qr_dram", [HEADS * ROPE, 2, SEQ], F32).ap()
        k.kn_dram = nc.dram_tensor("kn_dram", [HEADS * NOPE, 2, SEQ], F32).ap()
        k.kr_dram = nc.dram_tensor("kr_dram", [ROPE, 2, SEQ], F32).ap()
        k.v_dram = nc.dram_tensor("v_dram", [SEQ, HEADS * 2 * VD], F32).ap()
        k.attn_dram = nc.dram_tensor("attn_dram", [HEADS * VD, 2, SEQ], F32).ap()
        with ExitStack() as early:
            sb, sem = open_tensors(early, nc, "early")
            k.cos, k.sin = sb("cos", [P, SEQ]), sb("sin", [P, SEQ])
            k.tokens = sb("tokens", [P, TT, D])
            k.ss, k.rstd = sb("ss", [P, TT]), sb("rstd", [P, TT])
            k.wuq = sb("wuq", [P, QT, 2, HEADS * QK], F32R)
            k.wukv = sb("wukv", [P, KT, 2, HEADS * (NOPE + VD)], F32R)
            k.x_progress = [sem(n) for n in ("x_loaded", "x_squared", "x_std", "x_rstd", "x_scaled")]
            modulation(nc, w, k)
            project(nc, w, k)
        with ExitStack() as late:
            sb, sem = open_tensors(late, nc, "late")
            sb("region_a", [P, 2 * TT, D])
            k.late_x_progress = [sem(n) for n in ("x_loaded", "x_squared", "x_std", "x_rstd", "x_scaled")]
            k.region_a = nc.sbuf_base - 2 * TT * D * 4
            k.xtok = nc.alloc_sbuf_tensor_at("xtok", [P, TT, D], F32, offset=k.region_a)
            k.xn = nc.alloc_sbuf_tensor_at("xn", [P, TT, D], F32, offset=k.region_a + TT * D * 4)
            attend(nc, w, k)
            mix(nc, w, k, out)


_NAMES = ["x", "c", "positions", "w_ada", "b_ada", "g_mix", "w_in", "g_q", "w_uq", "g_kv", "w_ukv", "w_o_attn",
          "w_dw", "b_dw", "g_cn", "b_cn", "w_pw2", "w_out", "g_ffn", "w_gu", "w_down", "g_final"]


def kernel(**inputs):
    import numpy as _np
    import concourse.bacc as _bacc
    from concourse import mybir as _mybir
    from concourse.bass_utils import run_bass_kernel_spmd as _run

    nc = _bacc.Bacc("TRN2", target_bir_lowering=False, num_devices=1)
    row = _np.arange(P) % ROPE
    freq = ROPE_THETA ** (-2.0 * (row % (ROPE // 2)) / ROPE)
    rope_const = _np.stack([freq, _np.where(row < ROPE // 2, -1.0, 1.0)], axis=1).astype(_np.float32)
    arrays, w = {}, {}
    for name in _NAMES + ["rope_const"]:
        a = _np.ascontiguousarray(inputs[name]) if name in inputs else rope_const
        arrays[f"in_{name}"] = a
        w[name] = nc.dram_tensor(f"in_{name}", a.shape, _mybir.dt.from_np(a.dtype), kind="ExternalInput").ap()
    out = nc.dram_tensor("out", (1, SEQ, D), F32, kind="ExternalOutput").ap()
    layer(nc, w, out)
    r = _run(nc, [arrays], core_ids=[0])
    return r.results[0]["out"]
```
